# Optimizing a Trainium2 kernel written in Bass

```python
import math
import jax, jax.numpy as jnp
from jax import lax
import numpy as np

D_MODEL = 1024
BATCH = 1
SEQ = 1024
DEPTH = 1

CHUNK = 64
NORM_EPS = 1e-6
NEG_INF = -1e30

SWA_HEADS = 8
SWA_KV_HEADS = 2
SWA_HEAD_DIM = 64
SWA_WINDOW = 128
SWA_WINDOW_CHUNKS = SWA_WINDOW // CHUNK

DIFF_HEADS = 4
DIFF_HEAD_DIM = 64
DIFF_Q_BLOCK = 128

A_Q = SWA_HEADS * SWA_HEAD_DIM
A_KV = SWA_KV_HEADS * SWA_HEAD_DIM
B_QK = DIFF_HEADS * 2 * DIFF_HEAD_DIM
B_V = DIFF_HEADS * 2 * DIFF_HEAD_DIM
N_BRANCHES = 2
GATE_W = N_BRANCHES * D_MODEL
SPLIT_WIDTHS = (A_Q, A_KV, A_KV, B_QK, B_QK, B_V, GATE_W)
IN_WIDTH = sum(SPLIT_WIDTHS)

PEER_HEADS = 8
PEER_N_KEYS = 128
PEER_EXPERTS = PEER_N_KEYS * PEER_N_KEYS
PEER_QUERY_DIM = 256
PEER_HALF = PEER_QUERY_DIM // 2
PEER_TOPK = 16
PEER_TOKEN_BLOCK = 128

kernel_name = "hybrid_swa_sink_diffattn_peer_block"

def rms_norm(x, g):
    xf = x.astype(jnp.float32)
    y = xf * lax.rsqrt(jnp.mean(xf * xf, axis=-1, keepdims=True) + NORM_EPS)
    return (y * g.astype(jnp.float32)).astype(x.dtype)

def alibi_slopes(n_heads):
    start = 2.0 ** (-8.0 / n_heads)
    return jnp.asarray(np.array([start ** (i + 1) for i in range(n_heads)], dtype=np.float32))

def shift_chunks(a, j):
    if j == 0:
        return a
    pad = jnp.zeros_like(a[:, :j])
    return jnp.concatenate([pad, a[:, :-j]], axis=1)

def sliding_window_sink_attention(q, k, v, sinks):
    B, S = q.shape[0], q.shape[1]
    n_c = S // CHUNK
    G = SWA_HEADS // SWA_KV_HEADS
    W = SWA_WINDOW_CHUNKS
    qc = q.reshape(B, n_c, CHUNK, SWA_KV_HEADS, G, SWA_HEAD_DIM)
    kc = k.reshape(B, n_c, CHUNK, SWA_KV_HEADS, SWA_HEAD_DIM)
    vc = v.reshape(B, n_c, CHUNK, SWA_KV_HEADS, SWA_HEAD_DIM)
    kw = jnp.concatenate([shift_chunks(kc, j) for j in reversed(range(W))], axis=2)
    vw = jnp.concatenate([shift_chunks(vc, j) for j in reversed(range(W))], axis=2)
    scores = jnp.einsum('bcqhgd,bckhd->bchgqk', qc, kw).astype(jnp.float32) * (SWA_HEAD_DIM ** -0.5)
    q_off = jnp.arange(CHUNK)
    k_off = jnp.arange(W * CHUNK) - (W - 1) * CHUNK
    dist = jnp.abs(q_off[:, None] - k_off[None, :]).astype(jnp.float32)
    slopes = alibi_slopes(SWA_HEADS).reshape(SWA_KV_HEADS, G)
    scores = scores - slopes[:, :, None, None] * dist
    key_chunk = jnp.arange(n_c)[:, None] + (jnp.arange(W * CHUNK) // CHUNK - (W - 1))[None, :]
    valid = key_chunk >= 0
    scores = jnp.where(valid[None, :, None, None, None, :], scores, NEG_INF)
    sink = sinks.astype(jnp.float32).reshape(SWA_KV_HEADS, G)[None, None, :, :, None, None]
    m = jnp.maximum(jnp.max(scores, axis=-1, keepdims=True), sink)
    p = jnp.exp(scores - m)
    probs = p / (jnp.sum(p, axis=-1, keepdims=True) + jnp.exp(sink - m))
    out = jnp.einsum('bchgqk,bckhd->bcqhgd', probs.astype(v.dtype), vw)
    return out.reshape(B, S, SWA_HEADS * SWA_HEAD_DIM)

def differential_attention(q, k, v, lam_params, subln_g, layer_idx):
    B, S = q.shape[0], q.shape[1]
    n_qb = S // DIFF_Q_BLOCK
    lambda_init = 0.8 - 0.6 * math.exp(-0.3 * layer_idx)
    lp = lam_params.astype(jnp.float32)
    lam = jnp.exp(jnp.sum(lp[0] * lp[1])) - jnp.exp(jnp.sum(lp[2] * lp[3])) + lambda_init
    slopes = alibi_slopes(DIFF_HEADS)
    k_pos = jnp.arange(S)
    k_chunk = k_pos // CHUNK
    scale = DIFF_HEAD_DIM ** -0.5
    q_blocks = jnp.moveaxis(q.reshape(B, n_qb, DIFF_Q_BLOCK, DIFF_HEADS, 2, DIFF_HEAD_DIM), 1, 0)

    def block(args):
        qb, bi = args
        q_pos = bi * DIFF_Q_BLOCK + jnp.arange(DIFF_Q_BLOCK)
        s = jnp.einsum('bqhmd,bkhmd->bhmqk', qb, k).astype(jnp.float32) * scale
        dist = jnp.abs(q_pos[:, None] - k_pos[None, :]).astype(jnp.float32)
        s = s - slopes[:, None, None, None] * dist
        allowed = k_chunk[None, :] <= (q_pos // CHUNK)[:, None]
        s = jnp.where(allowed, s, NEG_INF)
        a = jax.nn.softmax(s, axis=-1)
        w = a[:, :, 0] - lam * a[:, :, 1]
        return jnp.einsum('bhqk,bkhe->bqhe', w.astype(v.dtype), v)

    out = lax.map(block, (q_blocks, jnp.arange(n_qb)))
    out = jnp.moveaxis(out, 0, 1).reshape(B, S, DIFF_HEADS, 2 * DIFF_HEAD_DIM)
    out = rms_norm(out, subln_g) * (1.0 - lambda_init)
    return out.reshape(B, S, DIFF_HEADS * 2 * DIFF_HEAD_DIM)

def peer_ffn(xn, wq, subkeys, u, v):
    B, S, D = xn.shape
    n_tb = (B * S) // PEER_TOKEN_BLOCK
    xb = xn.reshape(n_tb, PEER_TOKEN_BLOCK, D)
    K = PEER_TOPK

    def block(xt):
        q = (xt @ wq).reshape(PEER_TOKEN_BLOCK, PEER_HEADS, 2, PEER_HALF)
        s = jnp.einsum('thpd,hpnd->thpn', q, subkeys).astype(jnp.float32)
        v_top, i_top = lax.top_k(s, K)
        cand = v_top[:, :, 0, :, None] + v_top[:, :, 1, None, :]
        cand_idx = i_top[:, :, 0, :, None] * PEER_N_KEYS + i_top[:, :, 1, None, :]
        best, pos = lax.top_k(cand.reshape(PEER_TOKEN_BLOCK, PEER_HEADS, K * K), K)
        experts = jnp.take_along_axis(cand_idx.reshape(PEER_TOKEN_BLOCK, PEER_HEADS, K * K), pos, axis=-1)
        g = jax.nn.softmax(best, axis=-1)
        h = jnp.einsum('td,thkd->thk', xt, u[experts])
        act = jax.nn.gelu(h, approximate=False) * g.astype(h.dtype)
        return jnp.einsum('thk,thkd->td', act, v[experts])

    return lax.map(block, xb).reshape(B, S, D)

def setup_inputs(seed: int = 0) -> dict:
    key = jax.random.key(seed)
    ks = jax.random.split(key, 18)
    D = D_MODEL
    nrm = lambda k, shape, s: jax.random.normal(k, shape, jnp.float32) * s
    return {
        "x": nrm(ks[0], (BATCH, SEQ, D), 1.0),
        "norm_mix_g": 1.0 + nrm(ks[1], (DEPTH, D), 0.02),
        "w_in": nrm(ks[2], (DEPTH, D, IN_WIDTH), D ** -0.5),
        "gate_bias": nrm(ks[3], (DEPTH, GATE_W), 0.1),
        "sinks": nrm(ks[4], (DEPTH, SWA_HEADS), 0.5),
        "diff_lambda": nrm(ks[5], (DEPTH, 4, DIFF_HEAD_DIM), 0.1),
        "diff_subln_g": 1.0 + nrm(ks[6], (DEPTH, 2 * DIFF_HEAD_DIM), 0.02),
        "w_up_a": nrm(ks[7], (DEPTH, A_Q, D), A_Q ** -0.5),
        "w_up_b": nrm(ks[8], (DEPTH, B_V, D), B_V ** -0.5),
        "w_out": nrm(ks[9], (DEPTH, D, D), D ** -0.5),
        "norm_ffn_g": 1.0 + nrm(ks[10], (DEPTH, D), 0.02),
        "peer_wq": nrm(ks[11], (DEPTH, D, PEER_HEADS * PEER_QUERY_DIM), D ** -0.5),
        "peer_subkeys": nrm(ks[12], (DEPTH, PEER_HEADS, 2, PEER_N_KEYS, PEER_HALF), PEER_HALF ** -0.5),
        "peer_u": nrm(ks[13], (DEPTH, PEER_EXPERTS, D), D ** -0.5),
        "peer_v": nrm(ks[14], (DEPTH, PEER_EXPERTS, D), PEER_HEADS ** -0.5),
        "norm_final_g": 1.0 + nrm(ks[15], (D,), 0.02),
    }

def reference(x, norm_mix_g, w_in, gate_bias, sinks, diff_lambda, diff_subln_g, w_up_a, w_up_b,
              w_out, norm_ffn_g, peer_wq, peer_subkeys, peer_u, peer_v, norm_final_g):
    B, S, D = x.shape
    split_pts = list(np.cumsum(SPLIT_WIDTHS)[:-1])
    for l in range(DEPTH):
        xn = rms_norm(x, norm_mix_g[l])
        proj = xn @ w_in[l]
        qa, ka, va, qb, kb, vb, gl = jnp.split(proj, split_pts, axis=-1)
        qa = qa.reshape(B, S, SWA_HEADS, SWA_HEAD_DIM)
        ka = ka.reshape(B, S, SWA_KV_HEADS, SWA_HEAD_DIM)
        va = va.reshape(B, S, SWA_KV_HEADS, SWA_HEAD_DIM)
        qb = qb.reshape(B, S, DIFF_HEADS, 2, DIFF_HEAD_DIM)
        kb = kb.reshape(B, S, DIFF_HEADS, 2, DIFF_HEAD_DIM)
        vb = vb.reshape(B, S, DIFF_HEADS, 2 * DIFF_HEAD_DIM)
        gates = jax.nn.sigmoid(gl + gate_bias[l]).reshape(B, S, N_BRANCHES, D)
        ya = sliding_window_sink_attention(qa, ka, va, sinks[l]) @ w_up_a[l]
        yb = differential_attention(qb, kb, vb, diff_lambda[l], diff_subln_g[l], l) @ w_up_b[l]
        merged = gates[:, :, 0] * ya + gates[:, :, 1] * yb
        x = x + merged @ w_out[l]
        xn2 = rms_norm(x, norm_ffn_g[l])
        x = x + peer_ffn(xn2, peer_wq[l], peer_subkeys[l], peer_u[l], peer_v[l])
    return rms_norm(x, norm_final_g)


_drawn_inputs = setup_inputs


def setup_inputs(seed=0):
    import zlib

    import numpy as np

    out = dict(_drawn_inputs(seed))
    spreads = {}
    factors = {'sinks': 6.239, 'diff_subln_g': 3.192, 'norm_final_g': 8.196, 'norm_ffn_g': 3.649}
    for name, (base, spread) in spreads.items():
        noise = np.random.default_rng([zlib.crc32(name.encode()), seed]).standard_normal(out[name].shape)
        drawn = base * np.exp(spread * noise) if base else spread * noise
        out[name] = __import__('jax').numpy.asarray(drawn.astype(out[name].dtype))
    for name, factor in factors.items():
        out[name] = (out[name] * factor).astype(out[name].dtype)
    return out
```

```python
import numpy as np
import concourse.bass as bass
from concourse import mybir
from concourse.alu_op_type import AluOpType as ALU

F32 = mybir.dt.float32
F32R = mybir.dt.float32r
U32 = mybir.dt.uint32
ACT = mybir.ActivationFunctionType
AX = mybir.AxisListType
ds = bass.ds

P = 128
D = 1024
T = 1024
KT = D // P
TT = T // P
HALF = 512
EPS = 1e-6
CHUNK = 64
HD = 64
QA, KA, VA, QB, KB, VB, GL = 0, 512, 640, 768, 1280, 1792, 2304
WC = 256
SWA_HEADS, DIFF_HEADS = 8, 4
LAMBDA_INIT = 0.2
PH, NK, TOPK = 8, 128, 16
HP = 2 * PH
E_TILES = NK
LOWEST = -3.0e38

T_QA, T_QB, T_KB, T_KA = 0, 4, 8, 12

C_ID, C_IOTA, C_IOTA16, C_SWA = 0, 128, 256, 272
C_DIFF = C_SWA + SWA_HEADS * 256
C_END = C_DIFF + DIFF_HEADS * 1024


def constant_table():
    c = np.zeros((P, C_END), np.float32)
    c[:, C_ID:C_ID + P] = np.eye(P)
    c[:, C_IOTA:C_IOTA + P] = np.arange(P)
    c[:, C_IOTA16:C_IOTA16 + 16] = np.arange(16)
    q = np.arange(P)[:, None]
    k = np.arange(256)[None, :] - P
    behind = q // CHUNK - k // CHUNK
    for j in range(4):
        for a in range(2):
            slope = 2.0 ** -(4 * a + j + 1)
            at = C_SWA + (2 * j + a) * 256
            c[:, at:at + 256] = np.where((behind == 0) | (behind == 1), -8 * slope * np.abs(q - k), -8e30)
    k = np.arange(1024)[None, :] - 896
    for h in range(DIFF_HEADS):
        slope = 2.0 ** (-2 * (h + 1))
        at = C_DIFF + h * 1024
        c[:, at:at + 1024] = np.where(k // CHUNK <= q // CHUNK, -8 * slope * np.abs(q - k), -8e30)
    return c


class Space:

    def __init__(self, nc):
        self.nc, self.n, self.sems = nc, 0, []
        self.base = 16512
        self.banks = nc.alloc_psum_tensor("banks", [P, 8, 512], F32)

    def at(self, name, kb, shape, dtype=F32):
        self.n += 1
        return self.nc.alloc_sbuf_tensor_at(f"{name}_{self.n}", shape, dtype, offset=self.base + int(kb * 1024))

    def sem(self, name):
        self.n += 1
        self.sems.append(self.nc.alloc_semaphore(f"{name}_{self.n}"))
        return self.sems[-1]

    def recycle(self):
        self.nc.clear_and_free_semaphores(self.sems)
        self.nc.all_engine_barrier()
        self.sems = []


def f32(ap):
    return ap.bitcast(F32)


def rep(ap, axis, n):
    ap = ap.unsqueeze(axis)
    return ap.broadcast_to([n if a == axis else c for a, c in enumerate(ap.shape)])


def norm_transpose(nc, sp, ident, src, gain, hi, lo, kb):
    xr = sp.at("norm_x", kb, [P, 2, D])
    xs = sp.at("norm_scaled", kb + 8, [P, 2, D])
    gb = sp.at("norm_gain", kb + 16, [P, D])
    junk = sp.at("norm_squares", kb + 20, [P, D])
    small = sp.at("norm_small", 206, [P, 8])
    bank = sp.banks
    x_in = [sp.sem("x_in0"), sp.sem("x_in1")]
    gain_in, eps_set, sumsq, std, rstd = (sp.sem(s) for s in ("gain_in", "eps_set", "sumsq", "std", "rstd"))
    scaled, turned, hi_done, lo_done = (
        sp.sem(s) for s in ("scaled", "turned", "hi_done", "lo_done"))
    rows = src.rearrange("(t p) d -> t p d", p=P)
    ss, sd, rs, eps = small[:, 0:2], small[:, 2:4], small[:, 4:6], small[:, 6:7]

    with nc.Block() as block:
        @block.sync
        def _(eng):
            eng.dma_start(gb[:, :], gain[0].partition_broadcast(P)).then_inc(gain_in, 16)
            with eng.Fori(0, TT // 2) as i:
                for u in range(2):
                    eng.wait_ge(scaled, 2 * i + u + 1)
                    eng.dma_start(xr[:, u, :], rows[2 * i + u, :, :]).then_inc(x_in[u], 16)

        @block.scalar
        def _(eng):
            eng.wait_ge(eps_set, 1)

            def stats(i, u):
                eng.wait_ge(x_in[u], 16 * i + 16)
                nc.scalar.activation(junk[:, :], xr[:, u, :], ACT.Square,
                                     accum_out=ss[:, u:u + 1]).then_inc(sumsq, 1)
                eng.wait_ge(sumsq, 2 * i + u + 1)
                nc.scalar.activation(sd[:, u:u + 1], ss[:, u:u + 1], ACT.Sqrt,
                                     bias=eps, scale=1.0 / D).then_inc(std, 1)

            def take_hi(i, u):
                for b in range(2):
                    eng.wait_ge(turned, 4 * i + 2 * u + b + 1)
                    nc.scalar.activation(hi[:, 4 * b:4 * b + 4, ds((2 * i + u) * P, P)],
                                         bank[:, 2 * u + b, :].rearrange("p (k t) -> p k t", k=4),
                                         ACT.Copy).then_inc(hi_done, 1)

            stats(0, 0)
            with eng.Fori(0, TT // 2 - 1) as i:
                for u in range(2):
                    stats(i + u, 1 - u)
                    take_hi(i, u)
            stats(TT // 2 - 1, 1)
            take_hi(TT // 2 - 1, 0)
            take_hi(TT // 2 - 1, 1)

        @block.vector
        def _(eng):
            nc.vector.memset(eps, EPS).then_inc(eps_set, 1)
            eng.sem_inc(scaled, 2)
            eng.sem_inc(lo_done, 4)
            eng.wait_ge(gain_in, 16)

            def scale(i, u):
                eng.wait_ge(std, 2 * i + u + 1)
                nc.vector.reciprocal(rs[:, u:u + 1], sd[:, u:u + 1]).then_inc(rstd, 1)
                eng.wait_ge(rstd, 2 * i + u + 1)
                nc.vector.scalar_tensor_tensor(
                    out=xs[:, u, :], in0=xr[:, u, :], scalar=rs[:, u:u + 1], in1=gb[:, :],
                    op0=ALU.mult, op1=ALU.mult).then_inc(scaled, 1)

            def take_lo(i, u):
                for b in range(2):
                    eng.wait_ge(hi_done, 4 * i + 2 * u + b + 1)
                    at = (slice(None), slice(4 * b, 4 * b + 4), ds((2 * i + u) * P, P))
                    nc.vector.tensor_tensor(lo[at], bank[:, 2 * u + b, :].rearrange("p (k t) -> p k t", k=4),
                                            f32(hi[at]), ALU.subtract).then_inc(lo_done, 1)

            scale(0, 0)
            with eng.Fori(0, TT // 2 - 1) as i:
                for u in range(2):
                    scale(i + u, 1 - u)
                    take_lo(i, u)
            scale(TT // 2 - 1, 1)
            take_lo(TT // 2 - 1, 0)
            take_lo(TT // 2 - 1, 1)

        @block.tensor
        def _(eng):
            with eng.Fori(0, TT // 2) as i:
                for u in range(2):
                    eng.wait_ge(scaled, 2 * i + u + 3)
                    for b in range(2):
                        eng.wait_ge(lo_done, 4 * i + 2 * u + b + 1)
                        for k in range(4):
                            last = nc.tensor.transpose(bank[:, 2 * u + b, k * P:(k + 1) * P],
                                                       xs[:, u, (4 * b + k) * P:(4 * b + k + 1) * P], ident)
                        last.then_inc(turned, 1)


def three_pass(nc, out, ah, al, bh, bl, first, last):
    nc.tensor.matmul(out, ah, bh, start=first, stop=False)
    nc.tensor.matmul(out, ah, bl, start=False, stop=False)
    return nc.tensor.matmul(out, al, bh, start=False, stop=last)


def project(nc, sp, xh, xl, kb, loop_pairs, loop_cols, loop_dst, rest):
    raw = [sp.at("w_raw", kb + 8 * u, [P, KT, WC]) for u in range(2)]
    wh = [sp.at("w_hi", kb + 16 + 8 * u, [P, KT, WC], F32R) for u in range(2)]
    wl = [sp.at("w_lo", kb + 32 + 8 * u, [P, KT, WC], F32R) for u in range(2)]
    bank = sp.banks
    w_in = [sp.sem("w_in0"), sp.sem("w_in1")]
    hi_done, split, job, free_act, free_dve = (
        sp.sem(s) for s in ("w_hi_done", "w_split", "job", "bank_free_act", "bank_free_dve"))
    n_loop = 2 * loop_pairs
    arrived, count = {}, [16 * loop_pairs] * 2
    for r, (_, sources, _) in enumerate(rest):
        c = n_loop + r
        count[c % 2] += 16 * len(sources)
        arrived[c] = count[c % 2]

    def pieces(kind, j):
        if kind == "T" or (kind == "KV" and j < 2):
            return [(0, 512, j // 2, j % 2)]
        if kind == "V":
            return [(256 * z, 256, 2 * j + z, None) for z in range(2)]
        return [(128 * z, 128, 4 * (j - 2) + z, None) for z in range(4)]

    with nc.Block() as block:
        @block.sync
        def _(eng):
            with eng.Fori(0, loop_pairs) as i:
                for u in range(2):
                    eng.wait_ge(split, 2 * i + u + 1)
                    eng.dma_start(raw[u][:, :, :], loop_cols(2 * i + u)).then_inc(w_in[u], 16)
            for r, (_, sources, _) in enumerate(rest):
                c = n_loop + r
                eng.wait_ge(split, c + 1)
                for at, src in sources:
                    eng.dma_start(raw[c % 2][:, :, at:at + src.shape[2]], src).then_inc(w_in[c % 2], 16)

        def evacuate(eng, c, u, j, dst, copy, free):
            eng.wait_ge(job, 4 * c + j + 9)
            src = bank[:, 4 * u + j, :]
            if len(dst.shape) == 3:
                src = src.rearrange("p (a b) -> p a b", a=dst.shape[1])
            copy(dst, src).then_inc(free, 1)

        @block.scalar
        def _(eng):
            eng.sem_inc(free_act, 4)

            def hi(c, u, there):
                eng.wait_ge(w_in[u], there)
                eng.wait_ge(job, 4 * c + 4)
                nc.scalar.activation(wh[u][:, :, :], raw[u][:, :, :], ACT.Copy).then_inc(hi_done, 1)

            def out(c, u, dst):
                for j in range(2):
                    evacuate(eng, c, u, j, dst(j), lambda o, s: nc.scalar.activation(o, s, ACT.Copy), free_act)

            hi(0, 0, 16)
            with eng.Fori(0, loop_pairs - 1) as i:
                hi(2 * i + 1, 1, 16 * i + 16)
                out(2 * i, 0, lambda j: loop_dst(2 * i, j))
                hi(2 * i + 2, 0, 16 * i + 32)
                out(2 * i + 1, 1, lambda j: loop_dst(2 * i + 1, j))
            c = n_loop - 1
            hi(c, 1, 16 * loop_pairs)
            out(c - 1, 0, lambda j: loop_dst(c - 1, j))
            for r, (_, _, dst) in enumerate(rest):
                hi(n_loop + r, (n_loop + r) % 2, arrived[n_loop + r])
                before = (lambda j: loop_dst(c, j)) if r == 0 else rest[r - 1][2]
                out(n_loop + r - 1, (n_loop + r - 1) % 2, before)
            out(n_loop + len(rest) - 1, (n_loop + len(rest) - 1) % 2,
                rest[-1][2] if rest else lambda j: loop_dst(c, j))

        @block.vector
        def _(eng):
            eng.sem_inc(free_dve, 4)
            eng.sem_inc(split, 2)

            def lo(c, u):
                eng.wait_ge(hi_done, c + 1)
                nc.vector.tensor_tensor(wl[u][:, :, :], raw[u][:, :, :], f32(wh[u][:, :, :]),
                                        ALU.subtract).then_inc(split, 1)

            def out(c, u, dst):
                for j in range(2, 4):
                    evacuate(eng, c, u, j, dst(j), nc.vector.tensor_copy, free_dve)

            lo(0, 0)
            with eng.Fori(0, loop_pairs - 1) as i:
                lo(2 * i + 1, 1)
                out(2 * i, 0, lambda j: loop_dst(2 * i, j))
                lo(2 * i + 2, 0)
                out(2 * i + 1, 1, lambda j: loop_dst(2 * i + 1, j))
            c = n_loop - 1
            lo(c, 1)
            out(c - 1, 0, lambda j: loop_dst(c - 1, j))
            for r in range(len(rest)):
                lo(n_loop + r, (n_loop + r) % 2)
                before = (lambda j: loop_dst(c, j)) if r == 0 else rest[r - 1][2]
                out(n_loop + r - 1, (n_loop + r - 1) % 2, before)
            out(n_loop + len(rest) - 1, (n_loop + len(rest) - 1) % 2,
                rest[-1][2] if rest else lambda j: loop_dst(c, j))

        @block.tensor
        def _(eng):
            eng.sem_inc(job, 8)

            def chunk(c, u, kind):
                eng.wait_ge(split, c + 3)
                for j in range(4):
                    eng.wait_ge(free_act if j < 2 else free_dve, 2 * c + j % 2 + 1)
                    for at, n, tile, half in pieces(kind, j):
                        for k in range(KT):
                            o = bank[:, 4 * u + j, at:at + n]
                            if half is None:
                                t = slice(tile * P, (tile + 1) * P)
                                cols = slice(0, WC) if kind == "V" else slice(P, WC)
                                last = three_pass(nc, o, xh[:, k, t], xl[:, k, t], wh[u][:, k, cols],
                                                  wl[u][:, k, cols], k == 0, k == KT - 1)
                            else:
                                w = slice(tile * P, (tile + 1) * P)
                                t = slice(half * HALF, (half + 1) * HALF)
                                last = three_pass(nc, o, wh[u][:, k, w], wl[u][:, k, w], xh[:, k, t],
                                                  xl[:, k, t], k == 0, k == KT - 1)
                    last.then_inc(job, 1)

            with eng.Fori(0, loop_pairs) as i:
                for u in range(2):
                    chunk(2 * i + u, u, "T")
            for r, (kind, _, _) in enumerate(rest):
                chunk(n_loop + r, (n_loop + r) % 2, kind)


def attention(nc, sp, ident, table, qkT, va, vb, sinks, diff_lambda):
    tab = sp.at("tables", 136, [P, C_END - C_SWA])
    s = [sp.at("scores", 160 + 8 * u, [P, 2, 1024]) for u in range(2)]
    wt = [sp.at("weights", 176 + 4 * u, [P, 1024]) for u in range(2)]
    wT = [sp.at("weightsT", 184 + 4 * u, [P, 1024]) for u in range(2)]
    sink = sp.at("sink", 192, [P, SWA_HEADS])
    lp = sp.at("lambda_parts", 192.25, [P, 4, HD])
    lprod = sp.at("lambda_products", 193.25, [P, 2, HD])
    lam = sp.at("lambda_small", 193.75, [P, 8])
    mx, ng, sm, rc = (sp.at(n, 194 + 0.25 * m, [P, 2, 2]) for m, n in enumerate(("max", "negmax", "sum", "recip")))
    es = sp.at("sink_term", 195, [P, 2, 2])
    rl = sp.at("lambda_recip", 195.25, [P, 2])
    bank = sp.banks
    s_ps = bank[:, 0:4, :].rearrange("p (m b) c -> p m (b c)", m=2)
    t_ps = bank[:, 4:6, :].rearrange("p b c -> p (b c)")
    o_ps = [bank[:, 6, 0:P], bank[:, 7, 0:P]]

    items = []
    for i in range(TT):
        for j in range(4):
            k0 = max(0, i - 1)
            items.append(("swa", i, j, list(range(k0, i + 1))))
        for h in range(DIFF_HEADS):
            items.append(("diff", i, h, list(range(i + 1))))
    N = len(items)
    tables_in, small_in, lam_sum, lam_exp, lam_ready = (
        sp.sem(n) for n in ("tables_in", "small_in", "lam_sum", "lam_exp", "lam_ready"))
    scored, masked, exped, weighed, turned, out_t, valued, out_o, dve = (
        sp.sem(n) for n in ("scored", "masked", "exped", "weighed", "turned", "wT_ready", "valued", "o_out", "dve"))

    def q_tile(kind, h):
        return (T_QA if kind == "swa" else T_QB) + h

    with nc.Block() as block:
        @block.sync
        def _(eng):
            eng.dma_start(tab[:, :], table[:, C_SWA:C_END]).then_inc(tables_in, 16)
            eng.dma_start(sink[:, :], sinks[0].partition_broadcast(P)).then_inc(small_in, 16)
            eng.dma_start(lp[:, :, :], diff_lambda[0].partition_broadcast(P)).then_inc(small_in, 16)

        @block.tensor
        def _(eng):
            def scores(n):
                kind, i, h, kts = items[n]
                if n >= 1:
                    eng.wait_ge(masked, n)
                k_tile = T_KA if kind == "swa" else T_KB + h
                for m in range(2):
                    r = slice(m * HD, (m + 1) * HD)
                    k0, k1 = kts[0] * P, (kts[-1] + 1) * P
                    for a in range(k0, k1, 512):
                        b = min(k1, a + 512)
                        last = nc.tensor.matmul(s_ps[:, m, a - k0:b - k0], qkT[r, q_tile(kind, h), i * P:(i + 1) * P],
                                                qkT[r, k_tile, a:b], start=True, stop=True)
                last.then_inc(scored, 1)

            def turn(n):
                kind, i, h, kts = items[n]
                eng.wait_ge(weighed, n + 1)
                if n >= 1:
                    eng.wait_ge(out_t, n)
                blocks = len(kts) * (2 if kind == "swa" else 1)
                for b in range(blocks):
                    last = nc.tensor.transpose(t_ps[:, b * P:(b + 1) * P], wt[n % 2][:, b * P:(b + 1) * P], ident)
                last.then_inc(turned, 1)

            def values(n):
                kind, i, h, kts = items[n]
                eng.wait_ge(out_t, n + 1)
                if n >= 2:
                    eng.wait_ge(out_o, n - 1)
                if kind == "swa":
                    for a in range(2):
                        r = slice(a * HD, (a + 1) * HD)
                        for b, kt in enumerate(kts):
                            at = (a * len(kts) + b) * P
                            last = nc.tensor.matmul(o_ps[n % 2][r, :], va[:, kt, r], wT[n % 2][:, at:at + P],
                                                    start=b == 0, stop=b == len(kts) - 1)
                else:
                    for b, kt in enumerate(kts):
                        last = nc.tensor.matmul(o_ps[n % 2], vb[:, kt, h * P:(h + 1) * P],
                                                wT[n % 2][:, b * P:(b + 1) * P], start=b == 0, stop=b == len(kts) - 1)
                last.then_inc(valued, 1)

            scores(0)
            scores(1)
            for n in range(N):
                if n + 2 < N:
                    scores(n + 2)
                if n >= 1:
                    values(n - 1)
                turn(n)
            values(N - 1)

        @block.vector
        def _(eng):
            count = [0]

            def link(ins):
                count[0] += 1
                ins.then_inc(dve, 1)
                eng.wait_ge(dve, count[0])

            eng.wait_ge(small_in, 32)
            for m in range(2):
                nc.vector.tensor_tensor_reduce(out=lprod[:, m, :], in0=lp[:, 2 * m, :], in1=lp[:, 2 * m + 1, :],
                                               scale=1.0, scalar=0.0, op0=ALU.mult, op1=ALU.add,
                                               accum_out=lam[:, m:m + 1]).then_inc(lam_sum, 1)
            eng.wait_ge(lam_exp, 1)
            link(nc.vector.tensor_tensor(lam[:, 4:5], lam[:, 3:4], lam[:, 2:3], ALU.subtract))
            link(nc.vector.tensor_scalar(lam[:, 5:6], lam[:, 4:5], LAMBDA_INIT, None, ALU.subtract))
            eng.wait_ge(tables_in, 16)

            def mask(n):
                kind, i, h, kts = items[n]
                u, k = n % 2, len(kts) * P
                eng.wait_ge(scored, n + 1)
                if n >= 2:
                    eng.wait_ge(weighed, n - 1)
                for m in range(2):
                    if kind == "swa":
                        at = (2 * h + m) * 256 + 256 - k
                    else:
                        at = C_DIFF - C_SWA + h * 1024 + 1024 - k
                    last = nc.vector.tensor_tensor_reduce(
                        out=s[u][:, m, 0:k], in0=s_ps[:, m, 0:k], in1=tab[:, at:at + k], scale=0.125,
                        scalar=LOWEST, op0=ALU.add, op1=ALU.max, accum_out=mx[:, u, m:m + 1])
                link(last)
                if kind == "swa":
                    link(nc.vector.tensor_tensor(mx[:, u, :], mx[:, u, :], sink[:, h:h + 5:4], ALU.max))
                    nc.vector.tensor_tensor(es[:, u, :], sink[:, h:h + 5:4], mx[:, u, :], ALU.subtract)
                nc.vector.tensor_scalar(ng[:, u, :], mx[:, u, :], -1.0, None, ALU.mult).then_inc(masked, 1)

            def weigh(n):
                kind, i, h, kts = items[n]
                u, k = n % 2, len(kts) * P
                eng.wait_ge(exped, n + 1)
                if kind == "swa":
                    link(nc.vector.tensor_tensor(sm[:, u, :], sm[:, u, :], es[:, u, :], ALU.add))
                link(nc.vector.reciprocal(rc[:, u, :], sm[:, u, :]))
                if n >= 2:
                    eng.wait_ge(turned, n - 1)
                if kind == "swa":
                    nc.vector.tensor_scalar(wt[u][:, 0:k], s[u][:, 0, 0:k], rc[:, u, 0:1], None, ALU.mult)
                    nc.vector.tensor_scalar(wt[u][:, k:2 * k], s[u][:, 1, 0:k], rc[:, u, 1:2], None,
                                            ALU.mult).then_inc(weighed, 1)
                else:
                    nc.vector.tensor_tensor(rl[:, u:u + 1], rc[:, u, 1:2], lam[:, 5:6], ALU.mult)
                    link(nc.vector.tensor_scalar(wt[u][:, 0:k], s[u][:, 0, 0:k], rc[:, u, 0:1], None, ALU.mult))
                    nc.vector.scalar_tensor_tensor(
                        out=wt[u][:, 0:k], in0=s[u][:, 1, 0:k], scalar=rl[:, u:u + 1], in1=wt[u][:, 0:k],
                        op0=ALU.mult, op1=ALU.add).then_inc(weighed, 1)

            def output(n):
                kind, i, h, _ = items[n]
                eng.wait_ge(valued, n + 1)
                nc.vector.tensor_copy(qkT[:, q_tile(kind, h), i * P:(i + 1) * P], o_ps[n % 2]).then_inc(out_o, 1)

            mask(0)
            for n in range(N):
                if n + 1 < N:
                    mask(n + 1)
                weigh(n)
                if n >= 2:
                    output(n - 2)
            output(N - 2)
            output(N - 1)

        @block.scalar
        def _(eng):
            eng.wait_ge(lam_sum, 2)
            nc.scalar.activation(lam[:, 2:4], lam[:, 0:2], ACT.Exp).then_inc(lam_exp, 1)

            def exps(n):
                kind, i, h, kts = items[n]
                u, k = n % 2, len(kts) * P
                eng.wait_ge(masked, n + 1)
                for m in range(2):
                    last = nc.scalar.activation(s[u][:, m, 0:k], s[u][:, m, 0:k], ACT.Exp, bias=ng[:, u, m:m + 1],
                                                accum_out=sm[:, u, m:m + 1])
                if kind == "swa":
                    last = nc.scalar.activation(es[:, u, :], es[:, u, :], ACT.Exp)
                last.then_inc(exped, 1)

            def out_turned(n):
                kind, i, h, kts = items[n]
                c = len(kts) * P * (2 if kind == "swa" else 1)
                eng.wait_ge(turned, n + 1)
                if n >= 2:
                    eng.wait_ge(valued, n - 1)
                nc.scalar.activation(wT[n % 2][:, 0:c], t_ps[:, 0:c], ACT.Copy).then_inc(out_t, 1)

            exps(0)
            for n in range(N):
                if n + 1 < N:
                    exps(n + 1)
                out_turned(n)


def finish_heads(nc, sp, oT, oh, ol, subln_g):
    sq = sp.at("head_squares", 160, [P, 4, T])
    sd = sp.at("head_std", 176, [P, 2, T])
    ones = sp.at("mean_matrix", 184, [P, P])
    g = sp.at("subln_gain", 184.5, [P, 2])
    eps = sp.at("head_eps", 184.75, [P, 1])
    bank = sp.banks
    g_in, made, squared, meaned, std, dve, hi_swa, hi_diff = (
        sp.sem(n) for n in ("g_in", "const_set", "squared", "meaned", "std", "dve", "hi_swa", "hi_diff"))
    pair = [bank[:, 2 * h:2 * h + 2, :].rearrange("p b c -> p (b c)") for h in range(4)]

    with nc.Block() as block:
        @block.sync
        def _(eng):
            with nc.allow_non_contiguous_dma(reason="128 gains, one to a partition"):
                eng.dma_start(g[:, 0:1], subln_g.rearrange("o d -> d o")).then_inc(g_in, 16)

        @block.scalar
        def _(eng):
            for h in range(4):
                nc.scalar.activation(sq[:, h, :], oT[:, T_QB + h, :], ACT.Square).then_inc(squared, 1)
            eng.wait_ge(made, 2)
            for h in range(4):
                eng.wait_ge(meaned, h + 1)
                if h >= 2:
                    eng.wait_ge(dve, 4 * (h - 1) + 1)
                nc.scalar.activation(sd[:, h % 2, :], pair[h], ACT.Sqrt, bias=eps[:, 0:1]).then_inc(std, 1)
            for h in range(4):
                nc.scalar.activation(oh[:, h, :], oT[:, T_QA + h, :], ACT.Copy).then_inc(hi_swa, 1)

        @block.vector
        def _(eng):
            nc.vector.memset(ones[:, :], 1.0 / P).then_inc(made, 1)
            nc.vector.memset(eps[:, :], EPS).then_inc(made, 1)
            count = [0]

            def link(ins):
                count[0] += 1
                ins.then_inc(dve, 1)
                eng.wait_ge(dve, count[0])

            eng.wait_ge(g_in, 16)
            link(nc.vector.tensor_scalar(g[:, 1:2], g[:, 0:1], 1.0 - LAMBDA_INIT, None, ALU.mult))
            for h in range(4):
                eng.wait_ge(std, h + 1)
                r, o = sd[:, h % 2, :], oT[:, T_QB + h, :]
                link(nc.vector.reciprocal(r, r))
                link(nc.vector.tensor_tensor(r, o, r, ALU.mult))
                link(nc.vector.tensor_scalar(oh[:, 4 + h, :], r, g[:, 1:2], None, ALU.mult))
                link(nc.vector.scalar_tensor_tensor(out=ol[:, 4 + h, :], in0=r, scalar=g[:, 1:2],
                                                    in1=f32(oh[:, 4 + h, :]), op0=ALU.mult, op1=ALU.subtract))
            for h in range(4):
                eng.wait_ge(hi_swa, h + 1)
                nc.vector.tensor_tensor(ol[:, h, :], oT[:, T_QA + h, :], f32(oh[:, h, :]), ALU.subtract)

        @block.tensor
        def _(eng):
            eng.wait_ge(made, 1)
            for h in range(4):
                eng.wait_ge(squared, h + 1)
                for b in range(2):
                    last = nc.tensor.matmul(bank[:, 2 * h + b, :], ones[:, :], sq[:, h, b * 512:(b + 1) * 512],
                                            start=True, stop=True)
                last.then_inc(meaned, 1)


def gate_and_up(nc, sp, xh, xl, oh, ol, mT, w_in, gate_bias, w_up_a, w_up_b):
    raw = [sp.at("gate_raw", 160 + 4 * s, [P, KT, P]) for s in range(3)]
    wh = [sp.at("gate_hi", 172 + 4 * s, [P, KT, P], F32R) for s in range(3)]
    wl = [sp.at("gate_lo", 184 + 4 * s, [P, KT, P], F32R) for s in range(3)]
    sg = [sp.at("sigmoid", 196 + 4 * s, [P, T]) for s in range(2)]
    bias = sp.at("gate_bias", 204, [P, 16])
    bank = sp.banks
    pair = [bank[:, 2 * s:2 * s + 2, :].rearrange("p b c -> p (b c)") for s in range(4)]
    w_in3 = w_in.rearrange("(k p) c -> p k c", p=P)
    ua = w_up_a.rearrange("(a j c) n -> a c j n", a=2, c=HD)
    ub = w_up_b.rearrange("(k p) n -> p k n", p=P)
    loaded = [sp.sem(f"loaded{s}") for s in range(3)]
    hi_done = [sp.sem(f"hi_done{s}") for s in range(3)]
    split = [sp.sem(f"split{s}") for s in range(3)]
    multiplied = [sp.sem(f"multiplied{s}") for s in range(3)]
    squashed = [sp.sem(f"squashed{s}") for s in range(2)]
    sig_free, bias_in, mixed = sp.sem("sig_free"), sp.sem("bias_in"), sp.sem("mixed")

    with nc.Block() as block:
        @block.sync
        def _(eng):
            with nc.allow_non_contiguous_dma(reason="2048 biases, one to a partition"):
                eng.dma_start(bias[:, :], gate_bias.rearrange("o (t p) -> p (o t)", p=P)).then_inc(bias_in, 16)
            with eng.Fori(0, KT) as j:
                for s in range(2):
                    eng.wait_ge(split[s], j + 1)
                    eng.dma_start(raw[s][:, :, :], w_in3[:, :, ds(GL + s * D + j * P, P)]).then_inc(loaded[s], 16)
                eng.wait_ge(split[2], j + 1)
                for a in (1, 0):
                    eng.dma_start(raw[2][a * HD:(a + 1) * HD, 0:4, :], ua[a, :, :, ds(j * P, P)]).then_inc(loaded[2], 16)
                eng.dma_start(raw[2][:, 4:8, :], ub[:, :, ds(j * P, P)]).then_inc(loaded[2], 16)

        @block.scalar
        def _(eng):
            eng.wait_ge(bias_in, 16)
            with eng.Fori(0, KT) as j:
                for s in range(3):
                    eng.wait_ge(loaded[s], (16 if s < 2 else 48) * (j + 1))
                    eng.wait_ge(multiplied[s], j + 1)
                    nc.scalar.activation(wh[s][:, :, :], raw[s][:, :, :], ACT.Copy).then_inc(hi_done[s], 1)
                eng.wait_ge(sig_free, j + 1)
                for s in range(2):
                    eng.wait_ge(multiplied[s], j + 2)
                    nc.scalar.activation(sg[s][:, :], pair[s], ACT.Sigmoid,
                                         bias=bias[:, ds(8 * s + j, 1)]).then_inc(squashed[s], 1)

        @block.vector
        def _(eng):
            for s in range(3):
                eng.sem_inc(split[s], 1)
            eng.sem_inc(sig_free, 1)
            with eng.Fori(0, KT) as j:
                for s in range(3):
                    eng.wait_ge(hi_done[s], j + 1)
                    nc.vector.tensor_tensor(wl[s][:, :, :], raw[s][:, :, :], f32(wh[s][:, :, :]),
                                            ALU.subtract).then_inc(split[s], 1)
                eng.wait_ge(multiplied[2], j + 2)
                for s in range(2):
                    eng.wait_ge(squashed[s], j + 1)
                    nc.vector.tensor_tensor(sg[s][:, :], sg[s][:, :], pair[2 + s], ALU.mult).then_inc(mixed, 1)
                eng.wait_ge(mixed, 2 * j + 2)
                nc.vector.tensor_tensor(mT[:, ds(j, 1), :].rearrange("p o t -> p (o t)"), sg[0][:, :], sg[1][:, :],
                                        ALU.add).then_inc(sig_free, 1)

        @block.tensor
        def _(eng):
            for s in range(3):
                eng.sem_inc(multiplied[s], 1)
            with eng.Fori(0, KT) as j:
                for s in range(2):
                    eng.wait_ge(split[s], j + 2)
                    if s == 0:
                        eng.wait_ge(sig_free, j + 1)
                    for half in range(2):
                        t = slice(half * HALF, (half + 1) * HALF)
                        for k in range(KT):
                            last = three_pass(nc, bank[:, 2 * s + half, :], wh[s][:, k, :], wl[s][:, k, :],
                                              xh[:, k, t], xl[:, k, t], k == 0, k == KT - 1)
                    last.then_inc(multiplied[s], 1)
                eng.wait_ge(split[2], j + 2)
                for s in range(2):
                    for half in range(2):
                        t = slice(half * HALF, (half + 1) * HALF)
                        for k in range(4 * s, 4 * s + 4):
                            last = three_pass(nc, bank[:, 4 + 2 * s + half, :], wh[2][:, k, :], wl[2][:, k, :],
                                              oh[:, k, t], ol[:, k, t], k == 4 * s, k == 4 * s + 3)
                last.then_inc(multiplied[2], 1)


def mix_out(nc, sp, mT, x, w_out, x1):
    mh = [sp.at("merged_hi", 4 * u, [P, KT, P], F32R) for u in range(2)]
    ml = [sp.at("merged_lo", 8 + 4 * u, [P, KT, P], F32R) for u in range(2)]
    raw = [sp.at("wo_raw", 16 + 8 * u, [P, KT, WC]) for u in range(2)]
    wh = sp.at("wo_hi", 96, [P, KT, D], F32R)
    wl = sp.at("wo_lo", 128, [P, KT, D], F32R)
    xr = [sp.at("residual", 160 + 4 * u, [P, D]) for u in range(2)]
    y = [sp.at("x1_tile", 168 + 4 * u, [P, D]) for u in range(2)]
    bank = sp.banks
    pair = [bank[:, 2 * u:2 * u + 2, :].rearrange("p b c -> p (b c)") for u in range(2)]
    wo = w_out.rearrange("(k p) c -> p k c", p=P)
    xt = x.rearrange("(t p) d -> t p d", p=P)
    x1t = x1.rearrange("(t p) d -> t p d", p=P)
    w_in = [sp.sem("wo_in0"), sp.sem("wo_in1")]
    x_in = [sp.sem("x_in0"), sp.sem("x_in1")]
    stored = [sp.sem("stored0"), sp.sem("stored1")]
    w_hi, w_lo, m_hi, m_lo, multiplied, added, y_free = (
        sp.sem(n) for n in ("w_hi", "w_lo", "m_hi", "m_lo", "multiplied", "added", "y_free"))
    NC = D // WC

    with nc.Block() as block:
        @block.sync
        def _(eng):
            for c in range(NC):
                if c >= 2:
                    eng.wait_ge(w_lo, c - 1)
                eng.dma_start(raw[c % 2][:, :, :], wo[:, :, c * WC:(c + 1) * WC]).then_inc(w_in[c % 2], 16)
            with eng.Fori(0, TT // 2) as i:
                for u in range(2):
                    eng.wait_ge(added, 2 * i + u + 1)
                    eng.dma_start(xr[u][:, :], xt[2 * i + u, :, :]).then_inc(x_in[u], 16)

        @block.gpsimd
        def _(eng):
            eng.sem_inc(y_free, 2)
            with eng.Fori(0, TT // 2) as i:
                for u in range(2):
                    eng.wait_ge(added, 2 * i + u + 3)
                    eng.dma_start(x1t[2 * i + u, :, :], y[u][:, :]).then_inc(stored[u], 16)
                    eng.wait_ge(stored[u], 16 * i + 16)
                    eng.sem_inc(y_free, 1)

        @block.scalar
        def _(eng):
            for c in range(NC):
                eng.wait_ge(w_in[c % 2], 16 * (c // 2) + 16)
                nc.scalar.activation(wh[:, :, c * WC:(c + 1) * WC], raw[c % 2][:, :, :], ACT.Copy).then_inc(w_hi, 1)
            with eng.Fori(0, TT // 2) as i:
                for u in range(2):
                    eng.wait_ge(multiplied, 2 * i + u + 1)
                    nc.scalar.activation(mh[u][:, :, :], mT[:, :, ds((2 * i + u) * P, P)], ACT.Copy).then_inc(m_hi, 1)

        @block.vector
        def _(eng):
            eng.sem_inc(added, 2)
            for c in range(NC):
                eng.wait_ge(w_hi, c + 1)
                at = (slice(None), slice(None), slice(c * WC, (c + 1) * WC))
                nc.vector.tensor_tensor(wl[at], raw[c % 2][:, :, :], f32(wh[at]), ALU.subtract).then_inc(w_lo, 1)

            def split(t, u):
                eng.wait_ge(m_hi, t + 1)
                nc.vector.tensor_tensor(ml[u][:, :, :], mT[:, :, ds(t * P, P)], f32(mh[u][:, :, :]),
                                        ALU.subtract).then_inc(m_lo, 1)

            def add(t, i, u):
                eng.wait_ge(multiplied, t + 3)
                eng.wait_ge(x_in[u], 16 * i + 16)
                eng.wait_ge(y_free, t + 1)
                nc.vector.tensor_tensor(y[u][:, :], pair[u], xr[u][:, :],
                                        ALU.add).then_inc(added, 1)

            split(0, 0)
            with eng.Fori(0, TT // 2 - 1) as i:
                split(2 * i + 1, 1)
                add(2 * i, i, 0)
                split(2 * i + 2, 0)
                add(2 * i + 1, i, 1)
            split(TT - 1, 1)
            add(TT - 2, TT // 2 - 1, 0)
            add(TT - 1, TT // 2 - 1, 1)

        @block.tensor
        def _(eng):
            eng.sem_inc(multiplied, 2)
            eng.wait_ge(w_lo, NC)

            def tile(t, u):
                eng.wait_ge(m_lo, t + 1)
                eng.wait_ge(added, t + 1)
                for b in range(2):
                    c = slice(b * 512, (b + 1) * 512)
                    for k in range(KT):
                        last = three_pass(nc, bank[:, 2 * u + b, :], mh[u][:, k, :], ml[u][:, k, :],
                                          wh[:, k, c], wl[:, k, c], k == 0, k == KT - 1)
                last.then_inc(multiplied, 1)

            with eng.Fori(0, TT // 2) as i:
                for u in range(2):
                    tile(2 * i + u, u)


def turn_subkeys(nc, sp, ident, subkeys, skT):
    raw = sp.at("subkeys", 128, [P, HP, P])
    bank = sp.banks
    key_in, turned = sp.sem("key_in"), sp.sem("turned")
    with nc.Block() as block:
        @block.sync
        def _(eng):
            eng.dma_start(raw[:, :, :], subkeys.rearrange("h q n d -> n (h q) d")).then_inc(key_in, 16)

        @block.tensor
        def _(eng):
            eng.wait_ge(key_in, 16)
            for hp in range(HP):
                last = nc.tensor.transpose(bank[:, hp // 4, (hp % 4) * P:(hp % 4 + 1) * P], raw[:, hp, :], ident)
            last.then_inc(turned, 1)

        @block.scalar
        def _(eng):
            eng.wait_ge(turned, 1)
            nc.scalar.activation(skT[:, :, :], bank[:, 0:4, :].rearrange("p b (q n) -> p (b q) n", n=P), ACT.Copy)


def select_experts(nc, sp, ident, qT, skT, picks, table, kb):
    qs = sp.at("q_tile", kb, [P, HP, P])
    s = sp.at("key_scores", kb + 8, [P, HP, NK])
    s2 = sp.at("key_scores_left", kb + 16, [P, HP, NK])
    cand = sp.at("candidates", kb + 24, [P, PH, TOPK, TOPK])
    cand2 = sp.at("candidates_left", kb + 32, [P, PH, TOPK, TOPK])
    hot = sp.at("rank_match", kb + 40, [P, PH, TOPK, TOPK])
    top = sp.at("top", kb + 48, [P, HP, TOPK])
    top_i = sp.at("top_index", kb + 49, [P, HP, TOPK], U32)
    top_f = sp.at("top_index_f", kb + 50, [P, HP, TOPK])
    best = sp.at("best", kb + 51, [P, PH, TOPK])
    best_i = sp.at("best_index", kb + 51.5, [P, PH, TOPK], U32)
    rank_i = sp.at("rank", kb + 52, [P, 2, PH, TOPK], U32)
    rank_f = sp.at("rank_f", kb + 53, [P, 2, PH, TOPK])
    e = sp.at("best_exp", kb + 54, [P, PH, TOPK])
    found = sp.at("found", kb + 54.5, [P, 3, PH * TOPK])
    norm = sp.at("best_norm", kb + 56, [P, 2, PH])
    iota16 = sp.at("iota16", kb + 56.25, [P, TOPK])
    bank = sp.banks
    iota_in, q_here, scored, s_here, exp_in, exped, found_all, turned, picked, dve = (
        sp.sem(n) for n in ("iota_in", "q_here", "scored", "s_here", "exp_in", "exped", "found_all", "turned",
                            "picked", "dve"))
    s_free, steady = sp.sem("s_free"), sp.sem("steady")
    LINKS = 24

    with nc.Block() as block:
        @block.sync
        def _(eng):
            eng.dma_start(iota16[:, :], table[:, C_IOTA16:C_IOTA16 + TOPK]).then_inc(iota_in, 16)

        @block.gpsimd
        def _(eng):
            with eng.Fori(0, TT) as t:
                eng.wait_ge(scored, t + 1)
                nc.gpsimd.tensor_copy(qs[:, :, :], qT[:, :, ds(t * P, P)]).then_inc(q_here, 1)

        @block.tensor
        def _(eng):
            eng.sem_inc(scored, 1)
            with eng.Fori(0, TT) as t:
                eng.wait_ge(q_here, t + 1)
                eng.wait_ge(s_here, t + 1)
                for hp in range(HP):
                    last = nc.tensor.matmul(bank[:, hp // 4, (hp % 4) * P:(hp % 4 + 1) * P], qs[:, hp, :],
                                            skT[:, hp, :], start=True, stop=True)
                last.then_inc(scored, 1)
                eng.wait_ge(found_all, t + 1)
                eng.wait_ge(picked, t + 1)
                for m in range(3):
                    last = nc.tensor.transpose(bank[:, 4, m * P:(m + 1) * P], found[:, m, :], ident)
                last.then_inc(turned, 1)

        @block.scalar
        def _(eng):
            eng.sem_inc(s_here, 1)
            eng.sem_inc(picked, 1)
            with eng.Fori(0, TT) as t:
                eng.wait_ge(scored, t + 2)
                eng.wait_ge(s_free, t + 1)
                nc.scalar.activation(s[:, :, :], bank[:, 0:4, :].rearrange("p b (q n) -> p (b q) n", n=NK),
                                     ACT.Copy).then_inc(s_here, 1)
                eng.wait_ge(exp_in, t + 1)
                nc.scalar.activation(e[:, :, :], e[:, :, :], ACT.Exp).then_inc(exped, 1)
                eng.wait_ge(turned, t + 1)
                nc.scalar.activation(picks[:, :, ds(t * P, P)],
                                     bank[:, 4, 0:3 * P].rearrange("p (m t) -> p m t", m=3),
                                     ACT.Copy).then_inc(picked, 1)

        @block.vector
        def _(eng):
            eng.sem_inc(s_free, 1)
            eng.wait_ge(iota_in, 16)
            with eng.Fori(0, TT) as t:
                n = [0]

                def link(ins):
                    n[0] += 1
                    ins.then_inc(dve, 1)
                    eng.wait_ge(dve, LINKS * t + n[0])
                    eng.sem_inc(steady, 1)

                def top16(rows, values, left, out, out_i, after=None):
                    for r in range(rows):
                        last = nc.vector.max(out[:, r, 0:8], values(r))
                    link(last)
                    for r in range(rows):
                        nc.vector.max_index(out_i[:, r, 0:8], out[:, r, 0:8], values(r))
                    for r in range(rows):
                        last = nc.vector.match_replace(left(r), out[:, r, 0:8], values(r), LOWEST)
                    link(last)
                    if after is not None:
                        after()
                    for r in range(rows):
                        last = nc.vector.max(out[:, r, 8:16], left(r))
                    link(last)
                    for r in range(rows):
                        last = nc.vector.max_index(out_i[:, r, 8:16], out[:, r, 8:16], left(r))
                    link(last)

                eng.wait_ge(s_here, t + 2)
                eng.sem_inc(steady, 1)
                top16(HP, lambda r: s[:, r, :], lambda r: s2[:, r, :], top, top_i,
                      lambda: eng.sem_inc(s_free, 1))
                nc.vector.tensor_copy(top_f[:, :, :], top_i[:, :, :])
                a = top[:, :, :].rearrange("p (h q) k -> p h q k", q=2)
                link(nc.vector.tensor_tensor(
                    cand[:, :, :, :],
                    rep(a[:, :, 0, :], 3, TOPK), rep(a[:, :, 1, :], 2, TOPK),
                    ALU.add))
                top16(PH, lambda r: cand[:, r, :, :].rearrange("p a b -> p (a b)"),
                      lambda r: cand2[:, r, :, :].rearrange("p a b -> p (a b)"), best, best_i)
                nc.vector.tensor_tensor(e[:, :, :], best[:, :, :], rep(best[:, :, 0], 2, TOPK),
                                        ALU.subtract).then_inc(exp_in, 1)
                nc.vector.tensor_single_scalar(rank_i[:, 0, :, :], best_i[:, :, :], 4, ALU.logical_shift_right)
                link(nc.vector.tensor_single_scalar(rank_i[:, 1, :, :], best_i[:, :, :], 15, ALU.bitwise_and))
                link(nc.vector.tensor_copy(rank_f[:, :, :, :].rearrange("p q h k -> p (q h k)"),
                                           rank_i[:, :, :, :].rearrange("p q h k -> p (q h k)")))
                f = top_f[:, :, :].rearrange("p (h q) k -> p h q k", q=2)
                for q in range(2):
                    link(nc.vector.tensor_tensor(
                        hot[:, :, :, :].rearrange("p h k r -> p (h k) r"),
                        rep(rank_f[:, q, :, :].rearrange("p h k -> p (h k)"), 2, TOPK),
                        rep(iota16[:, :], 1, PH * TOPK), ALU.is_equal))
                    link(nc.vector.tensor_tensor(hot[:, :, :, :], hot[:, :, :, :],
                                                 rep(f[:, :, q, :], 2, TOPK), ALU.mult))
                    link(nc.vector.tensor_reduce(found[:, q, :], hot[:, :, :, :].rearrange("p h k r -> p (h k) r"),
                                                 axis=AX.X, op=ALU.add))
                eng.wait_ge(exped, t + 1)
                link(nc.vector.tensor_reduce(norm[:, 0, :], e[:, :, :], axis=AX.X, op=ALU.add))
                link(nc.vector.reciprocal(norm[:, 1, :], norm[:, 0, :]))
                nc.vector.tensor_tensor(found[:, 2, :].rearrange("p (h k) -> p h k", h=PH), e[:, :, :],
                                        rep(norm[:, 1, :], 2, TOPK), ALU.mult).then_inc(found_all, 1)
                eng.wait_ge(turned, t + 1)
                assert n[0] <= LINKS, n[0]
                if n[0] < LINKS:
                    eng.sem_inc(dve, LINKS - n[0])


def expert_weights(nc, sp, picks, table, gd, kb):
    iota = sp.at("iota", kb, [P, NK])
    wlo = sp.at("pick_weight_lo", kb + 0.5, [P, T])
    z_a = sp.at("first_hot", kb + 5, [P, 8, NK], F32R)
    z_h = sp.at("second_hot_hi", kb + 9, [P, 8, NK], F32R)
    z_l = sp.at("second_hot_lo", kb + 13, [P, 8, NK], F32R)
    stage = [sp.at("weights_stage", 64 + 64 * u, [P, NK, P]) for u in range(2)]
    key4 = sp.at("first_keys", 206, [P, 2, 4])
    keys, steady = sp.sem("first_keys_here"), sp.sem("steady")
    whi = sp.at("pick_weight_hi", kb + 17, [P, T], F32R)
    bank = sp.banks
    iota_in, w_hi, w_split, hot_a, hot_b, used, out = (
        sp.sem(n) for n in ("iota_in", "w_hi", "w_split", "hot_a", "hot_b", "hot_used", "g_out"))
    stored = [sp.sem("stored0"), sp.sem("stored1")]
    TURNS = P // 8

    with nc.Block() as block:
        @block.sync
        def _(eng):
            eng.dma_start(iota[:, :], table[:, C_IOTA:C_IOTA + NK]).then_inc(iota_in, 16)
            with eng.Fori(0, TT // 2) as i:
                for u in range(2):
                    eng.wait_ge(out, (2 * i + u + 1) * 2 * TURNS + 2)
                    eng.dma_start(gd[:, :, ds((2 * i + u) * P, P)].rearrange("a b t -> b a t"),
                                  stage[u][:, :, :]).then_inc(stored[u], 16)
            for u in range(2):
                eng.wait_ge(stored[u], 16 * (TT // 2) + 16)

        @block.gpsimd
        def _(eng):
            eng.wait_ge(iota_in, 16)
            with eng.Fori(0, T // 8) as n:
                for q in range(2):
                    eng.wait_ge(used, 2 * n + q + 1)
                    nc.gpsimd.tensor_copy(key4[:, q, :], picks[:, 0, ds(8 * n + 4 * q, 4)]).then_inc(keys, 1)
                    eng.wait_ge(keys, 2 * n + q + 1)
                    eng.sem_inc(steady, 1)
                    for z in range(4):
                        last = nc.gpsimd.tensor_scalar(z_a[:, 4 * q + z, :], iota[:, :], key4[:, q, z:z + 1], None,
                                                       ALU.is_equal)
                    last.then_inc(hot_a, 1)

        @block.vector
        def _(eng):
            eng.wait_ge(iota_in, 16)
            nc.vector.tensor_copy(whi[:, :], picks[:, 2, :]).then_inc(w_hi, 1)
            eng.wait_ge(w_hi, 1)
            nc.vector.tensor_tensor(wlo[:, :], picks[:, 2, :], f32(whi[:, :]), ALU.subtract).then_inc(w_split, 1)
            eng.wait_ge(w_split, 1)
            with eng.Fori(0, T // 8) as n:
                for q in range(2):
                    eng.wait_ge(used, 2 * n + q + 1)
                    for z in range(4 * q, 4 * q + 4):
                        key = picks[:, 1, ds(8 * n + z, 1)]
                        nc.vector.tensor_scalar(z_h[:, z, :], iota[:, :], key, picks[:, 2, ds(8 * n + z, 1)],
                                                ALU.is_equal, ALU.mult)
                        last = nc.vector.tensor_scalar(z_l[:, z, :], iota[:, :], key, wlo[:, ds(8 * n + z, 1)],
                                                       ALU.is_equal, ALU.mult)
                    last.then_inc(hot_b, 1)

        @block.tensor
        def _(eng):
            eng.sem_inc(used, 2)
            with eng.Fori(0, T // 8) as n:
                for q in range(2):
                    eng.wait_ge(hot_a, 2 * n + q + 1)
                    eng.wait_ge(hot_b, 2 * n + q + 1)
                    for z in range(4 * q, 4 * q + 4):
                        o = bank[:, q, (z % 4) * P:(z % 4 + 1) * P]
                        if z % 4 == 0:
                            eng.wait_ge(out, 2 * n + q + 1)
                        nc.tensor.matmul(o, z_h[:, z, :], z_a[:, z, :], start=True, stop=False)
                        last = nc.tensor.matmul(o, z_l[:, z, :], z_a[:, z, :], start=False, stop=True)
                    last.then_inc(used, 1)

        @block.scalar
        def _(eng):
            eng.sem_inc(out, 2)
            for u in range(2):
                eng.sem_inc(stored[u], 16)
            with eng.Fori(0, TT // 2) as i:
                for u in range(2):
                    eng.wait_ge(stored[u], 16 * i + 16)
                    with eng.Fori(0, TURNS) as m:
                        for q in range(2):
                            eng.wait_ge(used, ((2 * i + u) * TURNS + m) * 2 + q + 3)
                            nc.scalar.activation(stage[u][:, :, ds(8 * m + 4 * q, 4)],
                                                 bank[:, q, :].rearrange("p (t a) -> p a t", t=4),
                                                 ACT.Copy).then_inc(out, 1)


def experts(nc, sp, ident, xh, xl, half, x1, gd, u_w, v_w, g_final, out):
    acc = sp.at("acc", 64, [P, 4, D])
    ur = [sp.at("u_raw", 96 + 4 * e, [P, D]) for e in range(2)]
    uh = [sp.at("uT_hi", 104 + 4 * e, [P, KT, P], F32R) for e in range(2)]
    ul = [sp.at("uT_lo", 112 + 4 * e, [P, KT, P], F32R) for e in range(2)]
    vr = [sp.at("v_raw", 120 + 4 * e, [P, D]) for e in range(2)]
    vh = [sp.at("v_hi", 128 + 4 * b, [P, D], F32R) for b in range(4)]
    vl = [sp.at("v_lo", 144 + 4 * b, [P, D], F32R) for b in range(4)]
    ah = [sp.at("a_hi", 160 + 2 * b, [P, HALF], F32R) for b in range(4)]
    al = [sp.at("a_lo", 168 + 2 * b, [P, HALF], F32R) for b in range(4)]
    gt = [sp.at("g_tile", 176 + 2 * e, [P, HALF]) for e in range(2)]
    hg = [sp.at("gelu", 180 + 2 * e, [P, HALF]) for e in range(2)]
    gb = sp.at("final_gain", 184, [P, D])
    junk = sp.at("final_squares", 104, [P, 4, D])
    small = sp.at("final_small", 206, [P, 16])
    bank = sp.banks
    t_ps = bank[:, 0:2, :].rearrange("p b (k e) -> p (b k) e", e=P)
    o_ps = [bank[:, 4 + 2 * z:6 + 2 * z, :].rearrange("p b c -> p (b c)") for z in range(2)]
    S = sp.sem
    u_in, v_in, g_in = ([S(f"{n}{e}") for e in range(2)] for n in ("u_in", "v_in", "g_in"))
    acc_in, turned, uhi, ulo, hidden, gelued, weighed, ahi, alo, vhi, vlo, summed, flushed = (
        S(n) for n in ("acc_in", "turned", "u_hi", "u_lo", "hidden", "gelued", "weighed", "a_hi", "a_lo",
                       "v_hi", "v_lo", "summed", "flushed"))
    STEPS, TURN = E_TILES, 4
    TURNS = STEPS // TURN
    xt = x1.rearrange("(h t p) d -> h p t d", t=4, p=P)[half]
    ot = out.rearrange("(h t p) d -> h p t d", t=4, p=P)[half]

    def turns(eng, body):
        body(0, True, False)
        with eng.Fori(1, TURNS - 1) as i:
            body(i, False, False)
        body(TURNS - 1, False, True)

    with nc.Block() as block:
        @block.sync
        def _(eng):
            eng.dma_start(acc[:, :, :], xt).then_inc(acc_in, 16)

            def body(i, first, last):
                steps = [4 * i + s if isinstance(i, int) else eng.snap(4 * i + s) for s in range(TURN)]
                for s, n in enumerate(steps):
                    e = s % 2
                    if not (first and s < 2):
                        eng.wait_ge(turned, n - 1)
                    eng.dma_start(ur[e][:, :], u_w[ds(n * P, P), :]).then_inc(u_in[e], 16)
                    if not (first and s < 2):
                        eng.wait_ge(vlo, n - 1)
                    eng.dma_start(vr[e][:, :], v_w[ds(n * P, P), :]).then_inc(v_in[e], 16)
                    if not (first and s < 2):
                        eng.wait_ge(weighed, n - 1)
                    eng.dma_start(gt[e][:, :], gd[ds(n, 1), :, half * HALF:(half + 1) * HALF]
                                  .rearrange("o b t -> b (o t)")).then_inc(g_in[e], 16)
            turns(eng, body)

        @block.tensor
        def _(eng):
            def turn(n, e, value, wait_bank=True):
                eng.wait_ge(u_in[e], value)
                if wait_bank:
                    eng.wait_ge(ulo, n)
                for k in range(KT):
                    last = nc.tensor.transpose(t_ps[:, k, :], ur[e][:, k * P:(k + 1) * P], ident)
                last.then_inc(turned, 1)

            def hide(n, e, free):
                eng.wait_ge(ulo, n + 1)
                if free:
                    eng.wait_ge(gelued, n - 1)
                for k in range(KT):
                    last = three_pass(nc, bank[:, 2 + e, :], uh[e][:, k, :], ul[e][:, k, :],
                                      xh[:, k, :], xl[:, k, :], k == 0, k == KT - 1)
                last.then_inc(hidden, 1)

            def sum_up(m, b, part, free):
                if part == 0:
                    eng.wait_ge(alo, m)
                    eng.wait_ge(vlo, m)
                for z in range(2):
                    if free:
                        eng.wait_ge(flushed, 2 * (m - 3) + z + 1)
                    t = slice((2 * part + z) * P, (2 * part + z + 1) * P)
                    for c in range(2):
                        o, cols = bank[:, 4 + 2 * z + c, :], slice(c * 512, (c + 1) * 512)
                        for x in range(2):
                            y = 2 * b + x
                            last = three_pass(nc, o, ah[y][:, t], al[y][:, t], vh[y][:, cols], vl[y][:, cols],
                                              x == 0, x == 1)
                    last.then_inc(summed, 1)

            turn(0, 0, 16, False)

            def body(i, first, last):
                for s in range(TURN):
                    n, e = 4 * i + s, s % 2
                    if not (last and s == TURN - 1):
                        turn(n + 1, 1 - e, 16 * (2 * i + (s + 1) // 2) + 16)
                    hide(n, e, not (first and s < 2))
                    if not (first and s < 2):
                        sum_up(n, (s // 2 + 1) % 2, e, not (first and s == 2))
            turns(eng, body)
            for part in range(2):
                sum_up(STEPS + part, 1, part, True)

        @block.scalar
        def _(eng):
            def u_hi(n, e, free):
                eng.wait_ge(turned, n + 1)
                if free:
                    eng.wait_ge(hidden, n - 1)
                nc.scalar.activation(uh[e][:, :, :], t_ps, ACT.Copy).then_inc(uhi, 1)

            u_hi(0, 0, False)

            def body(i, first, last):
                for s in range(TURN):
                    n, e = 4 * i + s, s % 2
                    if not (last and s == TURN - 1):
                        u_hi(n + 1, 1 - e, not (first and s < 1))
                    eng.wait_ge(v_in[e], 16 * (2 * i + s // 2) + 16)
                    if not first:
                        eng.wait_ge(summed, 2 * (n - e) - 4)
                    nc.scalar.activation(vh[s][:, :], vr[e][:, :], ACT.Copy).then_inc(vhi, 1)
                    eng.wait_ge(hidden, n + 1)
                    if not (first and s < 2):
                        eng.wait_ge(alo, n - 1)
                    nc.scalar.activation(hg[e][:, :], bank[:, 2 + e, :], ACT.Gelu).then_inc(gelued, 1)
                    eng.wait_ge(weighed, n + 1)
                    nc.scalar.activation(ah[s][:, :], hg[e][:, :], ACT.Copy).then_inc(ahi, 1)
            turns(eng, body)

        @block.gpsimd
        def _(eng):
            def body(i, first, last):
                for s in range(TURN):
                    n, e = 4 * i + s, s % 2
                    eng.wait_ge(vhi, n + 1)
                    nc.gpsimd.tensor_tensor(vl[s][:, :], vr[e][:, :], f32(vh[s][:, :]), ALU.subtract).then_inc(vlo, 1)
            turns(eng, body)

        @block.vector
        def _(eng):
            eng.wait_ge(acc_in, 16)

            def u_lo(n, e):
                eng.wait_ge(uhi, n + 1)
                nc.vector.tensor_tensor(ul[e][:, :, :], t_ps, f32(uh[e][:, :, :]), ALU.subtract).then_inc(ulo, 1)

            def flush(m, part):
                for z in range(2):
                    eng.wait_ge(summed, 2 * (m - 2) + z + 1)
                    t = 2 * part + z
                    nc.vector.tensor_tensor(acc[:, t, :], acc[:, t, :], o_ps[z], ALU.add).then_inc(flushed, 1)

            u_lo(0, 0)

            def body(i, first, last):
                for s in range(TURN):
                    n, e = 4 * i + s, s % 2
                    if not (last and s == TURN - 1):
                        u_lo(n + 1, 1 - e)
                    eng.wait_ge(gelued, n + 1)
                    eng.wait_ge(g_in[e], 16 * (2 * i + s // 2) + 16)
                    nc.vector.tensor_tensor(hg[e][:, :], hg[e][:, :], gt[e][:, :], ALU.mult).then_inc(weighed, 1)
                    eng.wait_ge(ahi, n + 1)
                    nc.vector.tensor_tensor(al[s][:, :], hg[e][:, :], f32(ah[s][:, :]), ALU.subtract).then_inc(alo, 1)
                    if not (first and s < 2):
                        flush(n, e)
            turns(eng, body)
            for part in range(2):
                flush(STEPS + part, part)

    gain_in, eps_set, sumsq, std, rstd, done, stored = (
        S(n) for n in ("gain_in", "eps_set", "sumsq", "std", "rstd", "normed", "stored"))
    ss, sd, rs, eps = small[:, 0:4], small[:, 4:8], small[:, 8:12], small[:, 12:13]
    with nc.Block() as block:
        @block.sync
        def _(eng):
            eng.dma_start(gb[:, :], g_final.partition_broadcast(P)).then_inc(gain_in, 16)
            for t in range(4):
                eng.wait_ge(done, t + 1)
                eng.dma_start(ot[:, t, :], acc[:, t, :]).then_inc(stored, 16)
            eng.wait_ge(stored, 64)

        @block.scalar
        def _(eng):
            for t in range(4):
                last = nc.scalar.activation(junk[:, t, :], acc[:, t, :], ACT.Square, accum_out=ss[:, t:t + 1])
            last.then_inc(sumsq, 1)
            eng.wait_ge(sumsq, 1)
            eng.wait_ge(eps_set, 1)
            nc.scalar.activation(sd, ss, ACT.Sqrt, bias=eps, scale=1.0 / D).then_inc(std, 1)

        @block.vector
        def _(eng):
            nc.vector.memset(eps, EPS).then_inc(eps_set, 1)
            eng.wait_ge(gain_in, 16)
            eng.wait_ge(std, 1)
            nc.vector.reciprocal(rs, sd).then_inc(rstd, 1)
            eng.wait_ge(rstd, 1)
            for t in range(4):
                nc.vector.scalar_tensor_tensor(out=acc[:, t, :], in0=acc[:, t, :], scalar=rs[:, t:t + 1],
                                               in1=gb[:, :], op0=ALU.mult, op1=ALU.mult).then_inc(done, 1)


def park_tokens(nc, sp, xh, xl, park):
    stored = sp.sem("parked")
    with nc.Block() as block:
        @block.sync
        def _(eng):
            for half in range(2):
                for m, x in enumerate((xh, xl)):
                    eng.dma_start(park[half, m], f32(x[:, :, half * HALF:(half + 1) * HALF])).then_inc(stored, 16)
            eng.wait_ge(stored, 64)


def fetch_tokens(nc, sp, xh, xl, parked):
    loaded = sp.sem("fetched")
    with nc.Block() as block:
        @block.sync
        def _(eng):
            for m, x in enumerate((xh, xl)):
                eng.dma_start(f32(x[:, :, :]), parked[m]).then_inc(loaded, 16)
            eng.wait_ge(loaded, 32)


def block_kernel(nc, table, x, norm_mix_g, w_in, gate_bias, sinks, diff_lambda, diff_subln_g, w_up_a, w_up_b,
                 w_out, norm_ffn_g, peer_wq, peer_subkeys, peer_u, peer_v, norm_final_g, out):
    sp = Space(nc)
    x1 = nc.dram_tensor("x_after_mixing", [T, D], F32, kind="Internal").ap()
    gd = nc.dram_tensor("expert_weights", [NK, NK, T], F32, kind="Internal").ap()
    park = nc.dram_tensor("parked_tokens", [2, 2, P, KT, HALF], F32, kind="Internal").ap()
    x2, out2 = x[0], out[0]
    ident_t = sp.at("ident", 207, [P, P])
    ident = ident_t[:, :]
    id_in = sp.sem("ident_in")
    with nc.Block() as block:
        @block.sync
        def _(eng):
            eng.dma_start(ident, table[:, C_ID:C_ID + P]).then_inc(id_in, 16)
            eng.wait_ge(id_in, 16)

    xh = sp.at("xnT_hi", 0, [P, KT, T], F32R)
    xl = sp.at("xnT_lo", 32, [P, KT, T], F32R)
    norm_transpose(nc, sp, ident, x2, norm_mix_g, xh, xl, 136)

    qkT = sp.at("qkT", 64, [P, 13, T])
    va = sp.at("v_window", 116, [P, TT, P])
    vb = sp.at("v_diff", 120, [P, TT, 4 * P])
    wi = w_in[0].rearrange("(k p) c -> p k c", p=P)

    def tile_half(base, c, j):
        at = ds(base + 2 * c + j // 2, 1)
        return qkT[:, at, (j % 2) * HALF:(j % 2 + 1) * HALF].rearrange("p o t -> p (o t)")

    rest = []
    for q in range(2):
        sources = [(jj * P + a * HD, wi[:, :, QA + a * 256 + (2 * q + jj) * HD:QA + a * 256 + (2 * q + jj + 1) * HD])
                   for jj in range(2) for a in range(2)]
        rest.append(("T", sources, lambda j, q=q: qkT[:, T_QA + 2 * q + j // 2, (j % 2) * HALF:(j % 2 + 1) * HALF]))
    rest.append(("KV", [(0, wi[:, :, KA:KA + WC])],
                 lambda j: qkT[:, T_KA, j * HALF:(j + 1) * HALF] if j < 2 else va[:, 4 * (j - 2):4 * (j - 2) + 4, :]))
    for c in range(2):
        rest.append(("V", [(0, wi[:, :, VB + c * WC:VB + (c + 1) * WC])],
                     lambda j, c=c: vb[:, 2 * j:2 * j + 2, c * WC:(c + 1) * WC]))
    project(nc, sp, xh, xl, 136, 2, lambda c: wi[:, :, ds(QB + c * WC, WC)],
            lambda c, j: tile_half(T_QB, c, j), rest)

    attention(nc, sp, ident, table, qkT, va, vb, sinks, diff_lambda)
    oh = sp.at("o_hi", 96, [P, 8, T], F32R)
    ol = sp.at("o_lo", 128, [P, 8, T], F32R)
    finish_heads(nc, sp, qkT, oh, ol, diff_subln_g)
    mT = sp.at("mergedT", 64, [P, KT, T])
    gate_and_up(nc, sp, xh, xl, oh, ol, mT, w_in[0], gate_bias, w_up_a[0], w_up_b[0])
    mix_out(nc, sp, mT, x2, w_out[0], x1)
    sp.recycle()

    xh = sp.at("xn2T_hi", 0, [P, KT, T], F32R)
    xl = sp.at("xn2T_lo", 32, [P, KT, T], F32R)
    norm_transpose(nc, sp, ident, x1, norm_ffn_g, xh, xl, 136)
    qT = sp.at("peer_qT", 64, [P, HP, T])
    wq = peer_wq[0].rearrange("(k p) c -> p k c", p=P)

    def q_half(c, j):
        at = ds(2 * c + j // 2, 1)
        return qT[:, at, (j % 2) * HALF:(j % 2 + 1) * HALF].rearrange("p o t -> p (o t)")
    project(nc, sp, xh, xl, 128, HP * P // WC // 2, lambda c: wq[:, :, ds(c * WC, WC)], q_half, [])
    park_tokens(nc, sp, xh, xl, park)

    skT = sp.at("subkeysT", 136, [P, HP, P])
    turn_subkeys(nc, sp, ident, peer_subkeys[0], skT)
    picks = sp.at("picks", 0, [P, 3, T])
    select_experts(nc, sp, ident, qT, skT, picks, table, 144)
    expert_weights(nc, sp, picks, table, gd, 12)
    sp.recycle()

    xh = sp.at("half_hi", 0, [P, KT, HALF], F32R)
    xl = sp.at("half_lo", 16, [P, KT, HALF], F32R)
    for half in range(2):
        fetch_tokens(nc, sp, xh, xl, park[half])
        experts(nc, sp, ident, xh, xl, half, x1, gd, peer_u[0], peer_v[0], norm_final_g, out2)
        sp.recycle()


_INPUTS = ["x", "norm_mix_g", "w_in", "gate_bias", "sinks", "diff_lambda", "diff_subln_g", "w_up_a", "w_up_b",
           "w_out", "norm_ffn_g", "peer_wq", "peer_subkeys", "peer_u", "peer_v", "norm_final_g"]


def kernel(**inputs):
    import concourse.bacc as bacc
    from concourse.bass_utils import run_bass_kernel_spmd

    nc = bacc.Bacc("TRN2", target_bir_lowering=False, num_devices=1)
    arrays = {"table_dram": constant_table()}
    arrays.update((f"{n}_dram", np.ascontiguousarray(inputs[n])) for n in _INPUTS)
    aps = [nc.dram_tensor(n, a.shape, F32, kind="ExternalInput").ap() for n, a in arrays.items()]
    out = nc.dram_tensor("out_dram", (1, T, D), F32, kind="ExternalOutput").ap()
    block_kernel(nc, *aps, out)
    r = run_bass_kernel_spmd(nc, [arrays], core_ids=[0])
    return r.results[0]["out_dram"]
```

```python
import numpy as np
import concourse.bass as bass
from concourse import mybir
from concourse.alu_op_type import AluOpType as ALU

F32 = mybir.dt.float32
F32R = mybir.dt.float32r
BF16 = mybir.dt.bfloat16
U32 = mybir.dt.uint32
ACT = mybir.ActivationFunctionType
AX = mybir.AxisListType
ds = bass.ds

P = 128
D = 1024
T = 1024
KT = D // P
TT = T // P
HALF = 512
EPS = 1e-6
CHUNK = 64
HD = 64
QA, KA, VA, QB, KB, VB, GL = 0, 512, 640, 768, 1280, 1792, 2304
WC = 256
SWA_HEADS, DIFF_HEADS = 8, 4
LAMBDA_INIT = 0.2
PH, NK, TOPK = 8, 128, 16
HP = 2 * PH
E_TILES = NK
LOWEST = -3.0e38

T_QA, T_QB, T_KB, T_KA = 0, 4, 8, 12

C_ID, C_IOTA, C_IOTA16, C_SWA = 0, 128, 256, 272
C_DIFF = C_SWA + SWA_HEADS * 256
C_END = C_DIFF + DIFF_HEADS * 1024


def constant_table():
    c = np.zeros((P, C_END), np.float32)
    c[:, C_ID:C_ID + P] = np.eye(P)
    c[:, C_IOTA:C_IOTA + P] = np.arange(P)
    c[:, C_IOTA16:C_IOTA16 + 16] = np.arange(16)
    q = np.arange(P)[:, None]
    k = np.arange(256)[None, :] - P
    behind = q // CHUNK - k // CHUNK
    for j in range(4):
        for a in range(2):
            slope = 2.0 ** -(4 * a + j + 1)
            at = C_SWA + (2 * j + a) * 256
            c[:, at:at + 256] = np.where((behind == 0) | (behind == 1), -8 * slope * np.abs(q - k), -8e30)
    k = np.arange(1024)[None, :] - 896
    for h in range(DIFF_HEADS):
        slope = 2.0 ** (-2 * (h + 1))
        at = C_DIFF + h * 1024
        c[:, at:at + 1024] = np.where(k // CHUNK <= q // CHUNK, -8 * slope * np.abs(q - k), -8e30)
    return c


class Space:

    def __init__(self, nc):
        self.nc, self.n, self.sems = nc, 0, []
        self.base = 16512
        self.banks = nc.alloc_psum_tensor("banks", [P, 8, 512], F32)

    def at(self, name, kb, shape, dtype=F32):
        self.n += 1
        return self.nc.alloc_sbuf_tensor_at(f"{name}_{self.n}", shape, dtype, offset=self.base + int(kb * 1024))

    def sem(self, name):
        self.n += 1
        self.sems.append(self.nc.alloc_semaphore(f"{name}_{self.n}"))
        return self.sems[-1]

    def recycle(self):
        self.nc.clear_and_free_semaphores(self.sems)
        self.nc.all_engine_barrier()
        self.sems = []


def f32(ap):
    return ap.bitcast(F32)


def rep(ap, axis, n):
    ap = ap.unsqueeze(axis)
    return ap.broadcast_to([n if a == axis else c for a, c in enumerate(ap.shape)])


def norm_transpose(nc, sp, ident, src, gain, hi, lo, kb):
    xr = sp.at("norm_x", kb, [P, 2, D])
    xs = sp.at("norm_scaled", kb + 8, [P, 2, D])
    gb = sp.at("norm_gain", kb + 16, [P, D])
    junk = sp.at("norm_squares", kb + 20, [P, D])
    small = sp.at("norm_small", 206, [P, 8])
    bank = sp.banks
    x_in = [sp.sem("x_in0"), sp.sem("x_in1")]
    gain_in, eps_set, sumsq, std, rstd = (sp.sem(s) for s in ("gain_in", "eps_set", "sumsq", "std", "rstd"))
    scaled, turned, hi_done, lo_done = (
        sp.sem(s) for s in ("scaled", "turned", "hi_done", "lo_done"))
    rows = src.rearrange("(t p) d -> t p d", p=P)
    ss, sd, rs, eps = small[:, 0:2], small[:, 2:4], small[:, 4:6], small[:, 6:7]

    with nc.Block() as block:
        @block.sync
        def _(eng):
            eng.dma_start(gb[:, :], gain[0].partition_broadcast(P)).then_inc(gain_in, 16)
            with eng.Fori(0, TT // 2) as i:
                for u in range(2):
                    eng.wait_ge(scaled, 2 * i + u + 1)
                    eng.dma_start(xr[:, u, :], rows[2 * i + u, :, :]).then_inc(x_in[u], 16)

        @block.scalar
        def _(eng):
            eng.wait_ge(eps_set, 1)

            def stats(i, u):
                eng.wait_ge(x_in[u], 16 * i + 16)
                nc.scalar.activation(junk[:, :], xr[:, u, :], ACT.Square,
                                     accum_out=ss[:, u:u + 1]).then_inc(sumsq, 1)
                eng.wait_ge(sumsq, 2 * i + u + 1)
                nc.scalar.activation(sd[:, u:u + 1], ss[:, u:u + 1], ACT.Sqrt,
                                     bias=eps, scale=1.0 / D).then_inc(std, 1)

            def take_hi(i, u):
                for b in range(2):
                    eng.wait_ge(turned, 4 * i + 2 * u + b + 1)
                    nc.scalar.activation(hi[:, 4 * b:4 * b + 4, ds((2 * i + u) * P, P)],
                                         bank[:, 2 * u + b, :].rearrange("p (k t) -> p k t", k=4),
                                         ACT.Copy).then_inc(hi_done, 1)

            stats(0, 0)
            with eng.Fori(0, TT // 2 - 1) as i:
                for u in range(2):
                    stats(i + u, 1 - u)
                    take_hi(i, u)
            stats(TT // 2 - 1, 1)
            take_hi(TT // 2 - 1, 0)
            take_hi(TT // 2 - 1, 1)

        @block.vector
        def _(eng):
            nc.vector.memset(eps, EPS).then_inc(eps_set, 1)
            eng.sem_inc(scaled, 2)
            eng.sem_inc(lo_done, 4)
            eng.wait_ge(gain_in, 16)

            def scale(i, u):
                eng.wait_ge(std, 2 * i + u + 1)
                nc.vector.reciprocal(rs[:, u:u + 1], sd[:, u:u + 1]).then_inc(rstd, 1)
                eng.wait_ge(rstd, 2 * i + u + 1)
                nc.vector.scalar_tensor_tensor(
                    out=xs[:, u, :], in0=xr[:, u, :], scalar=rs[:, u:u + 1], in1=gb[:, :],
                    op0=ALU.mult, op1=ALU.mult).then_inc(scaled, 1)

            def take_lo(i, u):
                for b in range(2):
                    eng.wait_ge(hi_done, 4 * i + 2 * u + b + 1)
                    at = (slice(None), slice(4 * b, 4 * b + 4), ds((2 * i + u) * P, P))
                    nc.vector.tensor_tensor(lo[at], bank[:, 2 * u + b, :].rearrange("p (k t) -> p k t", k=4),
                                            f32(hi[at]), ALU.subtract).then_inc(lo_done, 1)

            scale(0, 0)
            with eng.Fori(0, TT // 2 - 1) as i:
                for u in range(2):
                    scale(i + u, 1 - u)
                    take_lo(i, u)
            scale(TT // 2 - 1, 1)
            take_lo(TT // 2 - 1, 0)
            take_lo(TT // 2 - 1, 1)

        @block.tensor
        def _(eng):
            with eng.Fori(0, TT // 2) as i:
                for u in range(2):
                    eng.wait_ge(scaled, 2 * i + u + 3)
                    for b in range(2):
                        eng.wait_ge(lo_done, 4 * i + 2 * u + b + 1)
                        for k in range(4):
                            last = nc.tensor.transpose(bank[:, 2 * u + b, k * P:(k + 1) * P],
                                                       xs[:, u, (4 * b + k) * P:(4 * b + k + 1) * P], ident)
                        last.then_inc(turned, 1)


def three_pass(nc, out, ah, al, bh, bl, first, last):
    nc.tensor.matmul(out, ah, bh, start=first, stop=False)
    nc.tensor.matmul(out, ah, bl, start=False, stop=False)
    return nc.tensor.matmul(out, al, bh, start=False, stop=last)


def project(nc, sp, xh, xl, kb, loop_pairs, loop_cols, loop_dst, rest):
    raw = [sp.at("w_raw", kb + 8 * u, [P, KT, WC]) for u in range(2)]
    wh = [sp.at("w_hi", kb + 16 + 8 * u, [P, KT, WC], F32R) for u in range(2)]
    wl = [sp.at("w_lo", kb + 32 + 8 * u, [P, KT, WC], F32R) for u in range(2)]
    bank = sp.banks
    w_in = [sp.sem("w_in0"), sp.sem("w_in1")]
    hi_done, split, job, free_act, free_dve = (
        sp.sem(s) for s in ("w_hi_done", "w_split", "job", "bank_free_act", "bank_free_dve"))
    n_loop = 2 * loop_pairs
    arrived, count = {}, [16 * loop_pairs] * 2
    for r, (_, sources, _) in enumerate(rest):
        c = n_loop + r
        count[c % 2] += 16 * len(sources)
        arrived[c] = count[c % 2]

    def pieces(kind, j):
        if kind == "T" or (kind == "KV" and j < 2):
            return [(0, 512, j // 2, j % 2)]
        if kind == "V":
            return [(256 * z, 256, 2 * j + z, None) for z in range(2)]
        return [(128 * z, 128, 4 * (j - 2) + z, None) for z in range(4)]

    with nc.Block() as block:
        @block.sync
        def _(eng):
            with eng.Fori(0, loop_pairs) as i:
                for u in range(2):
                    eng.wait_ge(split, 2 * i + u + 1)
                    eng.dma_start(raw[u][:, :, :], loop_cols(2 * i + u)).then_inc(w_in[u], 16)
            for r, (_, sources, _) in enumerate(rest):
                c = n_loop + r
                eng.wait_ge(split, c + 1)
                for at, src in sources:
                    eng.dma_start(raw[c % 2][:, :, at:at + src.shape[2]], src).then_inc(w_in[c % 2], 16)

        def evacuate(eng, c, u, j, dst, copy, free):
            eng.wait_ge(job, 4 * c + j + 9)
            src = bank[:, 4 * u + j, :]
            if len(dst.shape) == 3:
                src = src.rearrange("p (a b) -> p a b", a=dst.shape[1])
            copy(dst, src).then_inc(free, 1)

        @block.scalar
        def _(eng):
            eng.sem_inc(free_act, 4)

            def hi(c, u, there):
                eng.wait_ge(w_in[u], there)
                eng.wait_ge(job, 4 * c + 4)
                nc.scalar.activation(wh[u][:, :, :], raw[u][:, :, :], ACT.Copy).then_inc(hi_done, 1)

            def out(c, u, dst):
                for j in range(2):
                    evacuate(eng, c, u, j, dst(j), lambda o, s: nc.scalar.activation(o, s, ACT.Copy), free_act)

            hi(0, 0, 16)
            with eng.Fori(0, loop_pairs - 1) as i:
                hi(2 * i + 1, 1, 16 * i + 16)
                out(2 * i, 0, lambda j: loop_dst(2 * i, j))
                hi(2 * i + 2, 0, 16 * i + 32)
                out(2 * i + 1, 1, lambda j: loop_dst(2 * i + 1, j))
            c = n_loop - 1
            hi(c, 1, 16 * loop_pairs)
            out(c - 1, 0, lambda j: loop_dst(c - 1, j))
            for r, (_, _, dst) in enumerate(rest):
                hi(n_loop + r, (n_loop + r) % 2, arrived[n_loop + r])
                before = (lambda j: loop_dst(c, j)) if r == 0 else rest[r - 1][2]
                out(n_loop + r - 1, (n_loop + r - 1) % 2, before)
            out(n_loop + len(rest) - 1, (n_loop + len(rest) - 1) % 2,
                rest[-1][2] if rest else lambda j: loop_dst(c, j))

        @block.vector
        def _(eng):
            eng.sem_inc(free_dve, 4)
            eng.sem_inc(split, 2)

            def lo(c, u):
                eng.wait_ge(hi_done, c + 1)
                nc.vector.tensor_tensor(wl[u][:, :, :], raw[u][:, :, :], f32(wh[u][:, :, :]),
                                        ALU.subtract).then_inc(split, 1)

            def out(c, u, dst):
                for j in range(2, 4):
                    evacuate(eng, c, u, j, dst(j), nc.vector.tensor_copy, free_dve)

            lo(0, 0)
            with eng.Fori(0, loop_pairs - 1) as i:
                lo(2 * i + 1, 1)
                out(2 * i, 0, lambda j: loop_dst(2 * i, j))
                lo(2 * i + 2, 0)
                out(2 * i + 1, 1, lambda j: loop_dst(2 * i + 1, j))
            c = n_loop - 1
            lo(c, 1)
            out(c - 1, 0, lambda j: loop_dst(c - 1, j))
            for r in range(len(rest)):
                lo(n_loop + r, (n_loop + r) % 2)
                before = (lambda j: loop_dst(c, j)) if r == 0 else rest[r - 1][2]
                out(n_loop + r - 1, (n_loop + r - 1) % 2, before)
            out(n_loop + len(rest) - 1, (n_loop + len(rest) - 1) % 2,
                rest[-1][2] if rest else lambda j: loop_dst(c, j))

        @block.tensor
        def _(eng):
            eng.sem_inc(job, 8)

            def chunk(c, u, kind):
                eng.wait_ge(split, c + 3)
                for j in range(4):
                    eng.wait_ge(free_act if j < 2 else free_dve, 2 * c + j % 2 + 1)
                    for at, n, tile, half in pieces(kind, j):
                        for k in range(KT):
                            o = bank[:, 4 * u + j, at:at + n]
                            if half is None:
                                t = slice(tile * P, (tile + 1) * P)
                                cols = slice(0, WC) if kind == "V" else slice(P, WC)
                                last = three_pass(nc, o, xh[:, k, t], xl[:, k, t], wh[u][:, k, cols],
                                                  wl[u][:, k, cols], k == 0, k == KT - 1)
                            else:
                                w = slice(tile * P, (tile + 1) * P)
                                t = slice(half * HALF, (half + 1) * HALF)
                                last = three_pass(nc, o, wh[u][:, k, w], wl[u][:, k, w], xh[:, k, t],
                                                  xl[:, k, t], k == 0, k == KT - 1)
                    last.then_inc(job, 1)

            with eng.Fori(0, loop_pairs) as i:
                for u in range(2):
                    chunk(2 * i + u, u, "T")
            for r, (kind, _, _) in enumerate(rest):
                chunk(n_loop + r, (n_loop + r) % 2, kind)


def attention(nc, sp, ident, table, qkT, va, vb, sinks, diff_lambda):
    tab = sp.at("tables", 136, [P, C_END - C_SWA])
    s = [sp.at("scores", 160 + 8 * u, [P, 2, 1024]) for u in range(2)]
    wt = [sp.at("weights", 176 + 4 * u, [P, 1024]) for u in range(2)]
    wT = [sp.at("weightsT", 184 + 4 * u, [P, 1024]) for u in range(2)]
    sink = sp.at("sink", 192, [P, SWA_HEADS])
    lp = sp.at("lambda_parts", 192.25, [P, 4, HD])
    lprod = sp.at("lambda_products", 193.25, [P, 2, HD])
    lam = sp.at("lambda_small", 193.75, [P, 8])
    mx, ng, sm, rc = (sp.at(n, 194 + 0.25 * m, [P, 2, 2]) for m, n in enumerate(("max", "negmax", "sum", "recip")))
    es = sp.at("sink_term", 195, [P, 2, 2])
    rl = sp.at("lambda_recip", 195.25, [P, 2])
    bank = sp.banks
    s_ps = bank[:, 0:4, :].rearrange("p (m b) c -> p m (b c)", m=2)
    t_ps = bank[:, 4:6, :].rearrange("p b c -> p (b c)")
    o_ps = [bank[:, 6, 0:P], bank[:, 7, 0:P]]

    items = []
    for i in range(TT):
        for j in range(4):
            k0 = max(0, i - 1)
            items.append(("swa", i, j, list(range(k0, i + 1))))
        for h in range(DIFF_HEADS):
            items.append(("diff", i, h, list(range(i + 1))))
    N = len(items)
    tables_in, small_in, lam_sum, lam_exp, lam_ready = (
        sp.sem(n) for n in ("tables_in", "small_in", "lam_sum", "lam_exp", "lam_ready"))
    scored, masked, exped, weighed, turned, out_t, valued, out_o, dve = (
        sp.sem(n) for n in ("scored", "masked", "exped", "weighed", "turned", "wT_ready", "valued", "o_out", "dve"))

    def q_tile(kind, h):
        return (T_QA if kind == "swa" else T_QB) + h

    with nc.Block() as block:
        @block.sync
        def _(eng):
            eng.dma_start(tab[:, :], table[:, C_SWA:C_END]).then_inc(tables_in, 16)
            eng.dma_start(sink[:, :], sinks[0].partition_broadcast(P)).then_inc(small_in, 16)
            eng.dma_start(lp[:, :, :], diff_lambda[0].partition_broadcast(P)).then_inc(small_in, 16)

        @block.tensor
        def _(eng):
            def scores(n):
                kind, i, h, kts = items[n]
                if n >= 1:
                    eng.wait_ge(masked, n)
                k_tile = T_KA if kind == "swa" else T_KB + h
                for m in range(2):
                    r = slice(m * HD, (m + 1) * HD)
                    k0, k1 = kts[0] * P, (kts[-1] + 1) * P
                    for a in range(k0, k1, 512):
                        b = min(k1, a + 512)
                        last = nc.tensor.matmul(s_ps[:, m, a - k0:b - k0], qkT[r, q_tile(kind, h), i * P:(i + 1) * P],
                                                qkT[r, k_tile, a:b], start=True, stop=True)
                last.then_inc(scored, 1)

            def turn(n):
                kind, i, h, kts = items[n]
                eng.wait_ge(weighed, n + 1)
                if n >= 1:
                    eng.wait_ge(out_t, n)
                blocks = len(kts) * (2 if kind == "swa" else 1)
                for b in range(blocks):
                    last = nc.tensor.transpose(t_ps[:, b * P:(b + 1) * P], wt[n % 2][:, b * P:(b + 1) * P], ident)
                last.then_inc(turned, 1)

            def values(n):
                kind, i, h, kts = items[n]
                eng.wait_ge(out_t, n + 1)
                if n >= 2:
                    eng.wait_ge(out_o, n - 1)
                if kind == "swa":
                    for a in range(2):
                        r = slice(a * HD, (a + 1) * HD)
                        for b, kt in enumerate(kts):
                            at = (a * len(kts) + b) * P
                            last = nc.tensor.matmul(o_ps[n % 2][r, :], va[:, kt, r], wT[n % 2][:, at:at + P],
                                                    start=b == 0, stop=b == len(kts) - 1)
                else:
                    for b, kt in enumerate(kts):
                        last = nc.tensor.matmul(o_ps[n % 2], vb[:, kt, h * P:(h + 1) * P],
                                                wT[n % 2][:, b * P:(b + 1) * P], start=b == 0, stop=b == len(kts) - 1)
                last.then_inc(valued, 1)

            scores(0)
            scores(1)
            for n in range(N):
                if n + 2 < N:
                    scores(n + 2)
                if n >= 1:
                    values(n - 1)
                turn(n)
            values(N - 1)

        @block.vector
        def _(eng):
            count = [0]

            def link(ins):
                count[0] += 1
                ins.then_inc(dve, 1)
                eng.wait_ge(dve, count[0])

            eng.wait_ge(small_in, 32)
            for m in range(2):
                nc.vector.tensor_tensor_reduce(out=lprod[:, m, :], in0=lp[:, 2 * m, :], in1=lp[:, 2 * m + 1, :],
                                               scale=1.0, scalar=0.0, op0=ALU.mult, op1=ALU.add,
                                               accum_out=lam[:, m:m + 1]).then_inc(lam_sum, 1)
            eng.wait_ge(lam_exp, 1)
            link(nc.vector.tensor_tensor(lam[:, 4:5], lam[:, 3:4], lam[:, 2:3], ALU.subtract))
            link(nc.vector.tensor_scalar(lam[:, 5:6], lam[:, 4:5], LAMBDA_INIT, None, ALU.subtract))
            eng.wait_ge(tables_in, 16)

            def mask(n):
                kind, i, h, kts = items[n]
                u, k = n % 2, len(kts) * P
                eng.wait_ge(scored, n + 1)
                if n >= 2:
                    eng.wait_ge(weighed, n - 1)
                for m in range(2):
                    if kind == "swa":
                        at = (2 * h + m) * 256 + 256 - k
                    else:
                        at = C_DIFF - C_SWA + h * 1024 + 1024 - k
                    last = nc.vector.tensor_tensor_reduce(
                        out=s[u][:, m, 0:k], in0=s_ps[:, m, 0:k], in1=tab[:, at:at + k], scale=0.125,
                        scalar=LOWEST, op0=ALU.add, op1=ALU.max, accum_out=mx[:, u, m:m + 1])
                link(last)
                if kind == "swa":
                    link(nc.vector.tensor_tensor(mx[:, u, :], mx[:, u, :], sink[:, h:h + 5:4], ALU.max))
                    nc.vector.tensor_tensor(es[:, u, :], sink[:, h:h + 5:4], mx[:, u, :], ALU.subtract)
                nc.vector.tensor_scalar(ng[:, u, :], mx[:, u, :], -1.0, None, ALU.mult).then_inc(masked, 1)

            def weigh(n):
                kind, i, h, kts = items[n]
                u, k = n % 2, len(kts) * P
                eng.wait_ge(exped, n + 1)
                if kind == "swa":
                    link(nc.vector.tensor_tensor(sm[:, u, :], sm[:, u, :], es[:, u, :], ALU.add))
                link(nc.vector.reciprocal(rc[:, u, :], sm[:, u, :]))
                if n >= 2:
                    eng.wait_ge(turned, n - 1)
                if kind == "swa":
                    nc.vector.tensor_scalar(wt[u][:, 0:k], s[u][:, 0, 0:k], rc[:, u, 0:1], None, ALU.mult)
                    nc.vector.tensor_scalar(wt[u][:, k:2 * k], s[u][:, 1, 0:k], rc[:, u, 1:2], None,
                                            ALU.mult).then_inc(weighed, 1)
                else:
                    nc.vector.tensor_tensor(rl[:, u:u + 1], rc[:, u, 1:2], lam[:, 5:6], ALU.mult)
                    link(nc.vector.tensor_scalar(wt[u][:, 0:k], s[u][:, 0, 0:k], rc[:, u, 0:1], None, ALU.mult))
                    nc.vector.scalar_tensor_tensor(
                        out=wt[u][:, 0:k], in0=s[u][:, 1, 0:k], scalar=rl[:, u:u + 1], in1=wt[u][:, 0:k],
                        op0=ALU.mult, op1=ALU.add).then_inc(weighed, 1)

            def output(n):
                kind, i, h, _ = items[n]
                eng.wait_ge(valued, n + 1)
                nc.vector.tensor_copy(qkT[:, q_tile(kind, h), i * P:(i + 1) * P], o_ps[n % 2]).then_inc(out_o, 1)

            mask(0)
            for n in range(N):
                if n + 1 < N:
                    mask(n + 1)
                weigh(n)
                if n >= 2:
                    output(n - 2)
            output(N - 2)
            output(N - 1)

        @block.scalar
        def _(eng):
            eng.wait_ge(lam_sum, 2)
            nc.scalar.activation(lam[:, 2:4], lam[:, 0:2], ACT.Exp).then_inc(lam_exp, 1)

            def exps(n):
                kind, i, h, kts = items[n]
                u, k = n % 2, len(kts) * P
                eng.wait_ge(masked, n + 1)
                for m in range(2):
                    last = nc.scalar.activation(s[u][:, m, 0:k], s[u][:, m, 0:k], ACT.Exp, bias=ng[:, u, m:m + 1],
                                                accum_out=sm[:, u, m:m + 1])
                if kind == "swa":
                    last = nc.scalar.activation(es[:, u, :], es[:, u, :], ACT.Exp)
                last.then_inc(exped, 1)

            def out_turned(n):
                kind, i, h, kts = items[n]
                c = len(kts) * P * (2 if kind == "swa" else 1)
                eng.wait_ge(turned, n + 1)
                if n >= 2:
                    eng.wait_ge(valued, n - 1)
                nc.scalar.activation(wT[n % 2][:, 0:c], t_ps[:, 0:c], ACT.Copy).then_inc(out_t, 1)

            exps(0)
            for n in range(N):
                if n + 1 < N:
                    exps(n + 1)
                out_turned(n)


def finish_heads(nc, sp, oT, oh, ol, subln_g):
    sq = sp.at("head_squares", 160, [P, 4, T])
    sd = sp.at("head_std", 176, [P, 2, T])
    ones = sp.at("mean_matrix", 184, [P, P])
    g = sp.at("subln_gain", 184.5, [P, 2])
    eps = sp.at("head_eps", 184.75, [P, 1])
    bank = sp.banks
    g_in, made, squared, meaned, std, dve, hi_swa, hi_diff = (
        sp.sem(n) for n in ("g_in", "const_set", "squared", "meaned", "std", "dve", "hi_swa", "hi_diff"))
    pair = [bank[:, 2 * h:2 * h + 2, :].rearrange("p b c -> p (b c)") for h in range(4)]

    with nc.Block() as block:
        @block.sync
        def _(eng):
            with nc.allow_non_contiguous_dma(reason="128 gains, one to a partition"):
                eng.dma_start(g[:, 0:1], subln_g.rearrange("o d -> d o")).then_inc(g_in, 16)

        @block.scalar
        def _(eng):
            for h in range(4):
                nc.scalar.activation(sq[:, h, :], oT[:, T_QB + h, :], ACT.Square).then_inc(squared, 1)
            eng.wait_ge(made, 2)
            for h in range(4):
                eng.wait_ge(meaned, h + 1)
                if h >= 2:
                    eng.wait_ge(dve, 4 * (h - 1) + 1)
                nc.scalar.activation(sd[:, h % 2, :], pair[h], ACT.Sqrt, bias=eps[:, 0:1]).then_inc(std, 1)
            for h in range(4):
                nc.scalar.activation(oh[:, h, :], oT[:, T_QA + h, :], ACT.Copy).then_inc(hi_swa, 1)

        @block.vector
        def _(eng):
            nc.vector.memset(ones[:, :], 1.0 / P).then_inc(made, 1)
            nc.vector.memset(eps[:, :], EPS).then_inc(made, 1)
            count = [0]

            def link(ins):
                count[0] += 1
                ins.then_inc(dve, 1)
                eng.wait_ge(dve, count[0])

            eng.wait_ge(g_in, 16)
            link(nc.vector.tensor_scalar(g[:, 1:2], g[:, 0:1], 1.0 - LAMBDA_INIT, None, ALU.mult))
            for h in range(4):
                eng.wait_ge(std, h + 1)
                r, o = sd[:, h % 2, :], oT[:, T_QB + h, :]
                link(nc.vector.reciprocal(r, r))
                link(nc.vector.tensor_tensor(r, o, r, ALU.mult))
                link(nc.vector.tensor_scalar(oh[:, 4 + h, :], r, g[:, 1:2], None, ALU.mult))
                link(nc.vector.scalar_tensor_tensor(out=ol[:, 4 + h, :], in0=r, scalar=g[:, 1:2],
                                                    in1=f32(oh[:, 4 + h, :]), op0=ALU.mult, op1=ALU.subtract))
            for h in range(4):
                eng.wait_ge(hi_swa, h + 1)
                nc.vector.tensor_tensor(ol[:, h, :], oT[:, T_QA + h, :], f32(oh[:, h, :]), ALU.subtract)

        @block.tensor
        def _(eng):
            eng.wait_ge(made, 1)
            for h in range(4):
                eng.wait_ge(squared, h + 1)
                for b in range(2):
                    last = nc.tensor.matmul(bank[:, 2 * h + b, :], ones[:, :], sq[:, h, b * 512:(b + 1) * 512],
                                            start=True, stop=True)
                last.then_inc(meaned, 1)


def gate_and_up(nc, sp, xh, xl, oh, ol, mT, w_in, gate_bias, w_up_a, w_up_b):
    raw = [sp.at("gate_raw", 160 + 4 * s, [P, KT, P]) for s in range(3)]
    wh = [sp.at("gate_hi", 172 + 4 * s, [P, KT, P], F32R) for s in range(3)]
    wl = [sp.at("gate_lo", 184 + 4 * s, [P, KT, P], F32R) for s in range(3)]
    sg = [sp.at("sigmoid", 196 + 4 * s, [P, T]) for s in range(2)]
    bias = sp.at("gate_bias", 204, [P, 16])
    bank = sp.banks
    pair = [bank[:, 2 * s:2 * s + 2, :].rearrange("p b c -> p (b c)") for s in range(4)]
    w_in3 = w_in.rearrange("(k p) c -> p k c", p=P)
    ua = w_up_a.rearrange("(a j c) n -> a c j n", a=2, c=HD)
    ub = w_up_b.rearrange("(k p) n -> p k n", p=P)
    loaded = [sp.sem(f"loaded{s}") for s in range(3)]
    hi_done = [sp.sem(f"hi_done{s}") for s in range(3)]
    split = [sp.sem(f"split{s}") for s in range(3)]
    multiplied = [sp.sem(f"multiplied{s}") for s in range(3)]
    squashed = [sp.sem(f"squashed{s}") for s in range(2)]
    sig_free, bias_in, mixed = sp.sem("sig_free"), sp.sem("bias_in"), sp.sem("mixed")

    with nc.Block() as block:
        @block.sync
        def _(eng):
            with nc.allow_non_contiguous_dma(reason="2048 biases, one to a partition"):
                eng.dma_start(bias[:, :], gate_bias.rearrange("o (t p) -> p (o t)", p=P)).then_inc(bias_in, 16)
            with eng.Fori(0, KT) as j:
                for s in range(2):
                    eng.wait_ge(split[s], j + 1)
                    eng.dma_start(raw[s][:, :, :], w_in3[:, :, ds(GL + s * D + j * P, P)]).then_inc(loaded[s], 16)
                eng.wait_ge(split[2], j + 1)
                for a in (1, 0):
                    eng.dma_start(raw[2][a * HD:(a + 1) * HD, 0:4, :], ua[a, :, :, ds(j * P, P)]).then_inc(loaded[2], 16)
                eng.dma_start(raw[2][:, 4:8, :], ub[:, :, ds(j * P, P)]).then_inc(loaded[2], 16)

        @block.scalar
        def _(eng):
            eng.wait_ge(bias_in, 16)
            with eng.Fori(0, KT) as j:
                for s in range(3):
                    eng.wait_ge(loaded[s], (16 if s < 2 else 48) * (j + 1))
                    eng.wait_ge(multiplied[s], j + 1)
                    nc.scalar.activation(wh[s][:, :, :], raw[s][:, :, :], ACT.Copy).then_inc(hi_done[s], 1)
                eng.wait_ge(sig_free, j + 1)
                for s in range(2):
                    eng.wait_ge(multiplied[s], j + 2)
                    nc.scalar.activation(sg[s][:, :], pair[s], ACT.Sigmoid,
                                         bias=bias[:, ds(8 * s + j, 1)]).then_inc(squashed[s], 1)

        @block.vector
        def _(eng):
            for s in range(3):
                eng.sem_inc(split[s], 1)
            eng.sem_inc(sig_free, 1)
            with eng.Fori(0, KT) as j:
                for s in range(3):
                    eng.wait_ge(hi_done[s], j + 1)
                    nc.vector.tensor_tensor(wl[s][:, :, :], raw[s][:, :, :], f32(wh[s][:, :, :]),
                                            ALU.subtract).then_inc(split[s], 1)
                eng.wait_ge(multiplied[2], j + 2)
                for s in range(2):
                    eng.wait_ge(squashed[s], j + 1)
                    nc.vector.tensor_tensor(sg[s][:, :], sg[s][:, :], pair[2 + s], ALU.mult).then_inc(mixed, 1)
                eng.wait_ge(mixed, 2 * j + 2)
                nc.vector.tensor_tensor(mT[:, ds(j, 1), :].rearrange("p o t -> p (o t)"), sg[0][:, :], sg[1][:, :],
                                        ALU.add).then_inc(sig_free, 1)

        @block.tensor
        def _(eng):
            for s in range(3):
                eng.sem_inc(multiplied[s], 1)
            with eng.Fori(0, KT) as j:
                for s in range(2):
                    eng.wait_ge(split[s], j + 2)
                    if s == 0:
                        eng.wait_ge(sig_free, j + 1)
                    for half in range(2):
                        t = slice(half * HALF, (half + 1) * HALF)
                        for k in range(KT):
                            last = three_pass(nc, bank[:, 2 * s + half, :], wh[s][:, k, :], wl[s][:, k, :],
                                              xh[:, k, t], xl[:, k, t], k == 0, k == KT - 1)
                    last.then_inc(multiplied[s], 1)
                eng.wait_ge(split[2], j + 2)
                for s in range(2):
                    for half in range(2):
                        t = slice(half * HALF, (half + 1) * HALF)
                        for k in range(4 * s, 4 * s + 4):
                            last = three_pass(nc, bank[:, 4 + 2 * s + half, :], wh[2][:, k, :], wl[2][:, k, :],
                                              oh[:, k, t], ol[:, k, t], k == 4 * s, k == 4 * s + 3)
                last.then_inc(multiplied[2], 1)


def mix_out(nc, sp, mT, x, w_out, x1):
    mh = [sp.at("merged_hi", 4 * u, [P, KT, P], F32R) for u in range(2)]
    ml = [sp.at("merged_lo", 8 + 4 * u, [P, KT, P], F32R) for u in range(2)]
    raw = [sp.at("wo_raw", 16 + 8 * u, [P, KT, WC]) for u in range(2)]
    wh = sp.at("wo_hi", 96, [P, KT, D], F32R)
    wl = sp.at("wo_lo", 128, [P, KT, D], F32R)
    xr = [sp.at("residual", 160 + 4 * u, [P, D]) for u in range(2)]
    y = [sp.at("x1_tile", 168 + 4 * u, [P, D]) for u in range(2)]
    bank = sp.banks
    pair = [bank[:, 2 * u:2 * u + 2, :].rearrange("p b c -> p (b c)") for u in range(2)]
    wo = w_out.rearrange("(k p) c -> p k c", p=P)
    xt = x.rearrange("(t p) d -> t p d", p=P)
    x1t = x1.rearrange("(t p) d -> t p d", p=P)
    w_in = [sp.sem("wo_in0"), sp.sem("wo_in1")]
    x_in = [sp.sem("x_in0"), sp.sem("x_in1")]
    stored = [sp.sem("stored0"), sp.sem("stored1")]
    w_hi, w_lo, m_hi, m_lo, multiplied, added, y_free = (
        sp.sem(n) for n in ("w_hi", "w_lo", "m_hi", "m_lo", "multiplied", "added", "y_free"))
    NC = D // WC

    with nc.Block() as block:
        @block.sync
        def _(eng):
            for c in range(NC):
                if c >= 2:
                    eng.wait_ge(w_lo, c - 1)
                eng.dma_start(raw[c % 2][:, :, :], wo[:, :, c * WC:(c + 1) * WC]).then_inc(w_in[c % 2], 16)
            with eng.Fori(0, TT // 2) as i:
                for u in range(2):
                    eng.wait_ge(added, 2 * i + u + 1)
                    eng.dma_start(xr[u][:, :], xt[2 * i + u, :, :]).then_inc(x_in[u], 16)

        @block.gpsimd
        def _(eng):
            eng.sem_inc(y_free, 2)
            with eng.Fori(0, TT // 2) as i:
                for u in range(2):
                    eng.wait_ge(added, 2 * i + u + 3)
                    eng.dma_start(x1t[2 * i + u, :, :], y[u][:, :]).then_inc(stored[u], 16)
                    eng.wait_ge(stored[u], 16 * i + 16)
                    eng.sem_inc(y_free, 1)

        @block.scalar
        def _(eng):
            for c in range(NC):
                eng.wait_ge(w_in[c % 2], 16 * (c // 2) + 16)
                nc.scalar.activation(wh[:, :, c * WC:(c + 1) * WC], raw[c % 2][:, :, :], ACT.Copy).then_inc(w_hi, 1)
            with eng.Fori(0, TT // 2) as i:
                for u in range(2):
                    eng.wait_ge(multiplied, 2 * i + u + 1)
                    nc.scalar.activation(mh[u][:, :, :], mT[:, :, ds((2 * i + u) * P, P)], ACT.Copy).then_inc(m_hi, 1)

        @block.vector
        def _(eng):
            eng.sem_inc(added, 2)
            for c in range(NC):
                eng.wait_ge(w_hi, c + 1)
                at = (slice(None), slice(None), slice(c * WC, (c + 1) * WC))
                nc.vector.tensor_tensor(wl[at], raw[c % 2][:, :, :], f32(wh[at]), ALU.subtract).then_inc(w_lo, 1)

            def split(t, u):
                eng.wait_ge(m_hi, t + 1)
                nc.vector.tensor_tensor(ml[u][:, :, :], mT[:, :, ds(t * P, P)], f32(mh[u][:, :, :]),
                                        ALU.subtract).then_inc(m_lo, 1)

            def add(t, i, u):
                eng.wait_ge(multiplied, t + 3)
                eng.wait_ge(x_in[u], 16 * i + 16)
                eng.wait_ge(y_free, t + 1)
                nc.vector.tensor_tensor(y[u][:, :], pair[u], xr[u][:, :],
                                        ALU.add).then_inc(added, 1)

            split(0, 0)
            with eng.Fori(0, TT // 2 - 1) as i:
                split(2 * i + 1, 1)
                add(2 * i, i, 0)
                split(2 * i + 2, 0)
                add(2 * i + 1, i, 1)
            split(TT - 1, 1)
            add(TT - 2, TT // 2 - 1, 0)
            add(TT - 1, TT // 2 - 1, 1)

        @block.tensor
        def _(eng):
            eng.sem_inc(multiplied, 2)
            eng.wait_ge(w_lo, NC)

            def tile(t, u):
                eng.wait_ge(m_lo, t + 1)
                eng.wait_ge(added, t + 1)
                for b in range(2):
                    c = slice(b * 512, (b + 1) * 512)
                    for k in range(KT):
                        last = three_pass(nc, bank[:, 2 * u + b, :], mh[u][:, k, :], ml[u][:, k, :],
                                          wh[:, k, c], wl[:, k, c], k == 0, k == KT - 1)
                last.then_inc(multiplied, 1)

            with eng.Fori(0, TT // 2) as i:
                for u in range(2):
                    tile(2 * i + u, u)


def turn_subkeys(nc, sp, ident, subkeys, skT):
    raw = sp.at("subkeys", 128, [P, HP, P])
    bank = sp.banks
    key_in, turned = sp.sem("key_in"), sp.sem("turned")
    with nc.Block() as block:
        @block.sync
        def _(eng):
            eng.dma_start(raw[:, :, :], subkeys.rearrange("h q n d -> n (h q) d")).then_inc(key_in, 16)

        @block.tensor
        def _(eng):
            eng.wait_ge(key_in, 16)
            for hp in range(HP):
                last = nc.tensor.transpose(bank[:, hp // 4, (hp % 4) * P:(hp % 4 + 1) * P], raw[:, hp, :], ident)
            last.then_inc(turned, 1)

        @block.scalar
        def _(eng):
            eng.wait_ge(turned, 1)
            nc.scalar.activation(skT[:, :, :], bank[:, 0:4, :].rearrange("p b (q n) -> p (b q) n", n=P), ACT.Copy)


def select_experts(nc, sp, ident, qT, skT, picks, table, kb):
    qs = sp.at("q_tile", kb, [P, HP, P])
    s = sp.at("key_scores", kb + 8, [P, HP, NK])
    s2 = sp.at("key_scores_left", kb + 16, [P, HP, NK])
    cand = sp.at("candidates", kb + 24, [P, PH, TOPK, TOPK])
    cand2 = sp.at("candidates_left", kb + 32, [P, PH, TOPK, TOPK])
    hot = sp.at("rank_match", kb + 40, [P, PH, TOPK, TOPK])
    top = sp.at("top", kb + 48, [P, HP, TOPK])
    top_i = sp.at("top_index", kb + 49, [P, HP, TOPK], U32)
    top_f = sp.at("top_index_f", kb + 50, [P, HP, TOPK])
    best = sp.at("best", kb + 51, [P, PH, TOPK])
    best_i = sp.at("best_index", kb + 51.5, [P, PH, TOPK], U32)
    rank_i = sp.at("rank", kb + 52, [P, 2, PH, TOPK], U32)
    rank_f = sp.at("rank_f", kb + 53, [P, 2, PH, TOPK])
    e = sp.at("best_exp", kb + 54, [P, PH, TOPK])
    found = sp.at("found", kb + 54.5, [P, 3, PH * TOPK])
    norm = sp.at("best_norm", kb + 56, [P, 2, PH])
    iota16 = sp.at("iota16", kb + 56.25, [P, TOPK])
    bank = sp.banks
    iota_in, q_here, scored, s_here, exp_in, exped, found_all, turned, picked, dve = (
        sp.sem(n) for n in ("iota_in", "q_here", "scored", "s_here", "exp_in", "exped", "found_all", "turned",
                            "picked", "dve"))
    s_free, steady = sp.sem("s_free"), sp.sem("steady")
    LINKS = 24

    with nc.Block() as block:
        @block.sync
        def _(eng):
            eng.dma_start(iota16[:, :], table[:, C_IOTA16:C_IOTA16 + TOPK]).then_inc(iota_in, 16)

        @block.gpsimd
        def _(eng):
            with eng.Fori(0, TT) as t:
                eng.wait_ge(scored, t + 1)
                nc.gpsimd.tensor_copy(qs[:, :, :], qT[:, :, ds(t * P, P)]).then_inc(q_here, 1)

        @block.tensor
        def _(eng):
            eng.sem_inc(scored, 1)
            with eng.Fori(0, TT) as t:
                eng.wait_ge(q_here, t + 1)
                eng.wait_ge(s_here, t + 1)
                for hp in range(HP):
                    last = nc.tensor.matmul(bank[:, hp // 4, (hp % 4) * P:(hp % 4 + 1) * P], qs[:, hp, :],
                                            skT[:, hp, :], start=True, stop=True)
                last.then_inc(scored, 1)
                eng.wait_ge(found_all, t + 1)
                eng.wait_ge(picked, t + 1)
                for m in range(3):
                    last = nc.tensor.transpose(bank[:, 4, m * P:(m + 1) * P], found[:, m, :], ident)
                last.then_inc(turned, 1)

        @block.scalar
        def _(eng):
            eng.sem_inc(s_here, 1)
            eng.sem_inc(picked, 1)
            with eng.Fori(0, TT) as t:
                eng.wait_ge(scored, t + 2)
                eng.wait_ge(s_free, t + 1)
                nc.scalar.activation(s[:, :, :], bank[:, 0:4, :].rearrange("p b (q n) -> p (b q) n", n=NK),
                                     ACT.Copy).then_inc(s_here, 1)
                eng.wait_ge(exp_in, t + 1)
                nc.scalar.activation(e[:, :, :], e[:, :, :], ACT.Exp).then_inc(exped, 1)
                eng.wait_ge(turned, t + 1)
                nc.scalar.activation(picks[:, :, ds(t * P, P)],
                                     bank[:, 4, 0:3 * P].rearrange("p (m t) -> p m t", m=3),
                                     ACT.Copy).then_inc(picked, 1)

        @block.vector
        def _(eng):
            eng.sem_inc(s_free, 1)
            eng.wait_ge(iota_in, 16)
            with eng.Fori(0, TT) as t:
                n = [0]

                def link(ins):
                    n[0] += 1
                    ins.then_inc(dve, 1)
                    eng.wait_ge(dve, LINKS * t + n[0])
                    eng.sem_inc(steady, 1)

                def top16(rows, values, left, out, out_i, after=None):
                    for r in range(rows):
                        last = nc.vector.max(out[:, r, 0:8], values(r))
                    link(last)
                    for r in range(rows):
                        nc.vector.max_index(out_i[:, r, 0:8], out[:, r, 0:8], values(r))
                    for r in range(rows):
                        last = nc.vector.match_replace(left(r), out[:, r, 0:8], values(r), LOWEST)
                    link(last)
                    if after is not None:
                        after()
                    for r in range(rows):
                        last = nc.vector.max(out[:, r, 8:16], left(r))
                    link(last)
                    for r in range(rows):
                        last = nc.vector.max_index(out_i[:, r, 8:16], out[:, r, 8:16], left(r))
                    link(last)

                eng.wait_ge(s_here, t + 2)
                eng.sem_inc(steady, 1)
                top16(HP, lambda r: s[:, r, :], lambda r: s2[:, r, :], top, top_i,
                      lambda: eng.sem_inc(s_free, 1))
                nc.vector.tensor_copy(top_f[:, :, :], top_i[:, :, :])
                a = top[:, :, :].rearrange("p (h q) k -> p h q k", q=2)
                link(nc.vector.tensor_tensor(
                    cand[:, :, :, :],
                    rep(a[:, :, 0, :], 3, TOPK), rep(a[:, :, 1, :], 2, TOPK),
                    ALU.add))
                top16(PH, lambda r: cand[:, r, :, :].rearrange("p a b -> p (a b)"),
                      lambda r: cand2[:, r, :, :].rearrange("p a b -> p (a b)"), best, best_i)
                nc.vector.tensor_tensor(e[:, :, :], best[:, :, :], rep(best[:, :, 0], 2, TOPK),
                                        ALU.subtract).then_inc(exp_in, 1)
                nc.vector.tensor_single_scalar(rank_i[:, 0, :, :], best_i[:, :, :], 4, ALU.logical_shift_right)
                link(nc.vector.tensor_single_scalar(rank_i[:, 1, :, :], best_i[:, :, :], 15, ALU.bitwise_and))
                link(nc.vector.tensor_copy(rank_f[:, :, :, :].rearrange("p q h k -> p (q h k)"),
                                           rank_i[:, :, :, :].rearrange("p q h k -> p (q h k)")))
                f = top_f[:, :, :].rearrange("p (h q) k -> p h q k", q=2)
                for q in range(2):
                    link(nc.vector.tensor_tensor(
                        hot[:, :, :, :].rearrange("p h k r -> p (h k) r"),
                        rep(rank_f[:, q, :, :].rearrange("p h k -> p (h k)"), 2, TOPK),
                        rep(iota16[:, :], 1, PH * TOPK), ALU.is_equal))
                    link(nc.vector.tensor_tensor(hot[:, :, :, :], hot[:, :, :, :],
                                                 rep(f[:, :, q, :], 2, TOPK), ALU.mult))
                    link(nc.vector.tensor_reduce(found[:, q, :], hot[:, :, :, :].rearrange("p h k r -> p (h k) r"),
                                                 axis=AX.X, op=ALU.add))
                eng.wait_ge(exped, t + 1)
                link(nc.vector.tensor_reduce(norm[:, 0, :], e[:, :, :], axis=AX.X, op=ALU.add))
                link(nc.vector.reciprocal(norm[:, 1, :], norm[:, 0, :]))
                nc.vector.tensor_tensor(found[:, 2, :].rearrange("p (h k) -> p h k", h=PH), e[:, :, :],
                                        rep(norm[:, 1, :], 2, TOPK), ALU.mult).then_inc(found_all, 1)
                eng.wait_ge(turned, t + 1)
                assert n[0] <= LINKS, n[0]
                if n[0] < LINKS:
                    eng.sem_inc(dve, LINKS - n[0])


def expert_weights(nc, sp, picks, table, gd, kb, kb_stage, xl, parked, late):
    B = 8
    keys = sp.at("pick_keys", kb, [P, 2, T], BF16)
    part = sp.at("weight_parts", kb + 4, [P, 3, T], BF16)
    iota = sp.at("iota_each", kb + 10, [P, NK, B], BF16)
    iota_f = sp.at("iota", kb + 12, [P, NK])
    rest = sp.at("weight_rest", kb + 12.5, [P, T])
    first = [sp.at("first_hot", kb + 12.5 + 2 * z, [P, NK, B], BF16) for z in range(2)]
    second = [sp.at("second_hot", kb + 16.5 + 2 * z, [P, NK, B], BF16) for z in range(2)]
    scaled = [[sp.at("second_scaled", kb + 20.5 + 6 * z + 2 * m, [P, NK, B], BF16) for m in range(3)]
              for z in range(2)]
    stage = [sp.at("weights_stage", kb_stage + 64 * u, [P, NK, P]) for u in range(2)]
    bank = sp.banks
    iota_in, fetched, split, hot, matched, weighed, used, out = (
        sp.sem(n) for n in ("iota_in", "fetched", "split", "hot", "second_matched", "weighed", "hot_used", "g_out"))
    stored = [sp.sem("stored0"), sp.sem("stored1")]
    TURNS = P // B

    with nc.Block() as block:
        @block.sync
        def _(eng):
            eng.dma_start(iota_f[:, :], table[:, C_IOTA:C_IOTA + NK]).then_inc(iota_in, 16)

            def store(t, u, a0=0, a1=NK):
                return eng.dma_start(gd[a0:a1, :, ds(t * P, P)].rearrange("a b t -> b a t"), stage[u][:, a0:a1, :])

            with eng.Fori(0, TT // 2 - 1) as i:
                for u in range(2):
                    eng.wait_ge(out, (2 * i + u + 1) * TURNS + 2)
                    store(2 * i + u, u).then_inc(stored[u], 16)
            eng.wait_ge(out, (TT - 1) * TURNS + 2)
            store(TT - 2, 0).then_inc(stored[0], 16)
            eng.wait_ge(stored[0], 16 * (TT // 2) + 16)
            eng.dma_start(f32(xl[:, :, :]), parked).then_inc(fetched, 16)
            eng.wait_ge(out, TT * TURNS + 2)
            store(TT - 1, 1, 0, 4).then_inc(late[0], 16)
            store(TT - 1, 1, 4, NK).then_inc(late[1], 16)
            eng.wait_ge(stored[1], 16 * (TT // 2))
            eng.wait_ge(fetched, 16)

        @block.vector
        def _(eng):
            n = [0]

            def link(ins):
                n[0] += 1
                ins.then_inc(split, 1)
                eng.wait_ge(split, n[0])

            nc.vector.tensor_copy(keys[:, :, :], picks[:, 0:2, :])
            link(nc.vector.tensor_copy(part[:, 0, :], picks[:, 2, :]))
            link(nc.vector.tensor_tensor(rest[:, :], picks[:, 2, :], part[:, 0, :], ALU.subtract))
            link(nc.vector.tensor_copy(part[:, 1, :], rest[:, :]))
            link(nc.vector.tensor_tensor(rest[:, :], rest[:, :], part[:, 1, :], ALU.subtract))
            link(nc.vector.tensor_copy(part[:, 2, :], rest[:, :]))
            eng.wait_ge(iota_in, 16)
            link(nc.vector.tensor_copy(iota[:, :, :], rep(iota_f[:, :], 2, B)))
            def match(m, z):
                nc.vector.tensor_tensor(second[z][:, :, :], iota[:, :, :], rep(keys[:, 1, ds(m * B, B)], 1, NK),
                                        ALU.is_equal).then_inc(matched, 1)

            def body(i, last):
                for z in range(2):
                    m = 2 * i + z
                    eng.wait_ge(used, m + 1)
                    nc.vector.tensor_tensor(first[z][:, :, :], iota[:, :, :], rep(keys[:, 0, ds(m * B, B)], 1, NK),
                                            ALU.is_equal).then_inc(hot, 1)
                    if not (last and z == 1):
                        eng.wait_ge(weighed, 3 * m + 3)
                        match(m + 1, 1 - z)
                    eng.wait_ge(matched, m + 1)
                    for w in range(3):
                        nc.vector.tensor_tensor(scaled[z][w][:, :, :], second[z][:, :, :],
                                                rep(part[:, w, ds(m * B, B)], 1, NK), ALU.mult).then_inc(weighed, 1)

            eng.sem_inc(weighed, 3)
            match(0, 0)
            with eng.Fori(0, T // (2 * B) - 1) as i:
                body(i, False)
            body(T // (2 * B) - 1, True)

        @block.tensor
        def _(eng):
            eng.sem_inc(used, 2)
            with eng.Fori(0, T // (2 * B)) as i:
                for z in range(2):
                    m = 2 * i + z
                    eng.wait_ge(hot, m + 1)
                    eng.wait_ge(weighed, 3 * m + 6)
                    eng.wait_ge(out, m + 1)
                    for t in range(B):
                        o = bank[:, 2 * z + t // 4, (t % 4) * P:(t % 4 + 1) * P]
                        for w in range(3):
                            last = nc.tensor.matmul(o, scaled[z][w][:, :, t], first[z][:, :, t],
                                                    start=w == 0, stop=w == 2)
                    last.then_inc(used, 1)

        @block.scalar
        def _(eng):
            eng.sem_inc(out, 2)
            for u in range(2):
                eng.sem_inc(stored[u], 16)
            with eng.Fori(0, TT // 2) as i:
                for u in range(2):
                    eng.wait_ge(stored[u], 16 * i + 16)
                    with eng.Fori(0, TURNS // 2) as h:
                        for z in range(2):
                            eng.wait_ge(used, (2 * i + u) * TURNS + 2 * h + z + 3)
                            nc.scalar.activation(stage[u][:, :, ds((2 * h + z) * B, B)],
                                                 bank[:, 2 * z:2 * z + 2, :].rearrange("p q (t a) -> p a (q t)", t=4),
                                                 ACT.Copy).then_inc(out, 1)


def experts(nc, sp, ident, xh, xl, late, x1, gd, u_w, v_w, g_final, out):
    ur = [sp.at("u_raw", 32 + 4 * e, [P, D]) for e in range(2)]
    uh = [sp.at("uT_hi", 40 + 4 * e, [P, KT, P], F32R) for e in range(2)]
    ul = [sp.at("uT_lo", 48 + 4 * e, [P, KT, P], F32R) for e in range(2)]
    gt = [sp.at("g_tile", 56 + 4 * e, [P, T]) for e in range(2)]
    gb = sp.at("final_gain", 64, [P, D])
    ah = [sp.at("a_hi", 109 + 4 * b, [P, T], F32R) for b in range(4)]
    al = [sp.at("a_lo", 125 + 4 * b, [P, T], F32R) for b in range(4)]
    a_raw = [sp.at("a_raw", 125 + 4 * b, [P, T]) for b in range(4)]
    acc = sp.at("acc", 141, [P, TT, D])
    vh = [sp.at("v_hi", 173 + 4 * b, [P, D], F32R) for b in range(4)]
    vl = [sp.at("v_lo", 189 + 4 * b, [P, D], F32R) for b in range(4)]
    vr = [sp.at("v_raw", 189 + 4 * b, [P, D]) for b in range(4)]
    junk = sp.at("final_squares", 0, [P, TT, D])
    small = sp.at("final_small", 206, [P, 32])
    bank = sp.banks
    t_ps = bank[:, 0:2, :].rearrange("p b (k e) -> p (b k) e", e=P)
    o_ps = [bank[:, 4 + 2 * z:6 + 2 * z, :].rearrange("p b c -> p (b c)") for z in range(2)]
    S = sp.sem
    u_in, g_in = ([S(f"{n}{e}") for e in range(2)] for n in ("u_in", "g_in"))
    v_in = [S(f"v_in{s}") for s in range(4)]
    acc_in, gain_in, turned, uhi, ulo, hidden, gelued, weighed, ahi, alo, vhi, vlo, summed, flushed = (
        S(n) for n in ("acc_in", "gain_in", "turned", "u_hi", "u_lo", "hidden", "gelued", "weighed", "a_hi", "a_lo",
                       "v_hi", "v_lo", "summed", "flushed"))
    STEPS, TURN = E_TILES, 4
    TURNS = STEPS // TURN
    xt = x1.rearrange("(t p) d -> p t d", p=P)
    ot = out.rearrange("(t p) d -> p t d", p=P)

    def turns(eng, body):
        body(0, True, False)
        with eng.Fori(1, TURNS - 1) as i:
            body(i, False, False)
        body(TURNS - 1, False, True)

    with nc.Block() as block:
        @block.sync
        def _(eng):
            def load_u(n, e):
                eng.dma_start(ur[e][:, :], u_w[ds(n * P, P), :]).then_inc(u_in[e], 16)

            def load_g(n, e):
                eng.dma_start(gt[e][:, :], gd[ds(n, 1), :, :].rearrange("o b t -> b (o t)")).then_inc(g_in[e], 16)

            def load_v(n, s):
                eng.dma_start(vr[s][:, :], v_w[ds(n * P, P), :]).then_inc(v_in[s], 16)

            load_u(0, 0)
            load_u(1, 1)
            eng.wait_ge(late[0], 16)
            load_g(0, 0)
            load_g(1, 1)
            eng.wait_ge(turned, 1)
            load_u(2, 0)
            eng.wait_ge(late[1], 16)
            for n in range(2):
                load_v(n, n)
            eng.dma_start(acc[:, :, :], xt).then_inc(acc_in, 16)
            eng.dma_start(gb[:, :], g_final.partition_broadcast(P)).then_inc(gain_in, 16)

            def body(i, first, last):
                steps = [4 * i + s if isinstance(i, int) else eng.snap(4 * i + s) for s in range(TURN + 2)]
                for s in range(TURN):
                    n, e = steps[s], s % 2
                    if not (last and s >= 2) and not (first and s == 0):
                        eng.wait_ge(turned, n + 1)
                        load_u(steps[s + 2], e)
                    if first and s < 2:
                        continue
                    eng.wait_ge(weighed, 2 * n - 2)
                    load_g(n, e)
                    if not first:
                        eng.wait_ge(summed, 4 * (n - e) - 8)
                    load_v(n, s)
            turns(eng, body)

        @block.tensor
        def _(eng):
            def turn(n, e, value, wait_bank=True):
                eng.wait_ge(u_in[e], value)
                if wait_bank:
                    eng.wait_ge(ulo, n)
                for k in range(KT):
                    last = nc.tensor.transpose(t_ps[:, k, :], ur[e][:, k * P:(k + 1) * P], ident)
                last.then_inc(turned, 1)

            def hide(n, e, h, free):
                if h == 0:
                    eng.wait_ge(ulo, n + 1)
                if free:
                    eng.wait_ge(gelued, 2 * n + h - 1)
                for k in range(KT):
                    last = three_pass(nc, bank[:, 2 + h, :], uh[e][:, k, :], ul[e][:, k, :],
                                      xh[:, k, h * HALF:(h + 1) * HALF], xl[:, k, h * HALF:(h + 1) * HALF],
                                      k == 0, k == KT - 1)
                last.then_inc(hidden, 1)

            def sum_up(m, n, b, part, free):
                if part == 0:
                    eng.wait_ge(alo, 2 * n)
                    eng.wait_ge(vlo, n)
                for z in range(2):
                    if free:
                        eng.wait_ge(flushed, 2 * (m - 5) + z + 1)
                    t = slice((2 * part + z) * P, (2 * part + z + 1) * P)
                    for c in range(2):
                        o, cols = bank[:, 4 + 2 * z + c, :], slice(c * 512, (c + 1) * 512)
                        for x in range(2):
                            y = 2 * b + x
                            last = three_pass(nc, o, ah[y][:, t], al[y][:, t], vh[y][:, cols], vl[y][:, cols],
                                              x == 0, x == 1)
                    last.then_inc(summed, 1)

            turn(0, 0, 16, False)

            def body(i, first, last):
                for s in range(TURN):
                    n, e = 4 * i + s, s % 2
                    if not (last and s == TURN - 1):
                        turn(n + 1, 1 - e, 16 * (2 * i + (s + 1) // 2) + 16)
                    for h in range(2):
                        hide(n, e, h, not (first and s == 0))
                        if not (first and s < 2):
                            sum_up(2 * n + h, n, (s // 2 + 1) % 2, 2 * e + h, not (first and s == 2 and h == 0))
            turns(eng, body)
            for part in range(4):
                sum_up(2 * STEPS + part, STEPS, 1, part, True)

        @block.scalar
        def _(eng):
            def u_hi(n, e, free):
                eng.wait_ge(turned, n + 1)
                if free:
                    eng.wait_ge(hidden, 2 * n - 2)
                nc.scalar.activation(uh[e][:, :, :], t_ps, ACT.Copy).then_inc(uhi, 1)

            u_hi(0, 0, False)

            def body(i, first, last):
                for s in range(TURN):
                    n, e = 4 * i + s, s % 2
                    if not (last and s == TURN - 1):
                        u_hi(n + 1, 1 - e, not (first and s < 1))
                    if not first:
                        eng.wait_ge(summed, 4 * (n - e) - 8)
                    for h in range(2):
                        cols = slice(h * HALF, (h + 1) * HALF)
                        eng.wait_ge(hidden, 2 * n + h + 1)
                        nc.scalar.activation(a_raw[s][:, cols], bank[:, 2 + h, :], ACT.Gelu).then_inc(gelued, 1)
                        eng.wait_ge(weighed, 2 * n + h + 1)
                        nc.scalar.activation(ah[s][:, cols], a_raw[s][:, cols], ACT.Copy).then_inc(ahi, 1)
                    eng.wait_ge(v_in[s], 16 * i + 16)
                    nc.scalar.activation(vh[s][:, :], vr[s][:, :], ACT.Copy).then_inc(vhi, 1)
            turns(eng, body)

        @block.gpsimd
        def _(eng):
            def body(i, first, last):
                for s in range(TURN):
                    n, e = 4 * i + s, s % 2
                    eng.wait_ge(vhi, n + 1)
                    nc.gpsimd.tensor_tensor(vl[s][:, :], vr[s][:, :], f32(vh[s][:, :]),
                                            ALU.subtract).then_inc(vlo, 1)
            turns(eng, body)

        @block.vector
        def _(eng):
            def u_lo(n, e):
                eng.wait_ge(uhi, n + 1)
                nc.vector.tensor_tensor(ul[e][:, :, :], t_ps, f32(uh[e][:, :, :]), ALU.subtract).then_inc(ulo, 1)

            def flush(m, part):
                for z in range(2):
                    eng.wait_ge(summed, 2 * (m - 4) + z + 1)
                    t = 2 * part + z
                    nc.vector.tensor_tensor(acc[:, t, :], acc[:, t, :], o_ps[z], ALU.add).then_inc(flushed, 1)

            u_lo(0, 0)

            def body(i, first, last):
                for s in range(TURN):
                    n, e = 4 * i + s, s % 2
                    if first and s == 2:
                        eng.wait_ge(acc_in, 16)
                    if not (last and s == TURN - 1):
                        u_lo(n + 1, 1 - e)
                    for h in range(2):
                        cols = slice(h * HALF, (h + 1) * HALF)
                        eng.wait_ge(gelued, 2 * n + h + 1)
                        if h == 0:
                            eng.wait_ge(g_in[e], 16 * (2 * i + s // 2) + 16)
                        nc.vector.tensor_tensor(a_raw[s][:, cols], a_raw[s][:, cols], gt[e][:, cols],
                                                ALU.mult).then_inc(weighed, 1)
                        eng.wait_ge(ahi, 2 * n + h + 1)
                        nc.vector.tensor_tensor(al[s][:, cols], a_raw[s][:, cols], f32(ah[s][:, cols]),
                                                ALU.subtract).then_inc(alo, 1)
                        if not (first and s < 2):
                            flush(2 * n + h, 2 * e + h)
            turns(eng, body)
            for part in range(4):
                flush(2 * STEPS + part, part)

    eps_set, sumsq, std, rstd, done, stored = (
        S(n) for n in ("eps_set", "sumsq", "std", "rstd", "normed", "stored"))
    ss, sd, rs, eps = small[:, 0:TT], small[:, TT:2 * TT], small[:, 2 * TT:3 * TT], small[:, 3 * TT:3 * TT + 1]
    with nc.Block() as block:
        @block.sync
        def _(eng):
            for t in range(TT):
                eng.wait_ge(done, t + 1)
                eng.dma_start(ot[:, t, :], acc[:, t, :]).then_inc(stored, 16)
            eng.wait_ge(stored, 16 * TT)

        @block.scalar
        def _(eng):
            for t in range(TT):
                last = nc.scalar.activation(junk[:, t, :], acc[:, t, :], ACT.Square, accum_out=ss[:, t:t + 1])
            last.then_inc(sumsq, 1)
            eng.wait_ge(sumsq, 1)
            eng.wait_ge(eps_set, 1)
            nc.scalar.activation(sd, ss, ACT.Sqrt, bias=eps, scale=1.0 / D).then_inc(std, 1)

        @block.vector
        def _(eng):
            nc.vector.memset(eps, EPS).then_inc(eps_set, 1)
            eng.wait_ge(gain_in, 16)
            eng.wait_ge(std, 1)
            nc.vector.reciprocal(rs, sd).then_inc(rstd, 1)
            eng.wait_ge(rstd, 1)
            for t in range(TT):
                nc.vector.scalar_tensor_tensor(out=acc[:, t, :], in0=acc[:, t, :], scalar=rs[:, t:t + 1],
                                               in1=gb[:, :], op0=ALU.mult, op1=ALU.mult).then_inc(done, 1)


def park_tokens(nc, sp, xl, park):
    stored = sp.sem("parked")
    with nc.Block() as block:
        @block.sync
        def _(eng):
            eng.dma_start(park, f32(xl[:, :, :])).then_inc(stored, 16)
            eng.wait_ge(stored, 16)


def block_kernel(nc, table, x, norm_mix_g, w_in, gate_bias, sinks, diff_lambda, diff_subln_g, w_up_a, w_up_b,
                 w_out, norm_ffn_g, peer_wq, peer_subkeys, peer_u, peer_v, norm_final_g, out):
    sp = Space(nc)
    x1 = nc.dram_tensor("x_after_mixing", [T, D], F32, kind="Internal").ap()
    gd = nc.dram_tensor("expert_weights", [NK, NK, T], F32, kind="Internal").ap()
    park = nc.dram_tensor("parked_tokens", [P, KT, T], F32, kind="Internal").ap()
    x2, out2 = x[0], out[0]
    ident_t = sp.at("ident", 207, [P, P])
    ident = ident_t[:, :]
    id_in = sp.sem("ident_in")
    with nc.Block() as block:
        @block.sync
        def _(eng):
            eng.dma_start(ident, table[:, C_ID:C_ID + P]).then_inc(id_in, 16)
            eng.wait_ge(id_in, 16)

    xh = sp.at("xnT_hi", 0, [P, KT, T], F32R)
    xl = sp.at("xnT_lo", 32, [P, KT, T], F32R)
    norm_transpose(nc, sp, ident, x2, norm_mix_g, xh, xl, 136)

    qkT = sp.at("qkT", 64, [P, 13, T])
    va = sp.at("v_window", 116, [P, TT, P])
    vb = sp.at("v_diff", 120, [P, TT, 4 * P])
    wi = w_in[0].rearrange("(k p) c -> p k c", p=P)

    def tile_half(base, c, j):
        at = ds(base + 2 * c + j // 2, 1)
        return qkT[:, at, (j % 2) * HALF:(j % 2 + 1) * HALF].rearrange("p o t -> p (o t)")

    rest = []
    for q in range(2):
        sources = [(jj * P + a * HD, wi[:, :, QA + a * 256 + (2 * q + jj) * HD:QA + a * 256 + (2 * q + jj + 1) * HD])
                   for jj in range(2) for a in range(2)]
        rest.append(("T", sources, lambda j, q=q: qkT[:, T_QA + 2 * q + j // 2, (j % 2) * HALF:(j % 2 + 1) * HALF]))
    rest.append(("KV", [(0, wi[:, :, KA:KA + WC])],
                 lambda j: qkT[:, T_KA, j * HALF:(j + 1) * HALF] if j < 2 else va[:, 4 * (j - 2):4 * (j - 2) + 4, :]))
    for c in range(2):
        rest.append(("V", [(0, wi[:, :, VB + c * WC:VB + (c + 1) * WC])],
                     lambda j, c=c: vb[:, 2 * j:2 * j + 2, c * WC:(c + 1) * WC]))
    project(nc, sp, xh, xl, 136, 2, lambda c: wi[:, :, ds(QB + c * WC, WC)],
            lambda c, j: tile_half(T_QB, c, j), rest)

    attention(nc, sp, ident, table, qkT, va, vb, sinks, diff_lambda)
    oh = sp.at("o_hi", 96, [P, 8, T], F32R)
    ol = sp.at("o_lo", 128, [P, 8, T], F32R)
    finish_heads(nc, sp, qkT, oh, ol, diff_subln_g)
    mT = sp.at("mergedT", 64, [P, KT, T])
    gate_and_up(nc, sp, xh, xl, oh, ol, mT, w_in[0], gate_bias, w_up_a[0], w_up_b[0])
    mix_out(nc, sp, mT, x2, w_out[0], x1)
    sp.recycle()

    xh = sp.at("xn2T_hi", 0, [P, KT, T], F32R)
    xl = sp.at("xn2T_lo", 32, [P, KT, T], F32R)
    norm_transpose(nc, sp, ident, x1, norm_ffn_g, xh, xl, 136)
    qT = sp.at("peer_qT", 64, [P, HP, T])
    wq = peer_wq[0].rearrange("(k p) c -> p k c", p=P)

    def q_half(c, j):
        at = ds(2 * c + j // 2, 1)
        return qT[:, at, (j % 2) * HALF:(j % 2 + 1) * HALF].rearrange("p o t -> p (o t)")
    project(nc, sp, xh, xl, 128, HP * P // WC // 2, lambda c: wq[:, :, ds(c * WC, WC)], q_half, [])
    park_tokens(nc, sp, xl, park)

    skT = sp.at("subkeysT", 136, [P, HP, P])
    turn_subkeys(nc, sp, ident, peer_subkeys[0], skT)
    picks = sp.at("picks", 32, [P, 3, T])
    select_experts(nc, sp, ident, qT, skT, picks, table, 144)
    sp.recycle()
    xl = sp.at("xn2T_lo_again", 77, [P, KT, T], F32R)
    late = [sp.sem("g_late_first"), sp.sem("g_late_rest")]
    expert_weights(nc, sp, picks, table, gd, 44, 77, xl, park, late)
    experts(nc, sp, ident, xh, xl, late, x1, gd, peer_u[0], peer_v[0], norm_final_g, out2)
    sp.recycle()


_INPUTS = ["x", "norm_mix_g", "w_in", "gate_bias", "sinks", "diff_lambda", "diff_subln_g", "w_up_a", "w_up_b",
           "w_out", "norm_ffn_g", "peer_wq", "peer_subkeys", "peer_u", "peer_v", "norm_final_g"]


def kernel(**inputs):
    import concourse.bacc as bacc
    from concourse.bass_utils import run_bass_kernel_spmd

    nc = bacc.Bacc("TRN2", target_bir_lowering=False, num_devices=1)
    arrays = {"table_dram": constant_table()}
    arrays.update((f"{n}_dram", np.ascontiguousarray(inputs[n])) for n in _INPUTS)
    aps = [nc.dram_tensor(n, a.shape, F32, kind="ExternalInput").ap() for n, a in arrays.items()]
    out = nc.dram_tensor("out_dram", (1, T, D), F32, kind="ExternalOutput").ap()
    block_kernel(nc, *aps, out)
    r = run_bass_kernel_spmd(nc, [arrays], core_ids=[0])
    return r.results[0]["out_dram"]
```

```python
import numpy as np
import concourse.bass as bass
from concourse import mybir
from concourse.alu_op_type import AluOpType as ALU

F32 = mybir.dt.float32
F32R = mybir.dt.float32r
BF16 = mybir.dt.bfloat16
U32 = mybir.dt.uint32
ACT = mybir.ActivationFunctionType
AX = mybir.AxisListType
ds = bass.ds

P = 128
D = 1024
T = 1024
KT = D // P
TT = T // P
HALF = 512
EPS = 1e-6
CHUNK = 64
HD = 64
QA, KA, VA, QB, KB, VB, GL = 0, 512, 640, 768, 1280, 1792, 2304
WC = 256
SWA_HEADS, DIFF_HEADS = 8, 4
LAMBDA_INIT = 0.2
PH, NK, TOPK = 8, 128, 16
HP = 2 * PH
E_TILES = NK
LOWEST = -3.0e38

T_QA, T_QB, T_KB, T_KA = 0, 4, 8, 12

C_ID, C_IOTA, C_IOTA16, C_SWA = 0, 128, 256, 272
C_DIFF = C_SWA + SWA_HEADS * 256
C_END = C_DIFF + DIFF_HEADS * 1024


def constant_table():
    c = np.zeros((P, C_END), np.float32)
    c[:, C_ID:C_ID + P] = np.eye(P)
    c[:, C_IOTA:C_IOTA + P] = np.arange(P)
    c[:, C_IOTA16:C_IOTA16 + 16] = np.arange(16)
    q = np.arange(P)[:, None]
    k = np.arange(256)[None, :] - P
    behind = q // CHUNK - k // CHUNK
    for j in range(4):
        for a in range(2):
            slope = 2.0 ** -(4 * a + j + 1)
            at = C_SWA + (2 * j + a) * 256
            c[:, at:at + 256] = np.where((behind == 0) | (behind == 1), -8 * slope * np.abs(q - k), -8e30)
    k = np.arange(1024)[None, :] - 896
    for h in range(DIFF_HEADS):
        slope = 2.0 ** (-2 * (h + 1))
        at = C_DIFF + h * 1024
        c[:, at:at + 1024] = np.where(k // CHUNK <= q // CHUNK, -8 * slope * np.abs(q - k), -8e30)
    return c


class Space:

    def __init__(self, nc):
        self.nc, self.n, self.sems = nc, 0, []
        self.base = 16512
        self.banks = nc.alloc_psum_tensor("banks", [P, 8, 512], F32)

    def at(self, name, kb, shape, dtype=F32):
        self.n += 1
        return self.nc.alloc_sbuf_tensor_at(f"{name}_{self.n}", shape, dtype, offset=self.base + int(kb * 1024))

    def sem(self, name):
        self.n += 1
        self.sems.append(self.nc.alloc_semaphore(f"{name}_{self.n}"))
        return self.sems[-1]

    def recycle(self):
        self.nc.clear_and_free_semaphores(self.sems)
        self.nc.all_engine_barrier()
        self.sems = []


def f32(ap):
    return ap.bitcast(F32)


def rep(ap, axis, n):
    ap = ap.unsqueeze(axis)
    return ap.broadcast_to([n if a == axis else c for a, c in enumerate(ap.shape)])


def norm_transpose(nc, sp, ident, src, gain, hi, lo, kb):
    xr = sp.at("norm_x", kb, [P, 2, D])
    xs = sp.at("norm_scaled", kb + 8, [P, 2, D])
    gb = sp.at("norm_gain", kb + 16, [P, D])
    junk = sp.at("norm_squares", kb + 20, [P, D])
    small = sp.at("norm_small", 206, [P, 8])
    bank = sp.banks
    x_in = [sp.sem("x_in0"), sp.sem("x_in1")]
    gain_in, eps_set, sumsq, std, rstd = (sp.sem(s) for s in ("gain_in", "eps_set", "sumsq", "std", "rstd"))
    scaled, turned, hi_done, lo_done = (
        sp.sem(s) for s in ("scaled", "turned", "hi_done", "lo_done"))
    rows = src.rearrange("(t p) d -> t p d", p=P)
    ss, sd, rs, eps = small[:, 0:2], small[:, 2:4], small[:, 4:6], small[:, 6:7]

    with nc.Block() as block:
        @block.sync
        def _(eng):
            eng.dma_start(gb[:, :], gain[0].partition_broadcast(P)).then_inc(gain_in, 16)
            with eng.Fori(0, TT // 2) as i:
                for u in range(2):
                    eng.wait_ge(scaled, 2 * i + u + 1)
                    eng.dma_start(xr[:, u, :], rows[2 * i + u, :, :]).then_inc(x_in[u], 16)

        @block.scalar
        def _(eng):
            eng.wait_ge(eps_set, 1)

            def stats(i, u):
                eng.wait_ge(x_in[u], 16 * i + 16)
                nc.scalar.activation(junk[:, :], xr[:, u, :], ACT.Square,
                                     accum_out=ss[:, u:u + 1]).then_inc(sumsq, 1)
                eng.wait_ge(sumsq, 2 * i + u + 1)
                nc.scalar.activation(sd[:, u:u + 1], ss[:, u:u + 1], ACT.Sqrt,
                                     bias=eps, scale=1.0 / D).then_inc(std, 1)

            def take_hi(i, u):
                for b in range(2):
                    eng.wait_ge(turned, 4 * i + 2 * u + b + 1)
                    nc.scalar.activation(hi[:, 4 * b:4 * b + 4, ds((2 * i + u) * P, P)],
                                         bank[:, 2 * u + b, :].rearrange("p (k t) -> p k t", k=4),
                                         ACT.Copy).then_inc(hi_done, 1)

            stats(0, 0)
            with eng.Fori(0, TT // 2 - 1) as i:
                for u in range(2):
                    stats(i + u, 1 - u)
                    take_hi(i, u)
            stats(TT // 2 - 1, 1)
            take_hi(TT // 2 - 1, 0)
            take_hi(TT // 2 - 1, 1)

        @block.vector
        def _(eng):
            nc.vector.memset(eps, EPS).then_inc(eps_set, 1)
            eng.sem_inc(scaled, 2)
            eng.sem_inc(lo_done, 4)
            eng.wait_ge(gain_in, 16)

            def scale(i, u):
                eng.wait_ge(std, 2 * i + u + 1)
                nc.vector.reciprocal(rs[:, u:u + 1], sd[:, u:u + 1]).then_inc(rstd, 1)
                eng.wait_ge(rstd, 2 * i + u + 1)
                nc.vector.scalar_tensor_tensor(
                    out=xs[:, u, :], in0=xr[:, u, :], scalar=rs[:, u:u + 1], in1=gb[:, :],
                    op0=ALU.mult, op1=ALU.mult).then_inc(scaled, 1)

            def take_lo(i, u):
                for b in range(2):
                    eng.wait_ge(hi_done, 4 * i + 2 * u + b + 1)
                    at = (slice(None), slice(4 * b, 4 * b + 4), ds((2 * i + u) * P, P))
                    nc.vector.tensor_tensor(lo[at], bank[:, 2 * u + b, :].rearrange("p (k t) -> p k t", k=4),
                                            f32(hi[at]), ALU.subtract).then_inc(lo_done, 1)

            scale(0, 0)
            with eng.Fori(0, TT // 2 - 1) as i:
                for u in range(2):
                    scale(i + u, 1 - u)
                    take_lo(i, u)
            scale(TT // 2 - 1, 1)
            take_lo(TT // 2 - 1, 0)
            take_lo(TT // 2 - 1, 1)

        @block.tensor
        def _(eng):
            with eng.Fori(0, TT // 2) as i:
                for u in range(2):
                    eng.wait_ge(scaled, 2 * i + u + 3)
                    for b in range(2):
                        eng.wait_ge(lo_done, 4 * i + 2 * u + b + 1)
                        for k in range(4):
                            last = nc.tensor.transpose(bank[:, 2 * u + b, k * P:(k + 1) * P],
                                                       xs[:, u, (4 * b + k) * P:(4 * b + k + 1) * P], ident)
                        last.then_inc(turned, 1)


def three_pass(nc, out, ah, al, bh, bl, first, last):
    nc.tensor.matmul(out, ah, bh, start=first, stop=False)
    nc.tensor.matmul(out, ah, bl, start=False, stop=False)
    return nc.tensor.matmul(out, al, bh, start=False, stop=last)


def project(nc, sp, xh, xl, kb, loop_pairs, loop_cols, loop_dst, rest):
    raw = [sp.at("w_raw", kb + 8 * u, [P, KT, WC]) for u in range(2)]
    wh = [sp.at("w_hi", kb + 16 + 8 * u, [P, KT, WC], F32R) for u in range(2)]
    wl = [sp.at("w_lo", kb + 32 + 8 * u, [P, KT, WC], F32R) for u in range(2)]
    bank = sp.banks
    w_in = [sp.sem("w_in0"), sp.sem("w_in1")]
    hi_done, split, job, free_act, free_dve = (
        sp.sem(s) for s in ("w_hi_done", "w_split", "job", "bank_free_act", "bank_free_dve"))
    n_loop = 2 * loop_pairs
    arrived, count = {}, [16 * loop_pairs] * 2
    for r, (_, sources, _) in enumerate(rest):
        c = n_loop + r
        count[c % 2] += 16 * len(sources)
        arrived[c] = count[c % 2]

    def pieces(kind, j):
        if kind == "T" or (kind == "KV" and j < 2):
            return [(0, 512, j // 2, j % 2)]
        if kind == "V":
            return [(256 * z, 256, 2 * j + z, None) for z in range(2)]
        return [(128 * z, 128, 4 * (j - 2) + z, None) for z in range(4)]

    with nc.Block() as block:
        @block.sync
        def _(eng):
            with eng.Fori(0, loop_pairs) as i:
                for u in range(2):
                    eng.wait_ge(split, 2 * i + u + 1)
                    eng.dma_start(raw[u][:, :, :], loop_cols(2 * i + u)).then_inc(w_in[u], 16)
            for r, (_, sources, _) in enumerate(rest):
                c = n_loop + r
                eng.wait_ge(split, c + 1)
                for at, src in sources:
                    eng.dma_start(raw[c % 2][:, :, at:at + src.shape[2]], src).then_inc(w_in[c % 2], 16)

        def evacuate(eng, c, u, j, dst, copy, free):
            eng.wait_ge(job, 4 * c + j + 9)
            src = bank[:, 4 * u + j, :]
            if len(dst.shape) == 3:
                src = src.rearrange("p (a b) -> p a b", a=dst.shape[1])
            copy(dst, src).then_inc(free, 1)

        @block.scalar
        def _(eng):
            eng.sem_inc(free_act, 4)

            def hi(c, u, there):
                eng.wait_ge(w_in[u], there)
                eng.wait_ge(job, 4 * c + 4)
                nc.scalar.activation(wh[u][:, :, :], raw[u][:, :, :], ACT.Copy).then_inc(hi_done, 1)

            def out(c, u, dst):
                for j in range(2):
                    evacuate(eng, c, u, j, dst(j), lambda o, s: nc.scalar.activation(o, s, ACT.Copy), free_act)

            hi(0, 0, 16)
            with eng.Fori(0, loop_pairs - 1) as i:
                hi(2 * i + 1, 1, 16 * i + 16)
                out(2 * i, 0, lambda j: loop_dst(2 * i, j))
                hi(2 * i + 2, 0, 16 * i + 32)
                out(2 * i + 1, 1, lambda j: loop_dst(2 * i + 1, j))
            c = n_loop - 1
            hi(c, 1, 16 * loop_pairs)
            out(c - 1, 0, lambda j: loop_dst(c - 1, j))
            for r, (_, _, dst) in enumerate(rest):
                hi(n_loop + r, (n_loop + r) % 2, arrived[n_loop + r])
                before = (lambda j: loop_dst(c, j)) if r == 0 else rest[r - 1][2]
                out(n_loop + r - 1, (n_loop + r - 1) % 2, before)
            out(n_loop + len(rest) - 1, (n_loop + len(rest) - 1) % 2,
                rest[-1][2] if rest else lambda j: loop_dst(c, j))

        @block.vector
        def _(eng):
            eng.sem_inc(free_dve, 4)
            eng.sem_inc(split, 2)

            def lo(c, u):
                eng.wait_ge(hi_done, c + 1)
                nc.vector.tensor_tensor(wl[u][:, :, :], raw[u][:, :, :], f32(wh[u][:, :, :]),
                                        ALU.subtract).then_inc(split, 1)

            def out(c, u, dst):
                for j in range(2, 4):
                    evacuate(eng, c, u, j, dst(j), nc.vector.tensor_copy, free_dve)

            lo(0, 0)
            with eng.Fori(0, loop_pairs - 1) as i:
                lo(2 * i + 1, 1)
                out(2 * i, 0, lambda j: loop_dst(2 * i, j))
                lo(2 * i + 2, 0)
                out(2 * i + 1, 1, lambda j: loop_dst(2 * i + 1, j))
            c = n_loop - 1
            lo(c, 1)
            out(c - 1, 0, lambda j: loop_dst(c - 1, j))
            for r in range(len(rest)):
                lo(n_loop + r, (n_loop + r) % 2)
                before = (lambda j: loop_dst(c, j)) if r == 0 else rest[r - 1][2]
                out(n_loop + r - 1, (n_loop + r - 1) % 2, before)
            out(n_loop + len(rest) - 1, (n_loop + len(rest) - 1) % 2,
                rest[-1][2] if rest else lambda j: loop_dst(c, j))

        @block.tensor
        def _(eng):
            eng.sem_inc(job, 8)

            def chunk(c, u, kind):
                eng.wait_ge(split, c + 3)
                for j in range(4):
                    eng.wait_ge(free_act if j < 2 else free_dve, 2 * c + j % 2 + 1)
                    for at, n, tile, half in pieces(kind, j):
                        for k in range(KT):
                            o = bank[:, 4 * u + j, at:at + n]
                            if half is None:
                                t = slice(tile * P, (tile + 1) * P)
                                cols = slice(0, WC) if kind == "V" else slice(P, WC)
                                last = three_pass(nc, o, xh[:, k, t], xl[:, k, t], wh[u][:, k, cols],
                                                  wl[u][:, k, cols], k == 0, k == KT - 1)
                            else:
                                w = slice(tile * P, (tile + 1) * P)
                                t = slice(half * HALF, (half + 1) * HALF)
                                last = three_pass(nc, o, wh[u][:, k, w], wl[u][:, k, w], xh[:, k, t],
                                                  xl[:, k, t], k == 0, k == KT - 1)
                    last.then_inc(job, 1)

            with eng.Fori(0, loop_pairs) as i:
                for u in range(2):
                    chunk(2 * i + u, u, "T")
            for r, (kind, _, _) in enumerate(rest):
                chunk(n_loop + r, (n_loop + r) % 2, kind)


def attention(nc, sp, ident, table, qkT, va, vb, sinks, diff_lambda):
    tab = sp.at("tables", 136, [P, C_END - C_SWA])
    s = [sp.at("scores", 160 + 8 * u, [P, 2, 1024]) for u in range(2)]
    wt = [sp.at("weights", 176 + 4 * u, [P, 1024]) for u in range(2)]
    wT = [sp.at("weightsT", 184 + 4 * u, [P, 1024]) for u in range(2)]
    sink = sp.at("sink", 192, [P, SWA_HEADS])
    lp = sp.at("lambda_parts", 192.25, [P, 4, HD])
    lprod = sp.at("lambda_products", 193.25, [P, 2, HD])
    lam = sp.at("lambda_small", 193.75, [P, 8])
    mx, ng, sm, rc = (sp.at(n, 194 + 0.25 * m, [P, 2, 2]) for m, n in enumerate(("max", "negmax", "sum", "recip")))
    es = sp.at("sink_term", 195, [P, 2, 2])
    rl = sp.at("lambda_recip", 195.25, [P, 2])
    bank = sp.banks
    s_ps = bank[:, 0:4, :].rearrange("p (m b) c -> p m (b c)", m=2)
    t_ps = bank[:, 4:6, :].rearrange("p b c -> p (b c)")
    o_ps = [bank[:, 6, 0:P], bank[:, 7, 0:P]]

    items = []
    for i in range(TT):
        for j in range(4):
            k0 = max(0, i - 1)
            items.append(("swa", i, j, list(range(k0, i + 1))))
        for h in range(DIFF_HEADS):
            items.append(("diff", i, h, list(range(i + 1))))
    N = len(items)
    tables_in, small_in, lam_sum, lam_exp, lam_ready = (
        sp.sem(n) for n in ("tables_in", "small_in", "lam_sum", "lam_exp", "lam_ready"))
    scored, masked, exped, weighed, turned, out_t, valued, out_o, dve = (
        sp.sem(n) for n in ("scored", "masked", "exped", "weighed", "turned", "wT_ready", "valued", "o_out", "dve"))

    def q_tile(kind, h):
        return (T_QA if kind == "swa" else T_QB) + h

    with nc.Block() as block:
        @block.sync
        def _(eng):
            eng.dma_start(tab[:, :], table[:, C_SWA:C_END]).then_inc(tables_in, 16)
            eng.dma_start(sink[:, :], sinks[0].partition_broadcast(P)).then_inc(small_in, 16)
            eng.dma_start(lp[:, :, :], diff_lambda[0].partition_broadcast(P)).then_inc(small_in, 16)

        @block.tensor
        def _(eng):
            def scores(n):
                kind, i, h, kts = items[n]
                if n >= 1:
                    eng.wait_ge(masked, n)
                k_tile = T_KA if kind == "swa" else T_KB + h
                for m in range(2):
                    r = slice(m * HD, (m + 1) * HD)
                    k0, k1 = kts[0] * P, (kts[-1] + 1) * P
                    for a in range(k0, k1, 512):
                        b = min(k1, a + 512)
                        last = nc.tensor.matmul(s_ps[:, m, a - k0:b - k0], qkT[r, q_tile(kind, h), i * P:(i + 1) * P],
                                                qkT[r, k_tile, a:b], start=True, stop=True)
                last.then_inc(scored, 1)

            def turn(n):
                kind, i, h, kts = items[n]
                eng.wait_ge(weighed, n + 1)
                if n >= 1:
                    eng.wait_ge(out_t, n)
                blocks = len(kts) * (2 if kind == "swa" else 1)
                for b in range(blocks):
                    last = nc.tensor.transpose(t_ps[:, b * P:(b + 1) * P], wt[n % 2][:, b * P:(b + 1) * P], ident)
                last.then_inc(turned, 1)

            def values(n):
                kind, i, h, kts = items[n]
                eng.wait_ge(out_t, n + 1)
                if n >= 2:
                    eng.wait_ge(out_o, n - 1)
                if kind == "swa":
                    for a in range(2):
                        r = slice(a * HD, (a + 1) * HD)
                        for b, kt in enumerate(kts):
                            at = (a * len(kts) + b) * P
                            last = nc.tensor.matmul(o_ps[n % 2][r, :], va[:, kt, r], wT[n % 2][:, at:at + P],
                                                    start=b == 0, stop=b == len(kts) - 1)
                else:
                    for b, kt in enumerate(kts):
                        last = nc.tensor.matmul(o_ps[n % 2], vb[:, kt, h * P:(h + 1) * P],
                                                wT[n % 2][:, b * P:(b + 1) * P], start=b == 0, stop=b == len(kts) - 1)
                last.then_inc(valued, 1)

            scores(0)
            scores(1)
            for n in range(N):
                if n + 2 < N:
                    scores(n + 2)
                if n >= 1:
                    values(n - 1)
                turn(n)
            values(N - 1)

        @block.vector
        def _(eng):
            count = [0]

            def link(ins):
                count[0] += 1
                ins.then_inc(dve, 1)
                eng.wait_ge(dve, count[0])

            eng.wait_ge(small_in, 32)
            for m in range(2):
                nc.vector.tensor_tensor_reduce(out=lprod[:, m, :], in0=lp[:, 2 * m, :], in1=lp[:, 2 * m + 1, :],
                                               scale=1.0, scalar=0.0, op0=ALU.mult, op1=ALU.add,
                                               accum_out=lam[:, m:m + 1]).then_inc(lam_sum, 1)
            eng.wait_ge(lam_exp, 1)
            link(nc.vector.tensor_tensor(lam[:, 4:5], lam[:, 3:4], lam[:, 2:3], ALU.subtract))
            link(nc.vector.tensor_scalar(lam[:, 5:6], lam[:, 4:5], LAMBDA_INIT, None, ALU.subtract))
            eng.wait_ge(tables_in, 16)

            def mask(n):
                kind, i, h, kts = items[n]
                u, k = n % 2, len(kts) * P
                eng.wait_ge(scored, n + 1)
                if n >= 2:
                    eng.wait_ge(weighed, n - 1)
                for m in range(2):
                    if kind == "swa":
                        at = (2 * h + m) * 256 + 256 - k
                    else:
                        at = C_DIFF - C_SWA + h * 1024 + 1024 - k
                    last = nc.vector.tensor_tensor_reduce(
                        out=s[u][:, m, 0:k], in0=s_ps[:, m, 0:k], in1=tab[:, at:at + k], scale=0.125,
                        scalar=LOWEST, op0=ALU.add, op1=ALU.max, accum_out=mx[:, u, m:m + 1])
                link(last)
                if kind == "swa":
                    link(nc.vector.tensor_tensor(mx[:, u, :], mx[:, u, :], sink[:, h:h + 5:4], ALU.max))
                    nc.vector.tensor_tensor(es[:, u, :], sink[:, h:h + 5:4], mx[:, u, :], ALU.subtract)
                nc.vector.tensor_scalar(ng[:, u, :], mx[:, u, :], -1.0, None, ALU.mult).then_inc(masked, 1)

            def weigh(n):
                kind, i, h, kts = items[n]
                u, k = n % 2, len(kts) * P
                eng.wait_ge(exped, n + 1)
                if kind == "swa":
                    link(nc.vector.tensor_tensor(sm[:, u, :], sm[:, u, :], es[:, u, :], ALU.add))
                link(nc.vector.reciprocal(rc[:, u, :], sm[:, u, :]))
                if n >= 2:
                    eng.wait_ge(turned, n - 1)
                if kind == "swa":
                    nc.vector.tensor_scalar(wt[u][:, 0:k], s[u][:, 0, 0:k], rc[:, u, 0:1], None, ALU.mult)
                    nc.vector.tensor_scalar(wt[u][:, k:2 * k], s[u][:, 1, 0:k], rc[:, u, 1:2], None,
                                            ALU.mult).then_inc(weighed, 1)
                else:
                    nc.vector.tensor_tensor(rl[:, u:u + 1], rc[:, u, 1:2], lam[:, 5:6], ALU.mult)
                    link(nc.vector.tensor_scalar(wt[u][:, 0:k], s[u][:, 0, 0:k], rc[:, u, 0:1], None, ALU.mult))
                    nc.vector.scalar_tensor_tensor(
                        out=wt[u][:, 0:k], in0=s[u][:, 1, 0:k], scalar=rl[:, u:u + 1], in1=wt[u][:, 0:k],
                        op0=ALU.mult, op1=ALU.add).then_inc(weighed, 1)

            def output(n):
                kind, i, h, _ = items[n]
                eng.wait_ge(valued, n + 1)
                nc.vector.tensor_copy(qkT[:, q_tile(kind, h), i * P:(i + 1) * P], o_ps[n % 2]).then_inc(out_o, 1)

            mask(0)
            for n in range(N):
                if n + 1 < N:
                    mask(n + 1)
                weigh(n)
                if n >= 2:
                    output(n - 2)
            output(N - 2)
            output(N - 1)

        @block.scalar
        def _(eng):
            eng.wait_ge(lam_sum, 2)
            nc.scalar.activation(lam[:, 2:4], lam[:, 0:2], ACT.Exp).then_inc(lam_exp, 1)

            def exps(n):
                kind, i, h, kts = items[n]
                u, k = n % 2, len(kts) * P
                eng.wait_ge(masked, n + 1)
                for m in range(2):
                    last = nc.scalar.activation(s[u][:, m, 0:k], s[u][:, m, 0:k], ACT.Exp, bias=ng[:, u, m:m + 1],
                                                accum_out=sm[:, u, m:m + 1])
                if kind == "swa":
                    last = nc.scalar.activation(es[:, u, :], es[:, u, :], ACT.Exp)
                last.then_inc(exped, 1)

            def out_turned(n):
                kind, i, h, kts = items[n]
                c = len(kts) * P * (2 if kind == "swa" else 1)
                eng.wait_ge(turned, n + 1)
                if n >= 2:
                    eng.wait_ge(valued, n - 1)
                nc.scalar.activation(wT[n % 2][:, 0:c], t_ps[:, 0:c], ACT.Copy).then_inc(out_t, 1)

            exps(0)
            for n in range(N):
                if n + 1 < N:
                    exps(n + 1)
                out_turned(n)


def gate_and_up(nc, sp, xh, xl, oT, oh, ol, mT, subln_g, w_in, gate_bias, w_up_a, w_up_b):
    sq = sp.at("head_squares", 144, [P, 4, T])
    sd = sp.at("head_std", 128, [P, 2, T])
    ones = sp.at("mean_matrix", 205, [P, P])
    g = sp.at("subln_gain", 205.5, [P, 2])
    eps = sp.at("head_eps", 205.75, [P, 1])
    g_in, made, squared, meaned, std, dve, hi_swa, headed, headed_too = (
        sp.sem(n) for n in ("g_in", "const_set", "squared", "meaned", "std", "dve", "hi_swa", "headed",
                            "headed_by_pool"))
    raw = [sp.at("gate_raw", 160 + 4 * s, [P, KT, P]) for s in range(3)]
    wh = [sp.at("gate_hi", 172 + 4 * s, [P, KT, P], F32R) for s in range(3)]
    wl = [sp.at("gate_lo", 184 + 4 * s, [P, KT, P], F32R) for s in range(3)]
    sg = [sp.at("sigmoid", 196 + 4 * s, [P, T]) for s in range(2)]
    bias = sp.at("gate_bias", 204, [P, 16])
    bank = sp.banks
    pair = [bank[:, 2 * s:2 * s + 2, :].rearrange("p b c -> p (b c)") for s in range(4)]
    w_in3 = w_in.rearrange("(k p) c -> p k c", p=P)
    ua = w_up_a.rearrange("(a j c) n -> a c j n", a=2, c=HD)
    ub = w_up_b.rearrange("(k p) n -> p k n", p=P)
    loaded = [sp.sem(f"loaded{s}") for s in range(3)]
    hi_done = [sp.sem(f"hi_done{s}") for s in range(3)]
    split = [sp.sem(f"split{s}") for s in range(3)]
    multiplied = [sp.sem(f"multiplied{s}") for s in range(3)]
    squashed = [sp.sem(f"squashed{s}") for s in range(2)]
    sig_free, bias_in, mixed = sp.sem("sig_free"), sp.sem("bias_in"), sp.sem("mixed")

    with nc.Block() as block:
        @block.sync
        def _(eng):
            with nc.allow_non_contiguous_dma(reason="128 gains, one to a partition"):
                eng.dma_start(g[:, 0:1], subln_g.rearrange("o d -> d o")).then_inc(g_in, 16)
            with nc.allow_non_contiguous_dma(reason="2048 biases, one to a partition"):
                eng.dma_start(bias[:, :], gate_bias.rearrange("o (t p) -> p (o t)", p=P)).then_inc(bias_in, 16)
            with eng.Fori(0, KT) as j:
                for s in range(2):
                    eng.wait_ge(split[s], j + 1)
                    eng.dma_start(raw[s][:, :, :], w_in3[:, :, ds(GL + s * D + j * P, P)]).then_inc(loaded[s], 16)
                eng.wait_ge(split[2], j + 1)
                for a in (1, 0):
                    eng.dma_start(raw[2][a * HD:(a + 1) * HD, 0:4, :], ua[a, :, :, ds(j * P, P)]).then_inc(loaded[2], 16)
                eng.dma_start(raw[2][:, 4:8, :], ub[:, :, ds(j * P, P)]).then_inc(loaded[2], 16)

        @block.scalar
        def _(eng):
            def finish_heads():
                eng.wait_ge(made, 2)
                for h in range(4):
                    eng.wait_ge(meaned, h + 1)
                    if h >= 2:
                        eng.wait_ge(dve, 4 * (h - 1) + 1)
                    nc.scalar.activation(sd[:, h % 2, :], pair[2 + h % 2], ACT.Sqrt, bias=eps[:, 0:1]).then_inc(std, 1)
                    if h == 1:
                        for w in (2, 3, 0, 1):
                            nc.scalar.activation(oh[:, w, :], oT[:, T_QA + w, :], ACT.Copy).then_inc(hi_swa, 1)

            def take_hi(j, s):
                eng.wait_ge(loaded[s], (16 if s < 2 else 48) * (j + 1))
                eng.wait_ge(multiplied[s], j + 1)
                nc.scalar.activation(wh[s][:, :, :], raw[s][:, :, :], ACT.Copy).then_inc(hi_done[s], 1)

            def body(j, last):
                take_hi(j, 2)
                eng.wait_ge(sig_free, j + 1)
                for s in range(2):
                    eng.wait_ge(multiplied[s], j + 2)
                    nc.scalar.activation(sg[s][:, :], pair[s], ACT.Sigmoid,
                                         bias=bias[:, ds(8 * s + j, 1)]).then_inc(squashed[s], 1)
                    if not last:
                        take_hi(j + 1, s)

            for h in range(4):
                nc.scalar.activation(sq[:, h, :], oT[:, T_QB + h, :], ACT.Square).then_inc(squared, 1)
            for s in range(2):
                take_hi(0, s)
            finish_heads()
            eng.wait_ge(bias_in, 16)
            with eng.Fori(0, KT - 1) as j:
                body(j, False)
            body(KT - 1, True)

        @block.gpsimd
        def _(eng):
            for h in (2, 3):
                eng.wait_ge(hi_swa, h - 1)
                nc.gpsimd.tensor_tensor(ol[:, h, :], oT[:, T_QA + h, :], f32(oh[:, h, :]),
                                        ALU.subtract).then_inc(headed_too, 1)

        @block.vector
        def _(eng):
            for s in range(3):
                eng.sem_inc(split[s], 1)
            eng.sem_inc(sig_free, 1)
            nc.vector.memset(ones[:, :], 1.0 / P).then_inc(made, 1)
            nc.vector.memset(eps[:, :], EPS).then_inc(made, 1)

            def finish_heads():
                count = [0]

                def link(ins):
                    count[0] += 1
                    ins.then_inc(dve, 1)
                    eng.wait_ge(dve, count[0])

                eng.wait_ge(g_in, 16)
                link(nc.vector.tensor_scalar(g[:, 1:2], g[:, 0:1], 1.0 - LAMBDA_INIT, None, ALU.mult))
                for h in range(4):
                    eng.wait_ge(std, h + 1)
                    r, o = sd[:, h % 2, :], oT[:, T_QB + h, :]
                    link(nc.vector.reciprocal(r, r))
                    link(nc.vector.tensor_tensor(r, o, r, ALU.mult))
                    link(nc.vector.tensor_scalar(oh[:, 4 + h, :], r, g[:, 1:2], None, ALU.mult))
                    eng.wait_ge(meaned, h + 1)
                    link(nc.vector.scalar_tensor_tensor(out=ol[:, 4 + h, :], in0=r, scalar=g[:, 1:2],
                                                        in1=f32(oh[:, 4 + h, :]), op0=ALU.mult, op1=ALU.subtract))
                for h in range(2):
                    eng.wait_ge(hi_swa, h + 3)
                    nc.vector.tensor_tensor(ol[:, h, :], oT[:, T_QA + h, :], f32(oh[:, h, :]),
                                            ALU.subtract).then_inc(headed, 1)

            def take_lo(j, s):
                eng.wait_ge(hi_done[s], j + 1)
                nc.vector.tensor_tensor(wl[s][:, :, :], raw[s][:, :, :], f32(wh[s][:, :, :]),
                                        ALU.subtract).then_inc(split[s], 1)

            def body(j, last):
                take_lo(j, 2)
                if not last:
                    for s in range(2):
                        take_lo(j + 1, s)
                eng.wait_ge(multiplied[2], j + 2)
                for s in range(2):
                    eng.wait_ge(squashed[s], j + 1)
                    nc.vector.tensor_tensor(sg[s][:, :], sg[s][:, :], pair[2 + s], ALU.mult).then_inc(mixed, 1)
                eng.wait_ge(mixed, 2 * j + 2)
                nc.vector.tensor_tensor(mT[:, ds(j, 1), :].rearrange("p o t -> p (o t)"), sg[0][:, :], sg[1][:, :],
                                        ALU.add).then_inc(sig_free, 1)

            for s in range(2):
                take_lo(0, s)
            finish_heads()
            with eng.Fori(0, KT - 1) as j:
                body(j, False)
            body(KT - 1, True)

        @block.tensor
        def _(eng):
            for s in range(3):
                eng.sem_inc(multiplied[s], 1)

            def mean_squares(h):
                eng.wait_ge(squared, h + 1)
                if h >= 2:
                    eng.wait_ge(std, h - 1)
                for b in range(2):
                    last = nc.tensor.matmul(bank[:, 4 + 2 * (h % 2) + b, :], ones[:, :],
                                            sq[:, h, b * 512:(b + 1) * 512], start=True, stop=True)
                last.then_inc(meaned, 1)

            def body(j, first):
                for s in range(2):
                    if first:
                        for h in range(2 * s, 2 * s + 2):
                            mean_squares(h)
                    eng.wait_ge(split[s], j + 2)
                    if not first:
                        eng.wait_ge(squashed[s], j)
                    for half in range(2):
                        t = slice(half * HALF, (half + 1) * HALF)
                        for k in range(KT):
                            last = three_pass(nc, bank[:, 2 * s + half, :], wh[s][:, k, :], wl[s][:, k, :],
                                              xh[:, k, t], xl[:, k, t], k == 0, k == KT - 1)
                    last.then_inc(multiplied[s], 1)
                eng.wait_ge(split[2], j + 2)
                eng.wait_ge(sig_free, j + 1)
                if first:
                    eng.wait_ge(std, 4)
                    eng.wait_ge(headed, 2)
                    eng.wait_ge(headed_too, 2)
                    eng.wait_ge(dve, 4 * 4 + 1)
                for s in range(2):
                    for half in range(2):
                        t = slice(half * HALF, (half + 1) * HALF)
                        for k in range(4 * s, 4 * s + 4):
                            last = three_pass(nc, bank[:, 4 + 2 * s + half, :], wh[2][:, k, :], wl[2][:, k, :],
                                              oh[:, k, t], ol[:, k, t], k == 4 * s, k == 4 * s + 3)
                last.then_inc(multiplied[2], 1)

            eng.wait_ge(made, 1)
            body(0, True)
            with eng.Fori(1, KT) as j:
                body(j, False)


def mix_out(nc, sp, mT, x, w_out, x1):
    mh = [sp.at("merged_hi", 4 * u, [P, KT, P], F32R) for u in range(2)]
    ml = [sp.at("merged_lo", 8 + 4 * u, [P, KT, P], F32R) for u in range(2)]
    raw = [sp.at("wo_raw", 16 + 8 * u, [P, KT, WC]) for u in range(2)]
    wh = sp.at("wo_hi", 96, [P, KT, D], F32R)
    wl = sp.at("wo_lo", 128, [P, KT, D], F32R)
    xr = [sp.at("residual", 160 + 4 * u, [P, D]) for u in range(2)]
    y = [sp.at("x1_tile", 168 + 4 * u, [P, D]) for u in range(2)]
    bank = sp.banks
    pair = [bank[:, 2 * u:2 * u + 2, :].rearrange("p b c -> p (b c)") for u in range(2)]
    wo = w_out.rearrange("(k p) c -> p k c", p=P)
    xt = x.rearrange("(t p) d -> t p d", p=P)
    x1t = x1.rearrange("(t p) d -> t p d", p=P)
    w_in = [sp.sem("wo_in0"), sp.sem("wo_in1")]
    x_in = [sp.sem("x_in0"), sp.sem("x_in1")]
    stored = [sp.sem("stored0"), sp.sem("stored1")]
    w_hi, w_lo, m_hi, m_lo, multiplied, added, y_free = (
        sp.sem(n) for n in ("w_hi", "w_lo", "m_hi", "m_lo", "multiplied", "added", "y_free"))
    NC = D // WC

    with nc.Block() as block:
        @block.sync
        def _(eng):
            for c in range(NC):
                if c >= 2:
                    eng.wait_ge(w_lo, c - 1)
                eng.dma_start(raw[c % 2][:, :, :], wo[:, :, c * WC:(c + 1) * WC]).then_inc(w_in[c % 2], 16)
            with eng.Fori(0, TT // 2) as i:
                for u in range(2):
                    eng.wait_ge(added, 2 * i + u + 1)
                    eng.dma_start(xr[u][:, :], xt[2 * i + u, :, :]).then_inc(x_in[u], 16)

        @block.gpsimd
        def _(eng):
            eng.sem_inc(y_free, 2)
            with eng.Fori(0, TT // 2) as i:
                for u in range(2):
                    eng.wait_ge(added, 2 * i + u + 3)
                    eng.dma_start(x1t[2 * i + u, :, :], y[u][:, :]).then_inc(stored[u], 16)
                    eng.wait_ge(stored[u], 16 * i + 16)
                    eng.sem_inc(y_free, 1)

        @block.scalar
        def _(eng):
            def take_hi(t, u):
                nc.scalar.activation(mh[u][:, :, :], mT[:, :, ds(t * P, P)], ACT.Copy).then_inc(m_hi, 1)

            for u in range(2):
                take_hi(u, u)
            for c in range(NC):
                eng.wait_ge(w_in[c % 2], 16 * (c // 2) + 16)
                nc.scalar.activation(wh[:, :, c * WC:(c + 1) * WC], raw[c % 2][:, :, :], ACT.Copy).then_inc(w_hi, 1)
            with eng.Fori(1, TT // 2) as i:
                for u in range(2):
                    eng.wait_ge(multiplied, 2 * i + u + 1)
                    take_hi(2 * i + u, u)

        @block.vector
        def _(eng):
            eng.sem_inc(added, 2)

            def split(t, u):
                eng.wait_ge(m_hi, t + 1)
                nc.vector.tensor_tensor(ml[u][:, :, :], mT[:, :, ds(t * P, P)], f32(mh[u][:, :, :]),
                                        ALU.subtract).then_inc(m_lo, 1)

            split(0, 0)
            for c in range(NC):
                eng.wait_ge(w_hi, c + 1)
                at = (slice(None), slice(None), slice(c * WC, (c + 1) * WC))
                nc.vector.tensor_tensor(wl[at], raw[c % 2][:, :, :], f32(wh[at]), ALU.subtract).then_inc(w_lo, 1)

            def add(t, i, u):
                eng.wait_ge(multiplied, t + 3)
                eng.wait_ge(x_in[u], 16 * i + 16)
                eng.wait_ge(y_free, t + 1)
                nc.vector.tensor_tensor(y[u][:, :], pair[u], xr[u][:, :],
                                        ALU.add).then_inc(added, 1)

            with eng.Fori(0, TT // 2 - 1) as i:
                split(2 * i + 1, 1)
                add(2 * i, i, 0)
                split(2 * i + 2, 0)
                add(2 * i + 1, i, 1)
            split(TT - 1, 1)
            add(TT - 2, TT // 2 - 1, 0)
            add(TT - 1, TT // 2 - 1, 1)

        @block.tensor
        def _(eng):
            eng.sem_inc(multiplied, 2)

            def tile(t, u, first=False):
                eng.wait_ge(m_lo, t + 1)
                eng.wait_ge(added, t + 1)
                for b in range(2):
                    if first:
                        eng.wait_ge(w_lo, NC * (b + 1) // 2)
                    c = slice(b * 512, (b + 1) * 512)
                    for k in range(KT):
                        last = three_pass(nc, bank[:, 2 * u + b, :], mh[u][:, k, :], ml[u][:, k, :],
                                          wh[:, k, c], wl[:, k, c], k == 0, k == KT - 1)
                last.then_inc(multiplied, 1)

            tile(0, 0, True)
            tile(1, 1)
            with eng.Fori(1, TT // 2) as i:
                for u in range(2):
                    tile(2 * i + u, u)


def turn_subkeys(nc, sp, ident, subkeys, skT, xl, park, parked):
    raw = sp.at("subkeys", 128, [P, HP, P])
    bank = sp.banks
    key_in, turned = sp.sem("key_in"), sp.sem("turned")
    with nc.Block() as block:
        @block.sync
        def _(eng):
            eng.dma_start(raw[:, :, :], subkeys.rearrange("h q n d -> n (h q) d")).then_inc(key_in, 16)
            eng.dma_start(park, f32(xl[:, :, :])).then_inc(parked, 16)

        @block.tensor
        def _(eng):
            eng.wait_ge(key_in, 16)
            for hp in range(HP):
                last = nc.tensor.transpose(bank[:, hp // 4, (hp % 4) * P:(hp % 4 + 1) * P], raw[:, hp, :], ident)
            last.then_inc(turned, 1)

        @block.scalar
        def _(eng):
            eng.wait_ge(turned, 1)
            nc.scalar.activation(skT[:, :, :], bank[:, 0:4, :].rearrange("p b (q n) -> p (b q) n", n=P), ACT.Copy)


def select_experts(nc, sp, ident, qT, skT, picks, table, parked, kb):
    SHORT = TOPK // 2
    CANDS = TOPK + (TOPK - 1) * SHORT
    qs = sp.at("q_tile", kb, [P, HP, P])
    s = sp.at("key_scores", kb + 8, [P, HP, NK])
    s2 = sp.at("key_scores_left", kb + 16, [P, HP, NK])
    cand = sp.at("candidates", kb + 24, [P, PH, CANDS])
    cand2 = sp.at("candidates_left", kb + 32, [P, PH, CANDS])
    hot = sp.at("rank_match", kb + 40, [P, PH, TOPK, TOPK])
    top = sp.at("top", kb + 48, [P, HP, TOPK])
    top_i = sp.at("top_index", kb + 49, [P, HP, TOPK], U32)
    top_f = sp.at("top_index_f", kb + 50, [P, HP, TOPK])
    best = sp.at("best", kb + 51, [P, PH, TOPK])
    best_i = sp.at("best_index", kb + 51.5, [P, PH, TOPK], U32)
    rank_i = sp.at("rank", kb + 52, [P, PH, TOPK], U32)
    place_f = sp.at("place_f", kb + 56.5, [P, PH * TOPK])
    begin_f = sp.at("row_begin_f", kb + 57, [P, PH * TOPK])
    rank_f = sp.at("rank_f", kb + 53, [P, 2, PH, TOPK])
    e = sp.at("best_exp", kb + 54, [P, PH, TOPK])
    found = sp.at("found", kb + 54.5, [P, 3, PH * TOPK])
    norm = sp.at("best_norm", kb + 56, [P, 2, PH])
    iota16 = sp.at("iota16", kb + 56.25, [P, TOPK])
    bank = sp.banks
    iota_in, q_here, scored, s_here, exp_in, exped, found_all, turned, picked, dve = (
        sp.sem(n) for n in ("iota_in", "q_here", "scored", "s_here", "exp_in", "exped", "found_all", "turned",
                            "picked", "dve"))
    s_free, steady = sp.sem("s_free"), sp.sem("steady")
    LINKS = 26

    with nc.Block() as block:
        @block.sync
        def _(eng):
            eng.dma_start(iota16[:, :], table[:, C_IOTA16:C_IOTA16 + TOPK]).then_inc(iota_in, 16)

        @block.gpsimd
        def _(eng):
            with eng.Fori(0, TT) as t:
                eng.wait_ge(scored, t + 1)
                nc.gpsimd.tensor_copy(qs[:, :, :], qT[:, :, ds(t * P, P)]).then_inc(q_here, 1)

        @block.tensor
        def _(eng):
            def score(t):
                eng.wait_ge(q_here, t + 1)
                eng.wait_ge(s_here, t + 1)
                for hp in range(HP):
                    last = nc.tensor.matmul(bank[:, hp // 4, (hp % 4) * P:(hp % 4 + 1) * P], qs[:, hp, :],
                                            skT[:, hp, :], start=True, stop=True)
                last.then_inc(scored, 1)

            def body(t, last_tile):
                if not last_tile:
                    score(t + 1)
                eng.wait_ge(found_all, t + 1)
                eng.wait_ge(picked, t + 1)
                for m in range(3):
                    last = nc.tensor.transpose(bank[:, 4, m * P:(m + 1) * P], found[:, m, :], ident)
                last.then_inc(turned, 1)

            eng.sem_inc(scored, 1)
            eng.sem_inc(turned, 1)
            score(0)
            with eng.Fori(0, TT - 1) as t:
                body(t, False)
            body(TT - 1, True)

        @block.scalar
        def _(eng):
            eng.sem_inc(s_here, 1)
            eng.sem_inc(picked, 1)

            def take_scores(t):
                eng.wait_ge(scored, t + 2)
                eng.wait_ge(s_free, t + 1)
                nc.scalar.activation(s[:, :, :], bank[:, 0:4, :].rearrange("p b (q n) -> p (b q) n", n=NK),
                                     ACT.Copy).then_inc(s_here, 1)

            def body(t, last_tile):
                if not last_tile:
                    take_scores(t + 1)
                eng.wait_ge(exp_in, t + 1)
                nc.scalar.activation(e[:, :, :], e[:, :, :], ACT.Exp).then_inc(exped, 1)
                eng.wait_ge(turned, t + 2)
                nc.scalar.activation(picks[:, :, ds(t * P, P)],
                                     bank[:, 4, 0:3 * P].rearrange("p (m t) -> p m t", m=3),
                                     ACT.Copy).then_inc(picked, 1)

            take_scores(0)
            eng.wait_ge(parked, 16)
            with eng.Fori(0, TT - 1) as t:
                body(t, False)
            body(TT - 1, True)

        @block.vector
        def _(eng):
            eng.sem_inc(s_free, 1)
            eng.wait_ge(iota_in, 16)
            with eng.Fori(0, TT) as t:
                n = [0]

                def link(ins):
                    n[0] += 1
                    ins.then_inc(dve, 1)
                    eng.wait_ge(dve, LINKS * t + n[0])
                    eng.sem_inc(steady, 1)

                def top16(rows, values, left, out, out_i, after=None):
                    for r in range(rows):
                        last = nc.vector.max(out[:, r, 0:8], values(r))
                    link(last)
                    for r in range(rows):
                        nc.vector.max_index(out_i[:, r, 0:8], out[:, r, 0:8], values(r))
                    for r in range(rows):
                        last = nc.vector.match_replace(left(r), out[:, r, 0:8], values(r), LOWEST)
                    link(last)
                    if after is not None:
                        after()
                    for r in range(rows):
                        last = nc.vector.max(out[:, r, 8:16], left(r))
                    link(last)
                    for r in range(rows):
                        last = nc.vector.max_index(out_i[:, r, 8:16], out[:, r, 8:16], left(r))
                    link(last)

                eng.wait_ge(s_here, t + 2)
                eng.sem_inc(steady, 1)
                top16(HP, lambda r: s[:, r, :], lambda r: s2[:, r, :], top, top_i,
                      lambda: eng.sem_inc(s_free, 1))
                nc.vector.tensor_copy(top_f[:, :, :], top_i[:, :, :])
                a = top[:, :, :].rearrange("p (h q) k -> p h q k", q=2)
                nc.vector.tensor_tensor(cand[:, :, 0:TOPK], rep(a[:, :, 0, 0], 2, TOPK), a[:, :, 1, :], ALU.add)
                link(nc.vector.tensor_tensor(
                    cand[:, :, TOPK:CANDS].rearrange("p h (a b) -> p h a b", b=SHORT),
                    rep(a[:, :, 0, 1:TOPK], 3, SHORT), rep(a[:, :, 1, 0:SHORT], 2, TOPK - 1), ALU.add))
                top16(PH, lambda r: cand[:, r, :], lambda r: cand2[:, r, :], best, best_i)
                nc.vector.tensor_tensor(e[:, :, :], best[:, :, :], rep(best[:, :, 0], 2, TOPK),
                                        ALU.subtract).then_inc(exp_in, 1)
                flat = "p h k -> p (h k)"
                rank = [rank_f[:, q, :, :].rearrange(flat) for q in range(2)]
                link(nc.vector.tensor_copy(place_f[:, :], best_i[:, :, :].rearrange(flat)))
                link(nc.vector.tensor_scalar(rank_i[:, :, :].rearrange(flat), place_f[:, :], float(SHORT), 0.0,
                                             ALU.subtract, ALU.max))
                link(nc.vector.tensor_single_scalar(rank_i[:, :, :], rank_i[:, :, :], 3, ALU.logical_shift_right))
                link(nc.vector.tensor_copy(rank[0], rank_i[:, :, :].rearrange(flat)))
                nc.vector.scalar_tensor_tensor(out=begin_f[:, :], in0=rank[0], scalar=1.0, in1=rank[0],
                                               op0=ALU.min, op1=ALU.add)
                f = top_f[:, :, :].rearrange("p (h q) k -> p h q k", q=2)
                eng.wait_ge(turned, t + 1)
                for q in range(2):
                    if q == 1:
                        link(nc.vector.scalar_tensor_tensor(out=rank[1], in0=begin_f[:, :], scalar=-float(SHORT),
                                                            in1=place_f[:, :], op0=ALU.mult, op1=ALU.add))
                    link(nc.vector.tensor_tensor(
                        hot[:, :, :, :].rearrange("p h k r -> p (h k) r"),
                        rep(rank[q], 2, TOPK),
                        rep(iota16[:, :], 1, PH * TOPK), ALU.is_equal))
                    link(nc.vector.tensor_tensor(hot[:, :, :, :], hot[:, :, :, :],
                                                 rep(f[:, :, q, :], 2, TOPK), ALU.mult))
                    link(nc.vector.tensor_reduce(found[:, q, :], hot[:, :, :, :].rearrange("p h k r -> p (h k) r"),
                                                 axis=AX.X, op=ALU.add))
                eng.wait_ge(exped, t + 1)
                link(nc.vector.tensor_reduce(norm[:, 0, :], e[:, :, :], axis=AX.X, op=ALU.add))
                link(nc.vector.reciprocal(norm[:, 1, :], norm[:, 0, :]))
                nc.vector.tensor_tensor(found[:, 2, :].rearrange("p (h k) -> p h k", h=PH), e[:, :, :],
                                        rep(norm[:, 1, :], 2, TOPK), ALU.mult).then_inc(found_all, 1)
                assert n[0] <= LINKS, n[0]
                if n[0] < LINKS:
                    eng.sem_inc(dve, LINKS - n[0])


def expert_weights(nc, sp, picks, table, gd, kb, kb_stage, xl, parked, fetched, u_w, u_raw, u_in, late):
    B = 8
    keys = sp.at("pick_keys", kb, [P, 2, T], BF16)
    part = sp.at("weight_parts", kb + 4, [P, 3, T], BF16)
    rest = sp.at("weight_rest", kb + 10, [P, T])
    iota = sp.at("iota_each", kb + 14, [P, NK, B], BF16)
    iota_f = sp.at("iota", kb + 16, [P, NK])
    first = [sp.at("first_hot", kb + 16.5 + 2 * z, [P, NK, B], BF16) for z in range(2)]
    second = [sp.at("second_hot", kb + 20.5 + 2 * z, [P, NK, B], BF16) for z in range(2)]
    scaled = [[sp.at("second_scaled", (kb - 4, 205)[z] if m == 2 else kb + 24.5 + 4 * z + 2 * m,
                     [P, NK, B], BF16) for m in range(3)] for z in range(2)]
    stage = [sp.at("weights_stage", kb_stage + 64 * u, [P, NK, P]) for u in range(2)]
    bank = sp.banks
    iota_in, split, hot, matched, weighed, third, used, out = (
        sp.sem(n) for n in ("iota_in", "split", "hot", "second_matched", "weighed", "third_weighed",
                            "hot_used", "g_out"))
    stored = [sp.sem("stored0"), sp.sem("stored1")]
    TURNS, SPLITS = P // B, 6
    SHARE = B // 2

    with nc.Block() as block:
        @block.sync
        def _(eng):
            eng.dma_start(iota_f[:, :], table[:, C_IOTA:C_IOTA + NK]).then_inc(iota_in, 16)

            def store(t, u, a0=0, a1=NK):
                return eng.dma_start(gd[a0:a1, :, ds(t * P, P)].rearrange("a b t -> b a t"), stage[u][:, a0:a1, :])

            with eng.Fori(0, TT // 2 - 1) as i:
                for u in range(2):
                    eng.wait_ge(out, (2 * i + u + 1) * TURNS + 2)
                    store(2 * i + u, u).then_inc(stored[u], 16)
            eng.wait_ge(out, (TT - 1) * TURNS + 2)
            store(TT - 2, 0).then_inc(stored[0], 16)
            for n in range(2):
                eng.dma_start(u_raw[n][:, :], u_w[n * P:(n + 1) * P, :]).then_inc(u_in[n], 16)
            eng.wait_ge(stored[0], 16 * (TT // 2) + 16)
            for n in range(2):
                k = slice(n * KT // 2, (n + 1) * KT // 2)
                eng.dma_start(f32(xl[:, k, :]), parked[:, k, :]).then_inc(fetched[n], 16)
            eng.wait_ge(out, TT * TURNS + 2)
            store(TT - 1, 1, 0, 4).then_inc(late[0], 16)
            eng.wait_ge(stored[1], 16 * (TT // 2))

        @block.vector
        def _(eng):
            n = [0]

            def link(ins):
                n[0] += 1
                ins.then_inc(split, 1)
                eng.wait_ge(split, n[0])

            nc.vector.tensor_copy(keys[:, :, :], picks[:, 0:2, :])
            link(nc.vector.tensor_copy(part[:, 0, :], picks[:, 2, :]))
            link(nc.vector.tensor_tensor(rest[:, :], picks[:, 2, :], part[:, 0, :], ALU.subtract))
            link(nc.vector.tensor_copy(part[:, 1, :], rest[:, :]))
            link(nc.vector.tensor_tensor(rest[:, :], rest[:, :], part[:, 1, :], ALU.subtract))
            link(nc.vector.tensor_copy(part[:, 2, :], rest[:, :]))
            eng.wait_ge(iota_in, 16)
            link(nc.vector.tensor_copy(iota[:, :, :], rep(iota_f[:, :], 2, B)))
            def match(m, z):
                nc.vector.tensor_tensor(second[z][:, :, :], iota[:, :, :], rep(keys[:, 1, ds(m * B, B)], 1, NK),
                                        ALU.is_equal).then_inc(matched, 1)

            def body(i, last):
                for z in range(2):
                    m = 2 * i + z
                    eng.wait_ge(used, m + 1)
                    nc.vector.tensor_tensor(first[z][:, :, :], iota[:, :, :], rep(keys[:, 0, ds(m * B, B)], 1, NK),
                                            ALU.is_equal).then_inc(hot, 1)
                    if not (last and z == 1):
                        eng.wait_ge(weighed, 3 * m + 3)
                        eng.wait_ge(third, m + 1)
                        match(m + 1, 1 - z)
                    eng.wait_ge(matched, m + 1)
                    for w in range(2):
                        nc.vector.tensor_tensor(scaled[z][w][:, :, :], second[z][:, :, :],
                                                rep(part[:, w, ds(m * B, B)], 1, NK), ALU.mult).then_inc(weighed, 1)
                    nc.vector.tensor_tensor(scaled[z][2][:, :, 0:SHARE], second[z][:, :, 0:SHARE],
                                            rep(part[:, 2, ds(m * B, SHARE)], 1, NK), ALU.mult).then_inc(weighed, 1)

            eng.sem_inc(weighed, 3)
            match(0, 0)
            assert n[0] == SPLITS, n[0]
            with eng.Fori(0, T // (2 * B) - 1) as i:
                body(i, False)
            body(T // (2 * B) - 1, True)

        @block.tensor
        def _(eng):
            eng.sem_inc(used, 2)
            with eng.Fori(0, T // (2 * B)) as i:
                for z in range(2):
                    m = 2 * i + z
                    eng.wait_ge(hot, m + 1)
                    eng.wait_ge(weighed, 3 * m + 6)
                    eng.wait_ge(third, m + 2)
                    eng.wait_ge(out, m + 1)
                    for t in range(B):
                        o = bank[:, 2 * z + t // 4, (t % 4) * P:(t % 4 + 1) * P]
                        for w in range(3):
                            last = nc.tensor.matmul(o, scaled[z][w][:, :, t], first[z][:, :, t],
                                                    start=w == 0, stop=w == 2)
                    last.then_inc(used, 1)

        @block.scalar
        def _(eng):
            eng.sem_inc(out, 2)
            for u in range(2):
                eng.sem_inc(stored[u], 16)
            eng.sem_inc(third, 1)

            def scale_third(m, z):
                eng.wait_ge(matched, m + 1)
                eng.wait_ge(used, m + 1)
                for t in range(SHARE, B):
                    last = nc.scalar.activation(scaled[z][2][:, :, t], second[z][:, :, t], ACT.Copy,
                                                scale=rest[:, ds(m * B + t, 1)])
                last.then_inc(third, 1)

            def pair(i, u, h, last):
                for z in range(2):
                    m = (2 * i + u) * TURNS + 2 * h + z
                    if not (last and z == 1):
                        scale_third(m + 1, 1 - z)
                    eng.wait_ge(used, m + 3)
                    nc.scalar.activation(stage[u][:, :, ds((2 * h + z) * B, B)],
                                         bank[:, 2 * z:2 * z + 2, :].rearrange("p q (t a) -> p a (q t)", t=4),
                                         ACT.Copy).then_inc(out, 1)

            def tile(i, u, last):
                eng.wait_ge(stored[u], 16 * i + 16)
                with eng.Fori(0, TURNS // 2 - (1 if last else 0)) as h:
                    pair(i, u, h, False)
                if last:
                    pair(i, u, TURNS // 2 - 1, True)

            eng.wait_ge(split, SPLITS)
            scale_third(0, 0)
            with eng.Fori(0, TT // 2 - 1) as i:
                for u in range(2):
                    tile(i, u, False)
            for u in range(2):
                tile(TT // 2 - 1, u, u == 1)
            eng.wait_ge(out, TT * TURNS + 2)
            eng.dma_start(gd[4:NK, :, (TT - 1) * P:T].rearrange("a b t -> b a t"),
                          stage[1][:, 4:NK, :]).then_inc(late[1], 16)


def experts(nc, sp, ident, xh, xl, fetched, ur, u_in, late, x1, gd, u_w, v_w, g_final, out):
    uh = [sp.at("uT_hi", 40 + 4 * e, [P, KT, P], F32R) for e in range(2)]
    ul = [sp.at("uT_lo", 48 + 4 * e, [P, KT, P], F32R) for e in range(2)]
    gt = [sp.at("g_tile", 56 + 4 * e, [P, T]) for e in range(2)]
    gb = sp.at("final_gain", 64, [P, D])
    ah = [sp.at("a_hi", 109 + 4 * b, [P, T], F32R) for b in range(4)]
    al = [sp.at("a_lo", 125 + 4 * b, [P, T], F32R) for b in range(4)]
    a_raw = [sp.at("a_raw", 125 + 4 * b, [P, T]) for b in range(4)]
    acc = sp.at("acc", 141, [P, TT, D])
    vh = [sp.at("v_hi", 173 + 4 * b, [P, D], F32R) for b in range(4)]
    vl = [sp.at("v_lo", 189 + 4 * b, [P, D], F32R) for b in range(4)]
    vr = [sp.at("v_raw", 189 + 4 * b, [P, D]) for b in range(4)]
    junk = sp.at("final_squares", 32, [P, 2, D])
    small = sp.at("final_small", 206, [P, 32])
    bank = sp.banks
    t_ps = bank[:, 0:2, :].rearrange("p b (k e) -> p (b k) e", e=P)
    o_ps = [bank[:, 4 + 2 * z:6 + 2 * z, :].rearrange("p b c -> p (b c)") for z in range(2)]
    S = sp.sem
    g_in = [S(f"g_in{e}") for e in range(2)]
    v_in = [S(f"v_in{s}") for s in range(4)]
    acc_in, gain_in, turned, uhi, ulo, hidden, gelued, weighed, ahi, alo, vhi, vlo, summed, flushed = (
        S(n) for n in ("acc_in", "gain_in", "turned", "u_hi", "u_lo", "hidden", "gelued", "weighed", "a_hi", "a_lo",
                       "v_hi", "v_lo", "summed", "flushed"))
    STEPS, TURN = E_TILES, 4
    TURNS = STEPS // TURN
    eps_set, sumsq, std, rstd, done, stored = (
        S(n) for n in ("eps_set", "sumsq", "std", "rstd", "normed", "stored"))
    ss, sd, rs, eps = small[:, 0:TT], small[:, TT:2 * TT], small[:, 2 * TT:3 * TT], small[:, 3 * TT:3 * TT + 1]
    xt = x1.rearrange("(t p) d -> p t d", p=P)
    ot = out.rearrange("(t p) d -> p t d", p=P)

    def turns(eng, body):
        body(0, True, False)
        with eng.Fori(1, TURNS - 1) as i:
            body(i, False, False)
        body(TURNS - 1, False, True)

    with nc.Block() as block:
        @block.sync
        def _(eng):
            def load_u(n, e):
                eng.dma_start(ur[e][:, :], u_w[ds(n * P, P), :]).then_inc(u_in[e], 16)

            def load_g(n, e):
                eng.dma_start(gt[e][:, :], gd[ds(n, 1), :, :].rearrange("o b t -> b (o t)")).then_inc(g_in[e], 16)

            def load_v(n, s):
                eng.dma_start(vr[s][:, :], v_w[ds(n * P, P), :]).then_inc(v_in[s], 16)

            eng.wait_ge(late[0], 16)
            load_g(0, 0)
            load_g(1, 1)
            eng.wait_ge(turned, 1)
            load_u(2, 0)
            eng.wait_ge(late[1], 16)
            for n in range(2):
                load_v(n, n)
            eng.dma_start(acc[:, :, :], xt).then_inc(acc_in, 16)
            eng.dma_start(gb[:, :], g_final.partition_broadcast(P)).then_inc(gain_in, 16)

            def body(i, first, last):
                steps = [4 * i + s if isinstance(i, int) else eng.snap(4 * i + s) for s in range(TURN + 2)]
                for s in range(TURN):
                    n, e = steps[s], s % 2
                    if not (last and s >= 2) and not (first and s == 0):
                        eng.wait_ge(turned, n + 1)
                        load_u(steps[s + 2], e)
                    if first and s < 2:
                        continue
                    eng.wait_ge(weighed, 2 * n - 2)
                    load_g(n, e)
                    if not first:
                        eng.wait_ge(summed, 4 * (n - e) - 8)
                    load_v(n, s)
            turns(eng, body)
            for t in range(TT):
                eng.wait_ge(done, t + 1)
                eng.dma_start(ot[:, t, :], acc[:, t, :]).then_inc(stored, 16)
            eng.wait_ge(stored, 16 * TT)

        @block.tensor
        def _(eng):
            def turn(n, e, value, wait_bank=True):
                eng.wait_ge(u_in[e], value)
                if wait_bank:
                    eng.wait_ge(ulo, n)
                for k in range(KT):
                    last = nc.tensor.transpose(t_ps[:, k, :], ur[e][:, k * P:(k + 1) * P], ident)
                last.then_inc(turned, 1)

            def hide(n, e, h, free, first=False):
                if h == 0:
                    eng.wait_ge(ulo, n + 1)
                if free:
                    eng.wait_ge(gelued, 2 * n + h - 1)
                for k in range(KT):
                    if first and k % 4 == 0:
                        eng.wait_ge(fetched[k // 4], 16)
                    last = three_pass(nc, bank[:, 2 + h, :], uh[e][:, k, :], ul[e][:, k, :],
                                      xh[:, k, h * HALF:(h + 1) * HALF], xl[:, k, h * HALF:(h + 1) * HALF],
                                      k == 0, k == KT - 1)
                last.then_inc(hidden, 1)

            def sum_up(m, n, b, part, free):
                if part == 0:
                    eng.wait_ge(alo, 2 * n)
                    eng.wait_ge(vlo, n)
                for z in range(2):
                    if free:
                        eng.wait_ge(flushed, 2 * (m - 5) + z + 1)
                    t = slice((2 * part + z) * P, (2 * part + z + 1) * P)
                    for c in range(2):
                        o, cols = bank[:, 4 + 2 * z + c, :], slice(c * 512, (c + 1) * 512)
                        for x in range(2):
                            y = 2 * b + x
                            last = three_pass(nc, o, ah[y][:, t], al[y][:, t], vh[y][:, cols], vl[y][:, cols],
                                              x == 0, x == 1)
                    last.then_inc(summed, 1)

            turn(0, 0, 16, False)

            def body(i, first, last):
                for s in range(TURN):
                    n, e = 4 * i + s, s % 2
                    if not (last and s == TURN - 1):
                        turn(n + 1, 1 - e, 16 * (2 * i + (s + 1) // 2) + 16)
                    for h in range(2):
                        hide(n, e, h, not (first and s == 0), first and s == 0 and h == 0)
                        if not (first and s < 2):
                            sum_up(2 * n + h, n, (s // 2 + 1) % 2, 2 * e + h, not (first and s == 2 and h == 0))
            turns(eng, body)
            for part in range(4):
                sum_up(2 * STEPS + part, STEPS, 1, part, True)

        @block.scalar
        def _(eng):
            def u_hi(n, e, free):
                eng.wait_ge(turned, n + 1)
                if free:
                    eng.wait_ge(hidden, 2 * n - 2)
                nc.scalar.activation(uh[e][:, :, :], t_ps, ACT.Copy).then_inc(uhi, 1)

            u_hi(0, 0, False)

            def body(i, first, last):
                for s in range(TURN):
                    n, e = 4 * i + s, s % 2
                    if not (last and s == TURN - 1):
                        u_hi(n + 1, 1 - e, not (first and s < 1))
                    if not first:
                        eng.wait_ge(summed, 4 * (n - e) - 8)
                    for h in range(2):
                        cols = slice(h * HALF, (h + 1) * HALF)
                        eng.wait_ge(hidden, 2 * n + h + 1)
                        nc.scalar.activation(a_raw[s][:, cols], bank[:, 2 + h, :], ACT.Gelu).then_inc(gelued, 1)
                        eng.wait_ge(weighed, 2 * n + h + 1)
                        nc.scalar.activation(ah[s][:, cols], a_raw[s][:, cols], ACT.Copy).then_inc(ahi, 1)
                    eng.wait_ge(v_in[s], 16 * i + 16)
                    nc.scalar.activation(vh[s][:, :], vr[s][:, :], ACT.Copy).then_inc(vhi, 1)
            turns(eng, body)
            eng.wait_ge(turned, STEPS)
            eng.wait_ge(eps_set, 1)
            for t in range(TT):
                eng.wait_ge(flushed, 4 * STEPS - TT + t + 1)
                nc.scalar.activation(junk[:, t % 2, :], acc[:, t, :], ACT.Square,
                                     accum_out=ss[:, t:t + 1]).then_inc(sumsq, 1)
                eng.wait_ge(sumsq, t + 1)
                nc.scalar.activation(sd[:, t:t + 1], ss[:, t:t + 1], ACT.Sqrt, bias=eps, scale=1.0 / D).then_inc(std, 1)

        @block.gpsimd
        def _(eng):
            def body(i, first, last):
                for s in range(TURN):
                    n, e = 4 * i + s, s % 2
                    eng.wait_ge(vhi, n + 1)
                    nc.gpsimd.tensor_tensor(vl[s][:, :], vr[s][:, :], f32(vh[s][:, :]),
                                            ALU.subtract).then_inc(vlo, 1)
            turns(eng, body)

        @block.vector
        def _(eng):
            def u_lo(n, e):
                eng.wait_ge(uhi, n + 1)
                nc.vector.tensor_tensor(ul[e][:, :, :], t_ps, f32(uh[e][:, :, :]), ALU.subtract).then_inc(ulo, 1)

            def flush(m, part):
                for z in range(2):
                    eng.wait_ge(summed, 2 * (m - 4) + z + 1)
                    t = 2 * part + z
                    nc.vector.tensor_tensor(acc[:, t, :], acc[:, t, :], o_ps[z], ALU.add).then_inc(flushed, 1)

            nc.vector.memset(eps, EPS).then_inc(eps_set, 1)
            u_lo(0, 0)

            def body(i, first, last):
                for s in range(TURN):
                    n, e = 4 * i + s, s % 2
                    if first and s == 2:
                        eng.wait_ge(acc_in, 16)
                    if not (last and s == TURN - 1):
                        u_lo(n + 1, 1 - e)
                    for h in range(2):
                        cols = slice(h * HALF, (h + 1) * HALF)
                        eng.wait_ge(gelued, 2 * n + h + 1)
                        if h == 0:
                            eng.wait_ge(g_in[e], 16 * (2 * i + s // 2) + 16)
                        nc.vector.tensor_tensor(a_raw[s][:, cols], a_raw[s][:, cols], gt[e][:, cols],
                                                ALU.mult).then_inc(weighed, 1)
                        eng.wait_ge(ahi, 2 * n + h + 1)
                        nc.vector.tensor_tensor(al[s][:, cols], a_raw[s][:, cols], f32(ah[s][:, cols]),
                                                ALU.subtract).then_inc(alo, 1)
                        if not (first and s < 2):
                            flush(2 * n + h, 2 * e + h)
            turns(eng, body)

            def normalise(t):
                eng.wait_ge(std, t + 1)
                nc.vector.reciprocal(rs[:, t:t + 1], sd[:, t:t + 1]).then_inc(rstd, 1)
                eng.wait_ge(rstd, t + 1)
                nc.vector.scalar_tensor_tensor(out=acc[:, t, :], in0=acc[:, t, :], scalar=rs[:, t:t + 1],
                                               in1=gb[:, :], op0=ALU.mult, op1=ALU.mult).then_inc(done, 1)

            eng.wait_ge(gain_in, 16)
            for part in range(4):
                flush(2 * STEPS + part, part)
                if part > 0:
                    normalise(2 * part - 2)
                    normalise(2 * part - 1)
            normalise(TT - 2)
            normalise(TT - 1)


def block_kernel(nc, table, x, norm_mix_g, w_in, gate_bias, sinks, diff_lambda, diff_subln_g, w_up_a, w_up_b,
                 w_out, norm_ffn_g, peer_wq, peer_subkeys, peer_u, peer_v, norm_final_g, out):
    sp = Space(nc)
    x1 = nc.dram_tensor("x_after_mixing", [T, D], F32, kind="Internal").ap()
    gd = nc.dram_tensor("expert_weights", [NK, NK, T], F32, kind="Internal").ap()
    park = nc.dram_tensor("parked_tokens", [P, KT, T], F32, kind="Internal").ap()
    x2, out2 = x[0], out[0]
    ident_t = sp.at("ident", 207, [P, P])
    ident = ident_t[:, :]
    id_in = sp.sem("ident_in")
    with nc.Block() as block:
        @block.sync
        def _(eng):
            eng.dma_start(ident, table[:, C_ID:C_ID + P]).then_inc(id_in, 16)
            eng.wait_ge(id_in, 16)

    xh = sp.at("xnT_hi", 0, [P, KT, T], F32R)
    xl = sp.at("xnT_lo", 32, [P, KT, T], F32R)
    norm_transpose(nc, sp, ident, x2, norm_mix_g, xh, xl, 136)

    qkT = sp.at("qkT", 64, [P, 13, T])
    va = sp.at("v_window", 116, [P, TT, P])
    vb = sp.at("v_diff", 120, [P, TT, 4 * P])
    wi = w_in[0].rearrange("(k p) c -> p k c", p=P)

    def tile_half(base, c, j):
        at = ds(base + 2 * c + j // 2, 1)
        return qkT[:, at, (j % 2) * HALF:(j % 2 + 1) * HALF].rearrange("p o t -> p (o t)")

    rest = []
    for q in range(2):
        sources = [(jj * P + a * HD, wi[:, :, QA + a * 256 + (2 * q + jj) * HD:QA + a * 256 + (2 * q + jj + 1) * HD])
                   for jj in range(2) for a in range(2)]
        rest.append(("T", sources, lambda j, q=q: qkT[:, T_QA + 2 * q + j // 2, (j % 2) * HALF:(j % 2 + 1) * HALF]))
    rest.append(("KV", [(0, wi[:, :, KA:KA + WC])],
                 lambda j: qkT[:, T_KA, j * HALF:(j + 1) * HALF] if j < 2 else va[:, 4 * (j - 2):4 * (j - 2) + 4, :]))
    for c in range(2):
        rest.append(("V", [(0, wi[:, :, VB + c * WC:VB + (c + 1) * WC])],
                     lambda j, c=c: vb[:, 2 * j:2 * j + 2, c * WC:(c + 1) * WC]))
    project(nc, sp, xh, xl, 136, 2, lambda c: wi[:, :, ds(QB + c * WC, WC)],
            lambda c, j: tile_half(T_QB, c, j), rest)

    attention(nc, sp, ident, table, qkT, va, vb, sinks, diff_lambda)
    oh = sp.at("o_hi", 96, [P, 8, T], F32R)
    ol = sp.at("o_lo", 128, [P, 8, T], F32R)
    mT = sp.at("mergedT", 64, [P, KT, T])
    gate_and_up(nc, sp, xh, xl, qkT, oh, ol, mT, diff_subln_g, w_in[0], gate_bias, w_up_a[0], w_up_b[0])
    mix_out(nc, sp, mT, x2, w_out[0], x1)
    sp.recycle()

    xh = sp.at("xn2T_hi", 0, [P, KT, T], F32R)
    xl = sp.at("xn2T_lo", 32, [P, KT, T], F32R)
    norm_transpose(nc, sp, ident, x1, norm_ffn_g, xh, xl, 136)
    qT = sp.at("peer_qT", 64, [P, HP, T])
    wq = peer_wq[0].rearrange("(k p) c -> p k c", p=P)

    def q_half(c, j):
        at = ds(2 * c + j // 2, 1)
        return qT[:, at, (j % 2) * HALF:(j % 2 + 1) * HALF].rearrange("p o t -> p (o t)")
    project(nc, sp, xh, xl, 128, HP * P // WC // 2, lambda c: wq[:, :, ds(c * WC, WC)], q_half, [])
    parked = sp.sem("parked")

    skT = sp.at("subkeysT", 136, [P, HP, P])
    turn_subkeys(nc, sp, ident, peer_subkeys[0], skT, xl, park, parked)
    picks = sp.at("picks", 32, [P, 3, T])
    select_experts(nc, sp, ident, qT, skT, picks, table, parked, 144)
    sp.recycle()
    xl = sp.at("xn2T_lo_again", 77, [P, KT, T], F32R)
    fetched = [sp.sem("fetched0"), sp.sem("fetched1")]
    u_raw = [sp.at("u_raw", 32 + 4 * e, [P, D]) for e in range(2)]
    u_in = [sp.sem("u_in0"), sp.sem("u_in1")]
    late = [sp.sem("g_late_first"), sp.sem("g_late_rest")]
    expert_weights(nc, sp, picks, table, gd, 44, 77, xl, park, fetched, peer_u[0], u_raw, u_in, late)
    experts(nc, sp, ident, xh, xl, fetched, u_raw, u_in, late, x1, gd, peer_u[0], peer_v[0], norm_final_g, out2)
    sp.recycle()


_INPUTS = ["x", "norm_mix_g", "w_in", "gate_bias", "sinks", "diff_lambda", "diff_subln_g", "w_up_a", "w_up_b",
           "w_out", "norm_ffn_g", "peer_wq", "peer_subkeys", "peer_u", "peer_v", "norm_final_g"]


def kernel(**inputs):
    import concourse.bacc as bacc
    from concourse.bass_utils import run_bass_kernel_spmd

    nc = bacc.Bacc("TRN2", target_bir_lowering=False, num_devices=1)
    arrays = {"table_dram": constant_table()}
    arrays.update((f"{n}_dram", np.ascontiguousarray(inputs[n])) for n in _INPUTS)
    aps = [nc.dram_tensor(n, a.shape, F32, kind="ExternalInput").ap() for n, a in arrays.items()]
    out = nc.dram_tensor("out_dram", (1, T, D), F32, kind="ExternalOutput").ap()
    block_kernel(nc, *aps, out)
    r = run_bass_kernel_spmd(nc, [arrays], core_ids=[0])
    return r.results[0]["out_dram"]
```
